# Optimizing a Trainium2 kernel written in Bass

```python
import math
import jax, jax.numpy as jnp
from jax import lax
import numpy as np

D_MODEL = 1024
BATCH = 1
SEQ = 512
DEPTH = 1

N_HEADS = 8
HEAD_DIM = 64
ATT_WIDTH = N_HEADS * HEAD_DIM
PATTERNS = ((128, 1), (512, 4), (2048, 16))
SSM_GROUPS = 16
SSM_GROUP_CH = 16
SSM_WIDTH = SSM_GROUPS * SSM_GROUP_CH
SSM_STATE = 64
D_FF = 2048
CONV_W = 3
IN_WIDTH = 3 * ATT_WIDTH + SSM_WIDTH + 2 * D_MODEL
EPS = 1e-6
NEG_INF = -1e30


def _rmsnorm(x, g):
    x32 = x.astype(jnp.float32)
    y = x32 * lax.rsqrt(jnp.mean(x32 * x32, axis=-1, keepdims=True) + EPS)
    return y.astype(x.dtype) * g

def _modulate(x, g, shift, scale):
    return _rmsnorm(x, g) * (1 + scale[:, None, :]) + shift[:, None, :]

def _alibi_slopes():
    return np.array([2.0 ** (-8.0 * (h + 1) / N_HEADS) for h in range(N_HEADS)], dtype=np.float32)

def _dilated_window_attention(q, k, v, slopes, window, dilation):
    b, s, h, hd = q.shape
    w = window // dilation
    L = s // dilation
    nb = -(-L // w)
    Lp = nb * w
    X = b * dilation

    def to_sub(t):
        t = t.reshape(b, L, dilation, h, hd).transpose(0, 2, 3, 1, 4)
        return t.reshape(X, h, L, hd)

    qs, ks, vs = to_sub(q), to_sub(k), to_sub(v)
    qb = jnp.pad(qs, ((0, 0), (0, 0), (0, Lp - L), (0, 0))).reshape(X, h, nb, w, hd)
    kp = jnp.pad(ks, ((0, 0), (0, 0), (w, Lp - L), (0, 0)))
    vp = jnp.pad(vs, ((0, 0), (0, 0), (w, Lp - L), (0, 0)))
    kb = jnp.concatenate([kp[:, :, :Lp].reshape(X, h, nb, w, hd),
                          kp[:, :, w:].reshape(X, h, nb, w, hd)], axis=3)
    vb = jnp.concatenate([vp[:, :, :Lp].reshape(X, h, nb, w, hd),
                          vp[:, :, w:].reshape(X, h, nb, w, hd)], axis=3)

    a_idx = np.arange(w)[:, None]
    j_idx = np.arange(2 * w)[None, :]
    dist = (w + a_idx - j_idx).astype(np.float32)
    kpos = np.arange(nb)[:, None, None] * w - w + j_idx[None]
    valid = (dist[None] >= 0) & (dist[None] <= w) & (kpos >= 0)
    bias = -(slopes[:, None, None] * dilation) * dist[None]

    scale = HEAD_DIM ** -0.5
    sc = jnp.einsum('xhnqd,xhnkd->xhnqk', qb, kb).astype(jnp.float32) * scale
    sc = jnp.where(valid, sc + bias[:, None], NEG_INF)
    m = jnp.max(sc, axis=-1, keepdims=True)
    p = jnp.exp(sc - m)
    den = jnp.sum(p, axis=-1, keepdims=True)
    o = jnp.einsum('xhnqk,xhnkd->xhnqd', p, vb.astype(jnp.float32)) / den
    lse = (m + jnp.log(den))[..., 0]

    o = o.reshape(X, h, Lp, hd)[:, :, :L].reshape(b, dilation, h, L, hd)
    o = o.transpose(0, 3, 1, 2, 4).reshape(b, s, h, hd)
    lse = lse.reshape(X, h, Lp)[:, :, :L].reshape(b, dilation, h, L)
    lse = lse.transpose(0, 3, 1, 2).reshape(b, s, h)
    return o, lse

def _s5_branch(u, a_re, a_im, log_dt, b_re, b_im, c_re, c_im, d_skip, w_glu, b_glu):
    f32 = jnp.float32
    bsz, s, _ = u.shape
    lr, li = a_re.astype(f32), a_im.astype(f32)
    dt = jnp.exp(log_dt.astype(f32))[:, None]
    mag = jnp.exp(lr * dt)
    ang = li * dt
    ab_re, ab_im = mag * jnp.cos(ang), mag * jnp.sin(ang)
    nr, ni = ab_re - 1.0, ab_im
    den = lr * lr + li * li
    f_re = (nr * lr + ni * li) / den
    f_im = (ni * lr - nr * li) / den
    br, bi = b_re.astype(f32), b_im.astype(f32)
    bb_re = f_re[..., None] * br - f_im[..., None] * bi
    bb_im = f_re[..., None] * bi + f_im[..., None] * br

    ug = u.astype(f32).reshape(bsz, s, SSM_GROUPS, SSM_GROUP_CH)
    bu_re = jnp.einsum('bsgc,gnc->bsgn', ug, bb_re)
    bu_im = jnp.einsum('bsgc,gnc->bsgn', ug, bb_im)
    a_re_t = jnp.broadcast_to(ab_re, bu_re.shape)
    a_im_t = jnp.broadcast_to(ab_im, bu_re.shape)

    def combine(left, right):
        ar1, ai1, xr1, xi1 = left
        ar2, ai2, xr2, xi2 = right
        return (ar2 * ar1 - ai2 * ai1,
                ar2 * ai1 + ai2 * ar1,
                ar2 * xr1 - ai2 * xi1 + xr2,
                ar2 * xi1 + ai2 * xr1 + xi2)

    _, _, xr, xi = lax.associative_scan(combine, (a_re_t, a_im_t, bu_re, bu_im), axis=1)
    y = (jnp.einsum('bsgn,gcn->bsgc', xr, c_re.astype(f32))
         - jnp.einsum('bsgn,gcn->bsgc', xi, c_im.astype(f32))
         + d_skip.astype(f32).reshape(SSM_GROUPS, SSM_GROUP_CH) * ug)
    y = y.reshape(bsz, s, SSM_WIDTH).astype(u.dtype)
    y = jax.nn.gelu(y)
    return y * jax.nn.sigmoid(y @ w_glu + b_glu)

def _hybrid_mixer(u, w_in, b_gate, a_re, a_im, log_dt, b_re, b_im, c_re, c_im,
                  d_skip, w_glu, b_glu, w_proj_att, w_proj_ssm, w_out):
    bsz, s, _ = u.shape
    proj = u @ w_in
    q, k, v, us, g_att, g_ssm = jnp.split(
        proj, [ATT_WIDTH, 2 * ATT_WIDTH, 3 * ATT_WIDTH, 3 * ATT_WIDTH + SSM_WIDTH,
               3 * ATT_WIDTH + SSM_WIDTH + D_MODEL], axis=-1)
    q = q.reshape(bsz, s, N_HEADS, HEAD_DIM)
    k = k.reshape(bsz, s, N_HEADS, HEAD_DIM)
    v = v.reshape(bsz, s, N_HEADS, HEAD_DIM)

    slopes = _alibi_slopes()
    outs, lses = [], []
    for window, dilation in PATTERNS:
        o, lse = _dilated_window_attention(q, k, v, slopes, window, dilation)
        outs.append(o)
        lses.append(lse)
    wts = jax.nn.softmax(jnp.stack(lses, axis=0), axis=0)
    o_att = jnp.sum(wts[..., None] * jnp.stack(outs, axis=0), axis=0)
    o_att = o_att.reshape(bsz, s, ATT_WIDTH).astype(u.dtype)
    y_att = o_att @ w_proj_att

    y_ssm = _s5_branch(us, a_re, a_im, log_dt, b_re, b_im, c_re, c_im,
                       d_skip, w_glu, b_glu) @ w_proj_ssm

    gb_att, gb_ssm = jnp.split(b_gate, 2, axis=-1)
    merged = jax.nn.sigmoid(g_att + gb_att) * y_att + jax.nn.sigmoid(g_ssm + gb_ssm) * y_ssm
    return merged @ w_out

def _conv_ffn(u, w_up, w_conv, b_conv, w_down):
    s = u.shape[1]
    a, val = jnp.split(u @ w_up, 2, axis=-1)
    ap = jnp.pad(a, ((0, 0), (CONV_W - 1, 0), (0, 0)))
    conv = b_conv
    for j in range(CONV_W):
        conv = conv + w_conv[j] * ap[:, CONV_W - 1 - j:CONV_W - 1 - j + s]
    return (jax.nn.silu(conv) * val) @ w_down

def first_inputs(seed: int = 0) -> dict:
    key = jax.random.key(seed)
    ks = jax.random.split(key, 32)
    f32 = jnp.float32
    L, D, G, N, C = DEPTH, D_MODEL, SSM_GROUPS, SSM_STATE, SSM_GROUP_CH
    nrm = lambda k, shape, sc: jax.random.normal(k, shape, f32) * sc
    inp = {}
    inp["x"] = nrm(ks[0], (BATCH, SEQ, D), 1.0)
    inp["c"] = nrm(ks[1], (BATCH, D), 1.0)
    inp["w_ada"] = nrm(ks[2], (L, D, 6 * D), 0.5 * D ** -0.5)
    inp["b_ada"] = nrm(ks[3], (L, 6 * D), 0.02)
    inp["g_mix"] = 1.0 + nrm(ks[4], (L, D), 0.02)
    inp["w_in"] = nrm(ks[5], (L, D, IN_WIDTH), D ** -0.5)
    inp["b_gate"] = nrm(ks[6], (L, 2 * D), 0.02)
    inp["a_re"] = -0.5 + nrm(ks[7], (L, G, N), 0.01)
    inp["a_im"] = jnp.pi * jnp.arange(N, dtype=f32)[None, None, :] + nrm(ks[8], (L, G, N), 0.01)
    inp["log_dt"] = jax.random.uniform(ks[9], (L, G), f32, math.log(1e-3), math.log(1e-1))
    inp["b_re"] = nrm(ks[10], (L, G, N, C), (2 * C) ** -0.5)
    inp["b_im"] = nrm(ks[11], (L, G, N, C), (2 * C) ** -0.5)
    inp["c_re"] = nrm(ks[12], (L, G, C, N), (2 * N) ** -0.5)
    inp["c_im"] = nrm(ks[13], (L, G, C, N), (2 * N) ** -0.5)
    inp["d_skip"] = nrm(ks[14], (L, SSM_WIDTH), 1.0)
    inp["w_glu"] = nrm(ks[15], (L, SSM_WIDTH, SSM_WIDTH), SSM_WIDTH ** -0.5)
    inp["b_glu"] = nrm(ks[16], (L, SSM_WIDTH), 0.02)
    inp["w_proj_att"] = nrm(ks[17], (L, ATT_WIDTH, D), ATT_WIDTH ** -0.5)
    inp["w_proj_ssm"] = nrm(ks[18], (L, SSM_WIDTH, D), SSM_WIDTH ** -0.5)
    inp["w_out"] = nrm(ks[19], (L, D, D), D ** -0.5)
    inp["g_ffn"] = 1.0 + nrm(ks[20], (L, D), 0.02)
    inp["w_up"] = nrm(ks[21], (L, D, 2 * D_FF), D ** -0.5)
    inp["w_conv"] = nrm(ks[22], (L, CONV_W, D_FF), CONV_W ** -0.5)
    inp["b_conv"] = nrm(ks[23], (L, D_FF), 0.02)
    inp["w_down"] = nrm(ks[24], (L, D_FF, D), D_FF ** -0.5)
    inp["g_final"] = 1.0 + nrm(ks[25], (D,), 0.02)
    return inp

def first_block(x, c, w_ada, b_ada, g_mix, w_in, b_gate, a_re, a_im, log_dt, b_re, b_im,
              c_re, c_im, d_skip, w_glu, b_glu, w_proj_att, w_proj_ssm, w_out,
              g_ffn, w_up, w_conv, b_conv, w_down, g_final):
    h = x
    c_act = jax.nn.silu(c)
    for l in range(DEPTH):
        mod = c_act @ w_ada[l] + b_ada[l]
        sh1, sc1, gt1, sh2, sc2, gt2 = jnp.split(mod, 6, axis=-1)
        u = _modulate(h, g_mix[l], sh1, sc1)
        h = h + gt1[:, None, :] * _hybrid_mixer(
            u, w_in[l], b_gate[l], a_re[l], a_im[l], log_dt[l], b_re[l], b_im[l],
            c_re[l], c_im[l], d_skip[l], w_glu[l], b_glu[l],
            w_proj_att[l], w_proj_ssm[l], w_out[l])
        u = _modulate(h, g_ffn[l], sh2, sc2)
        h = h + gt2[:, None, :] * _conv_ffn(u, w_up[l], w_conv[l], b_conv[l], w_down[l])
    return _rmsnorm(h, g_final)


DEPTH_2 = 2

MIX_WIDTH = D_MODEL
ATTN_HEADS = 8
ATTN_HEAD_DIM = 64
ATTN_DIM = ATTN_HEADS * ATTN_HEAD_DIM
CONV_DIM = D_MODEL // 4
CONV_WIDTH = 3
POOL_WINDOWS = (2, 4, 8, 16)
N_POOL_GROUPS = len(POOL_WINDOWS)
POOL_DIM = D_MODEL // 4
POOL_GD = POOL_DIM // N_POOL_GROUPS
D_FF_2 = 2816
Q_BLOCK = 128
RMS_EPS = 1e-6
SPLIT_SIZES = (ATTN_DIM, ATTN_DIM, ATTN_DIM, CONV_DIM, CONV_DIM, CONV_DIM, POOL_DIM)
IN_PROJ_WIDTH = sum(SPLIT_SIZES)
SPLIT_POINTS = tuple(int(v) for v in np.cumsum(SPLIT_SIZES)[:-1])


def _rmsnorm_2(x, g):
    x32 = x.astype(jnp.float32)
    y = x32 * lax.rsqrt(jnp.mean(x32 * x32, axis=-1, keepdims=True) + RMS_EPS)
    return (y * g.astype(jnp.float32)).astype(x.dtype)

def _swiglu(h, w_gate, w_up, w_down):
    return (jax.nn.silu(h @ w_gate) * (h @ w_up)) @ w_down

def _stick_breaking_attention(q, k, v):
    B, S, H, dh = q.shape
    nb = S // Q_BLOCK
    scale = 1.0 / math.sqrt(dh)
    kh = k.transpose(0, 2, 1, 3)
    vh = v.transpose(0, 2, 1, 3)
    q_blocks = q.transpose(0, 2, 1, 3).reshape(B, H, nb, Q_BLOCK, dh).transpose(2, 0, 1, 3, 4)
    k_pos = jnp.arange(S)

    def block(args):
        q_blk, start = args
        q_pos = start + jnp.arange(Q_BLOCK)
        z = jnp.einsum('bhqd,bhkd->bhqk', q_blk, kh).astype(jnp.float32) * scale
        mask = k_pos[None, :] < q_pos[:, None]
        log_keep = jnp.where(mask, jax.nn.log_sigmoid(-z), 0.0)
        between = lax.cumsum(log_keep, axis=3, reverse=True) - log_keep
        a = jnp.where(mask, jnp.exp(jax.nn.log_sigmoid(z) + between), 0.0)
        return jnp.einsum('bhqk,bhkd->bhqd', a.astype(vh.dtype), vh)

    out = lax.map(block, (q_blocks, jnp.arange(nb) * Q_BLOCK))
    return out.transpose(1, 0, 3, 2, 4).reshape(B, S, H * dh)

def _short_conv(gate_b, gate_c, h, conv_w):
    S = h.shape[1]
    u = gate_c * h
    u_pad = jnp.pad(u, ((0, 0), (CONV_WIDTH - 1, 0), (0, 0)))
    y = conv_w[0] * u_pad[:, 0:S] + conv_w[1] * u_pad[:, 1:S + 1] + conv_w[2] * u_pad[:, 2:S + 2]
    return gate_b * y

def _multiscale_pool(p, pool_w, pool_scale):
    B, S, C = p.shape
    p32 = p.astype(jnp.float32).reshape(B, S, N_POOL_GROUPS, POOL_GD)
    cs0 = jnp.pad(jnp.cumsum(p32, axis=1), ((0, 0), (1, 0), (0, 0), (0, 0)))
    count_base = jnp.arange(1, S + 1, dtype=jnp.float32)
    outs = []
    for gi, w in enumerate(POOL_WINDOWS):
        lagged = jnp.pad(cs0[:, :S + 1 - w, gi], ((0, 0), (w - 1, 0), (0, 0)))
        mean = (cs0[:, 1:, gi] - lagged) / jnp.minimum(count_base, w)[None, :, None]
        outs.append(mean - p32[:, :, gi])
    d = jnp.stack(outs, axis=2).astype(p.dtype)
    y = jnp.einsum('bsgc,gcd->bsgd', d, pool_w).reshape(B, S, C)
    return y * pool_scale

def _mixer(h, w_in, conv_w, pool_w, pool_scale, w_out):
    B, S, _ = h.shape
    proj = h @ w_in
    q, k, v, gate_b, gate_c, conv_h, pool_in = jnp.split(proj, SPLIT_POINTS, axis=-1)
    q = q.reshape(B, S, ATTN_HEADS, ATTN_HEAD_DIM)
    k = k.reshape(B, S, ATTN_HEADS, ATTN_HEAD_DIM)
    v = v.reshape(B, S, ATTN_HEADS, ATTN_HEAD_DIM)
    attn = _stick_breaking_attention(q, k, v)
    conv = _short_conv(gate_b, gate_c, conv_h, conv_w)
    pool = _multiscale_pool(pool_in, pool_w, pool_scale)
    return jnp.concatenate([attn, conv, pool], axis=-1) @ w_out

def second_inputs(seed: int = 0) -> dict:
    key = jax.random.key(seed)
    ks = jax.random.split(key, 11)
    f32 = jnp.float32
    x = jax.random.normal(ks[0], (BATCH, SEQ, D_MODEL), f32)
    norm_g = 1.0 + 0.05 * jax.random.normal(ks[1], (DEPTH_2, 6, D_MODEL), f32)
    ffn_w_gate = jax.random.normal(ks[2], (DEPTH_2, 2, D_MODEL, D_FF_2), f32) * D_MODEL ** -0.5
    ffn_w_up = jax.random.normal(ks[3], (DEPTH_2, 2, D_MODEL, D_FF_2), f32) * D_MODEL ** -0.5
    ffn_w_down = jax.random.normal(ks[4], (DEPTH_2, 2, D_FF_2, D_MODEL), f32) * D_FF_2 ** -0.5
    w_in = jax.random.normal(ks[5], (DEPTH_2, D_MODEL, IN_PROJ_WIDTH), f32) * D_MODEL ** -0.5
    conv_w = jax.random.normal(ks[6], (DEPTH_2, CONV_WIDTH, CONV_DIM), f32) * CONV_WIDTH ** -0.5
    pool_w = jax.random.normal(ks[7], (DEPTH_2, N_POOL_GROUPS, POOL_GD, POOL_GD), f32) * POOL_GD ** -0.5
    pool_scale = 1.0 + 0.05 * jax.random.normal(ks[8], (DEPTH_2, POOL_DIM), f32)
    w_out = jax.random.normal(ks[9], (DEPTH_2, MIX_WIDTH, D_MODEL), f32) * MIX_WIDTH ** -0.5
    return {"x": x, "norm_g": norm_g, "ffn_w_gate": ffn_w_gate, "ffn_w_up": ffn_w_up,
            "ffn_w_down": ffn_w_down, "w_in": w_in, "conv_w": conv_w, "pool_w": pool_w,
            "pool_scale": pool_scale, "w_out": w_out}

def second_block(x, norm_g, ffn_w_gate, ffn_w_up, ffn_w_down, w_in, conv_w, pool_w, pool_scale, w_out):
    for l in range(DEPTH_2):
        g = norm_g[l]
        f = _swiglu(_rmsnorm_2(x, g[0]), ffn_w_gate[l, 0], ffn_w_up[l, 0], ffn_w_down[l, 0])
        x = x + 0.5 * _rmsnorm_2(f, g[1])
        m = _mixer(_rmsnorm_2(x, g[2]), w_in[l], conv_w[l], pool_w[l], pool_scale[l], w_out[l])
        x = x + _rmsnorm_2(m, g[3])
        f = _swiglu(_rmsnorm_2(x, g[4]), ffn_w_gate[l, 1], ffn_w_up[l, 1], ffn_w_down[l, 1])
        x = x + 0.5 * _rmsnorm_2(f, g[5])
    return x


def setup_inputs(seed=0):
    out = dict(first_inputs(seed))
    for name, value in second_inputs(seed + 1).items():
        if name != "x":
            out[name + "_2"] = value
    return out


def reference(
    x, c, w_ada, b_ada, g_mix, w_in, b_gate, a_re, a_im, log_dt, b_re, b_im, c_re, c_im, d_skip,
    w_glu, b_glu, w_proj_att, w_proj_ssm, w_out, g_ffn, w_up, w_conv, b_conv, w_down, g_final,
    norm_g_2, ffn_w_gate_2, ffn_w_up_2, ffn_w_down_2, w_in_2, conv_w_2, pool_w_2, pool_scale_2,
    w_out_2,
):
    x = first_block(
        x, c, w_ada, b_ada, g_mix, w_in, b_gate, a_re, a_im, log_dt, b_re, b_im, c_re, c_im,
        d_skip, w_glu, b_glu, w_proj_att, w_proj_ssm, w_out, g_ffn, w_up, w_conv, b_conv,
        w_down, g_final,
    )
    return second_block(
        x, norm_g_2, ffn_w_gate_2, ffn_w_up_2, ffn_w_down_2, w_in_2, conv_w_2, pool_w_2,
        pool_scale_2, w_out_2,
    )


_drawn_inputs = setup_inputs


def setup_inputs(seed=0):
    import zlib

    import numpy as np

    out = dict(_drawn_inputs(seed))
    spreads = {}
    factors = {'g_mix': 8.0,
     'b_gate': 8.0,
     'a_re': 64.0,
     'a_im': 60.408,
     'log_dt': 64.0,
     'b_re': 64.0,
     'b_im': 64.0,
     'c_re': 64.0,
     'c_im': 64.0,
     'b_glu': 8.0,
     'g_ffn': 6.137,
     'b_conv': 8.0}
    for name, (base, spread) in spreads.items():
        noise = np.random.default_rng([zlib.crc32(name.encode()), seed]).standard_normal(out[name].shape)
        drawn = base * np.exp(spread * noise) if base else spread * noise
        out[name] = __import__('jax').numpy.asarray(drawn.astype(out[name].dtype))
    for name, factor in factors.items():
        out[name] = (out[name] * factor).astype(out[name].dtype)
    return out
```

```python
from contextlib import ExitStack

import concourse.bass as bass
from concourse import mybir

F32 = mybir.dt.float32
F32R = mybir.dt.float32r
BF16 = mybir.dt.bfloat16
ALU = mybir.AluOpType
ACT = mybir.ActivationFunctionType

P = 128
T = 512
D = 1024
DC = D // P
EPS = 1e-6
HEADS, HD = 8, 64
HEAD_PAIRS = HEADS // 2
TB = T // P
ATT_SCALE = HD ** -0.5
LAYERS = 2
SSM_TILES = 8
SSM_CH = 16
HALF1 = 8
HALF2 = 11
RING = HALF2 * P

IN1, MERGE1, OUT1 = 0, 15, 19
FFN1 = 23
FFN1_HALF = HALF1 + DC // 2
LAYER0 = FFN1 + 2 * FFN1_HALF
FFN2_HALF = HALF2 + DC // 2
MIX2 = 2 * FFN2_HALF
MIX2_IN = 10
PAIRS_PER_LAYER = 2 * MIX2 + MIX2_IN + DC // 2

COLS = {}
_at = 0
for _name, _n in (("c", 8), ("b_ada", 48), ("g_mix", 8), ("g_ffn", 8), ("g_final", 8), ("norm_g", 96),
                  ("b_gate", 16), ("d_skip", 2), ("b_glu", 2), ("w_conv", 48), ("b_conv", 16),
                  ("conv_w2", 12), ("pool_scale", 4), ("slopes", 8), ("a_re", 8), ("a_im", 8), ("log_dt", 8),
                  ("inv_head", 32), ("inv_w", 2),
                  ("b_re", 128), ("b_im", 128), ("c_re", 128), ("c_im", 128)):
    COLS[_name] = (_at, _n)
    _at += _n
N_COLS = _at
TABS = {}
_at = 0
for _name, _n in (("ident", 128), ("tri", 128), ("ones", 128), ("strict", 128), ("dist", 512), ("count", 512),
                  ("w_glu", 512), ("pool_w", 256)):
    TABS[_name] = (_at, _n)
    _at += _n
N_TABS = _at
TILE_STEPS, HEADS1_STEPS, MERGE_STEPS, CONV_STEPS, HEADS2_STEPS = 19, 2 * 19 + 2 + 8, 2, 2, 8
LAYER_STEPS = 3 + 3 * 9 + 2 + HEAD_PAIRS * HEADS2_STEPS + 1 + 7 + 9 + 8

TWO_PI_1, TWO_PI_2, TWO_PI_3 = 6.28125, 0.0019350051879882812, 3.0199159819567e-07
INV_TWO_PI = 0.15915494309189535
ROUND_MAGIC = 12582912.0
PI_SAFE, HALF_PI = 3.1415925, 1.5707963267948966


class Steps:

    def __init__(self, eng, sem):
        self.eng, self.sem, self.at, self.calls = eng, sem, 0, 0

    def __call__(self, ins):
        ins.then_inc(self.sem, 1)
        self.at = self.at + 1
        self.calls += 1
        self.eng.wait_ge(self.sem, self.at)

    def enter(self, i, per_turn):
        start = self.at
        self.at = i * per_turn + start
        return start


def program(nc, d):
    ctx = ExitStack()
    with ctx:
        def sb(name, shape, dt=F32):
            return ctx.enter_context(nc.sbuf_tensor(name, shape, dt))

        def sem(name):
            return ctx.enter_context(nc.semaphore(name))

        cols = sb("cols", [P, N_COLS])
        tabs = sb("tabs", [P, N_TABS])
        x = sb("x", [P, DC, T])
        u_hi = sb("u_hi", [P, DC, T], F32R)
        u_lo = sb("u_lo", [P, DC, T], F32R)
        h_at = nc.sbuf_base
        h_hi = sb("h_hi", [P, HALF2, T], F32R)
        h_lo = sb("h_lo", [P, HALF2 + 1, T], F32R)
        f = sb("f", [P, DC, T])
        raw = sb("raw", [P, 2, RING])
        w_hi = sb("w_hi", [P, 2, RING], F32R)
        w_lo = sb("w_lo", [P, 2, RING], F32R)
        arena = sb("arena", [P, 26 * T])
        rstd = sb("rstd", [P, T])
        mod = sb("mod", [P, 48])
        amp = sb("amp", [P, 16])
        c_act = sb("c_act", [P, 8])
        half_g = sb("half_g", [P, 96])
        eps = sb("eps", [P, 1])
        ident_b = sb("ident_b", [P, P], BF16)
        mask_b = sb("mask_b", [P, P], BF16)
        stat = sb("stat", [P, 32])
        us = sb("us", [P, 2, T])
        B_t = sb("B_t", [P, 4, P])
        C_t = sb("C_t", [P, 2, SSM_TILES, 32])
        co = sb("co", [P, 26, 8])
        E1 = sb("E1", [P, 2, SSM_TILES, 16])
        E16 = sb("E16", [P, 2, SSM_TILES, 32])
        pool_w = sb("pool_w", [P, 2, P])

        def slot(n, k=1):
            return arena[:, n * T:(n + k) * T]

        def slots(n, k):
            return slot(n, k).rearrange("p (c t) -> p c t", t=T)

        gates = slots(0, 16)
        sq, acc, std, ux = slots(0, 2), slot(2), slot(3), slots(4, 2)
        ffn_g, ffn_s, ffn_u, ffn_h = slot(6), slot(7), slot(8), slot(9)
        a_pad = arena[:, 10 * T:10 * T + T + 2]
        q_st, k_st, vT_st = slot(16), slot(17), slot(18)
        v_nat = slots(19, 1)[:, 0, :].rearrange("p (i d) -> p i d", d=P)
        nsc, bias_h = slots(20, 2), slot(25)
        pt_all = arena[:, 22 * T:24 * T + 2 * P]
        sp = slots(0, 8).rearrange("p (h i) t -> p h i t", h=2)
        a_keys, softp, nq_st = slots(8, 4), slots(12, 2), slot(20)
        padded = arena[:, 0:2 * (T + 16)].rearrange("p (a t) -> p a t", a=2)
        cx = slots(6, 4)
        gelu_y, glu_s, ssm_y = slots(16, 2), slots(18, 2), slots(20, 2)
        ssm_tmp = nc.alloc_sbuf_tensor_at("ssm_tmp", [P, 7, T], F32, offset=h_at)
        bu_im = nc.alloc_sbuf_tensor_at("bu_im", [P, SSM_TILES, T], F32, offset=h_at + 15 * T * 4)
        ada_acc = nc.alloc_sbuf_tensor_at("ada_acc", [P, 2 * D], F32, offset=h_at)
        ada_w = nc.alloc_sbuf_tensor_at("ada_w", [P, 2, 2 * D], F32, offset=h_at + 2 * D * 4)
        bu_re = f
        banks = [ctx.enter_context(nc.psum_tensor(n, [P, T], F32)) for n in
                 ("unit_bank0", "unit_bank1", "stat_bank", "score0", "score1", "mix0", "mix1", "out_bank")]
        unit_bank, stat_bank, score, mix, out_bank = banks[0:2], banks[2], banks[3:5], banks[5:7], banks[7]

        consts_loaded = sem("consts_loaded")
        x_loaded = sem("x_loaded")
        ada_loaded = [sem(f"ada_loaded{i}") for i in range(2)]
        raw_loaded = [sem(f"raw_loaded{i}") for i in range(2)]
        hi_ready = sem("hi_ready")
        lo_ready = sem("lo_ready")
        unit_done = sem("unit_done")
        taken = [sem(f"taken{i}") for i in range(2)]
        cact_ready = sem("cact_ready")
        ada_used = sem("ada_used")
        mod_sum = sem("mod_sum")
        mod_ready = sem("mod_ready")
        prep_ready = sem("prep_ready")
        sq_ready = sem("sq_ready")
        sq_used = sem("sq_used")
        fsq_ready = sem("fsq_ready")
        fsq_added = sem("fsq_added")
        fsum_ready = sem("fsum_ready")
        std_ready = sem("std_ready")
        ux_ready = sem("ux_ready")
        uhi_ready = sem("uhi_ready")
        u_ready = sem("u_ready")
        x_ready = sem("x_ready")
        conv_ready = sem("conv_ready")
        silu_ready = sem("silu_ready")
        hidden_ready = sem("hidden_ready")
        hhi_ready = sem("hhi_ready")
        h_ready = sem("h_ready")
        ssm_act, ssm_vec = sem("ssm_act"), sem("ssm_vec")
        B_padded, B_turned, B_ready = sem("B_padded"), sem("B_turned"), sem("B_ready")
        bu_done, bu_ready = sem("bu_done"), sem("bu_ready")
        scan_ready = sem("scan_ready")
        y_done, y_ready, gelu_ready, glu_done, glu_ready, yy_ready, yhi_ready, y_split = (
            sem(n) for n in ("y_done", "y_ready", "gelu_ready", "glu_done", "glu_ready", "yy_ready",
                             "yhi_ready", "y_split"))
        v_turned, v_ready = sem("v_turned"), sem("v_ready")
        s_done, s_biased, p_ready, p_weighted, p_scaled, p_turned, pT_ready, pv_done = (
            sem(n) for n in ("s_done", "s_biased", "p_ready", "p_weighted", "p_scaled", "p_turned",
                             "pT_ready", "pv_done"))
        ohi_ready, o_taken = sem("ohi_ready"), sem("o_taken")
        sig_ready, ym_done, merged_ready, mhi_ready, m_ready = (
            sem(n) for n in ("sig_ready", "ym_done", "merged_ready", "mhi_ready", "m_ready"))
        v2_turned, v2_ready = sem("v2_turned"), sem("v2_ready")
        z_done, softp_ready, sp_ready, R_done, a_ready, pv2_done, ohi2_ready, o2_taken = (
            sem(n) for n in ("z_done", "softp_ready", "sp_ready", "R_done", "a_ready", "pv2_done",
                             "ohi2_ready", "o2_taken"))
        pool_in, pool_done, phi_ready, conv2_ready, chi_ready, cat_ready = (
            sem(n) for n in ("pool_in", "pool_done", "phi_ready", "conv2_ready", "chi_ready", "cat_ready"))
        vec_step, act_step = sem("vec_step"), sem("act_step")
        vec_passed = sem("vec_passed")
        out_stored = sem("out_stored")

        def col(name, i=0, n=1):
            return cols[:, bass.ds(COLS[name][0] + i, n)]

        def tab(name, a=0, b=None):
            at, n = TABS[name]
            return tabs[:, at + a:at + (n if b is None else b)]

        def as32(ap):
            return ap.bitcast(F32)

        def in_pair(j, n):
            return IN1 + 1 + 3 * j + n

        def layer(l):
            return LAYER0 + PAIRS_PER_LAYER * l

        def ffn2(l, s):
            return layer(l) + s * (MIX2 + MIX2_IN + DC // 2)

        def pT(b):
            return pt_all[:, P * b * (b + 1) // 2:P * (b + 1) * (b + 2) // 2].rearrange("p (i t) -> p i t", t=P)

        CONSTS = 32
        LAST_PAIR = LAYER0 + LAYERS * PAIRS_PER_LAYER
        block = ctx.enter_context(nc.Block())

        @block.sync
        def _(sp_eng):
            e = sp_eng
            e.dma_start(cols[:], d["cols"]).then_inc(consts_loaded, 16)
            e.dma_start(x[:], d["x"]).then_inc(x_loaded, 16)
            e.dma_start(tabs[:], d["tabs"]).then_inc(consts_loaded, 16)

            def load(p, s, src, n):
                if not isinstance(p, int) or p > 0:
                    e.wait_ge(lo_ready, 2 * p + s - 1)
                e.dma_start(raw[:, s, 0:n], src).then_inc(raw_loaded[s], 16)

            def load_pairs(p0, w, first, pairs):
                n = w.shape[2]
                with e.Fori(0, pairs) as i:
                    for s in range(2):
                        load(p0 + i, s, w[bass.ds(first + 2 * i + s, 1), :, :].rearrange("a p n -> p (a n)"), n)

            for s in range(2):
                load(0, s, d["w_in"][s], D)
            with e.Fori(0, 3) as g:
                for k in range(DC):
                    if k >= 2:
                        e.wait_ge(ada_used, DC * g + k - 1)
                    else:
                        e.wait_ge(mod_ready, g + 1)
                    e.dma_start(ada_w[:, k % 2, :], d["w_ada"][bass.ds(DC * g + k, 1), :, :].rearrange(
                        "a p n -> p (a n)")).then_inc(ada_loaded[k % 2], 16)
            load_pairs(1, d["w_in"], 2, MERGE1 - 1)
            load_pairs(MERGE1, d["w_merge"], 0, DC // 2)
            load_pairs(OUT1, d["w_out"], 0, DC // 2)
            for half in range(2):
                load_pairs(FFN1 + half * FFN1_HALF, d["w_up"], 2 * HALF1 * half, HALF1)
                load_pairs(FFN1 + half * FFN1_HALF + HALF1, d["w_down"], DC * half, DC // 2)
            with e.Fori(0, LAYERS) as l:
                for s in range(2):
                    for half in range(2):
                        n = 2 * (2 * l + s) + half
                        load_pairs(ffn2(l, s) + half * FFN2_HALF, d["w_gate_up"], 2 * HALF2 * n, HALF2)
                        load_pairs(ffn2(l, s) + half * FFN2_HALF + HALF2, d["w_down2"], DC * n, DC // 2)
                    if s == 0:
                        load_pairs(layer(l) + MIX2, d["w_in2"], 2 * MIX2_IN * l, MIX2_IN)
                        load_pairs(layer(l) + MIX2 + MIX2_IN, d["w_out2"], DC * l, DC // 2)
            for c in range(DC):
                e.wait_ge(x_ready, DC * 3 * LAYERS + c + 1)
                e.dma_start(d["out"][c], x[:, c, :]).then_inc(out_stored, 16)
            e.wait_ge(out_stored, 16 * DC)

        @block.gpsimd
        def _(e):
            def split_pairs(p0, pairs, n):
                with e.Fori(0, pairs) as i:
                    for s in range(2):
                        e.wait_ge(hi_ready, 2 * (p0 + i) + s + 1)
                        e.tensor_tensor(w_lo[:, s, 0:n], raw[:, s, 0:n], as32(w_hi[:, s, 0:n]),
                                        ALU.subtract).then_inc(lo_ready, 1)

            split_pairs(IN1, MERGE1 - IN1, D)
            split_pairs(MERGE1, DC // 2, 6 * P)
            split_pairs(OUT1, LAYER0 - OUT1, D)
            with e.Fori(0, LAYERS) as l:
                for s in range(2):
                    for half in range(2):
                        split_pairs(ffn2(l, s) + half * FFN2_HALF, HALF2, D)
                        split_pairs(ffn2(l, s) + half * FFN2_HALF + HALF2, DC // 2, RING)
                    if s == 0:
                        split_pairs(layer(l) + MIX2, MIX2_IN + DC // 2, D)

        @block.tensor
        def _(e):
            def unit(p, s, hi, lo, ks, bank=None, first=0, before=None, signal=True):
                bank = unit_bank[s] if bank is None else bank
                if signal is True or signal == "first":
                    e.wait_ge(lo_ready, 2 * p + s + 1)
                    e.wait_ge(taken[s], p + 1)
                for n, k in enumerate(ks):
                    if before:
                        before(n)
                    wh = w_hi[:, s, (first + n) * P:(first + n + 1) * P]
                    wl = w_lo[:, s, (first + n) * P:(first + n + 1) * P]
                    last = n == len(ks) - 1
                    e.matmul(bank[:], wh, hi(k), start=n == 0, stop=False)
                    e.matmul(bank[:], wh, lo(k), start=False, stop=False)
                    mm = e.matmul(bank[:], wl, hi(k), start=False, stop=last)
                if signal is True or signal == "last":
                    mm.then_inc(unit_done, 1)

            def from_u(k):
                return u_hi[:, k, :]

            def from_u_lo(k):
                return u_lo[:, k, :]

            def from_h(k):
                return h_hi[:, k, :]

            def from_h_lo(k):
                return h_lo[:, k, :]

            EIGHT = range(DC)

            def in_unit(p, s):
                unit(p, s, from_u, from_u_lo, EIGHT)

            def add_square(q, c):
                e.wait_ge(sq_ready, DC * q + c + 1)
                e.matmul(stat_bank[:], tab("ones"), sq[:, c % 2, :], start=c == 0,
                         stop=c == DC - 1).then_inc(sq_used, 1)

            def u_chunk(n, q=None):
                def wait(c):
                    if q is not None:
                        add_square(q, c)
                    e.wait_ge(u_ready, DC * n + c + 1)
                return wait

            def h_chunk(h0):
                return lambda c: e.wait_ge(h_ready, h0 + c + 1)

            def down(p0, h0, n_k):
                with e.Fori(0, DC // 2) as i:
                    unit(p0 + i, 0, from_h, from_h_lo, range(n_k), before=h_chunk(h0))
                    unit(p0 + i, 1, from_h, from_h_lo, range(n_k))

            def f_sum(r):
                e.wait_ge(fsq_added, (DC + 1) * (r + 1))
                e.matmul(stat_bank[:], tab("ones"), acc, start=True, stop=True).then_inc(fsum_ready, 1)

            def turn_v(free, free_at, src_sem, src_at, done):
                e.wait_ge(free, free_at)
                e.wait_ge(src_sem, src_at)
                for i in range(TB):
                    mm = e.transpose(out_bank[:, i * P:(i + 1) * P], vT_st[:, i * P:(i + 1) * P], tab("ident"))
                mm.then_inc(done, 1)

            def mixer2(l):
                pm = layer(l) + MIX2

                def head_pair(j, first):
                    J = HEAD_PAIRS * l + j

                    def z(n):
                        h, i = n // TB, TB - 1 - n % TB
                        if n == 0:
                            for s in range(2):
                                e.wait_ge(taken[s], pm + 2 * j + 2)
                        if n >= 2:
                            e.wait_ge(sp_ready, 8 * J + n - 1)
                        rows = slice(HD * h, HD * h + HD)
                        e.matmul(score[n % 2][:, 0:T - i * P], k_st[rows, i * P:(i + 1) * P], q_st[rows, i * P:T],
                                 start=True, stop=True).then_inc(z_done, 1)

                    def keep_sums(n):
                        h, i = n // TB, TB - 1 - n % TB
                        e.wait_ge(sp_ready, 8 * J + n + 1)
                        if n >= 2:
                            e.wait_ge(a_ready, 8 * J + n - 1)
                        R = mix[n % 2]
                        rows = slice(HD * h, HD * h + HD)
                        e.matmul(R[:, 0:T - i * P], tab("tri"), sp[:, h, i, 0:T - i * P], start=True, stop=False)
                        for m in range(i + 1, TB):
                            e.matmul(R[:, (m - i) * P:T - i * P], tab("ones"), sp[:, h, m, 0:T - m * P],
                                     start=False, stop=False)
                        e.matmul(R[:, 0:P], ident_b[:], mask_b[:], start=False, stop=False)
                        e.matmul(R[:, 0:T - i * P], k_st[rows, i * P:(i + 1) * P], nq_st[rows, i * P:T],
                                 start=False, stop=True).then_inc(R_done, 1)

                    def values(h):
                        if h == 0:
                            e.wait_ge(v2_ready, J + 1)
                        e.wait_ge(a_ready, 8 * J + TB * (h + 1))
                        rows = slice(HD * h, HD * h + HD)
                        for i in range(TB):
                            mm = e.matmul(out_bank[rows, i * P:T], v_nat[:, i, rows], a_keys[:, i, 0:T - i * P],
                                          start=i == 0, stop=i == TB - 1)
                        mm.then_inc(pv2_done, 1)

                    if first:
                        unit(pm, 0, from_u, from_u_lo, EIGHT, before=u_chunk(3 + 3 * l, 4 + 3 * l))
                    else:
                        in_unit(pm + 2 * j, 0)
                    in_unit(pm + 2 * j, 1)
                    in_unit(pm + 2 * j + 1, 0)
                    z(0)
                    z(1)
                    in_unit(pm + 2 * j + 1, 1)
                    turn_v(o2_taken, J + 1, taken[0], pm + 2 * j + 3, v2_turned)
                    for n in range(2 * TB):
                        keep_sums(n)
                        if n + 2 < 2 * TB:
                            z(n + 2)
                        if n == TB - 1:
                            values(0)
                    values(1)

                head_pair(0, True)
                with e.Fori(1, HEAD_PAIRS) as j:
                    head_pair(j, False)
                for i in range(2):
                    for s in range(2):
                        in_unit(pm + 2 * HEAD_PAIRS + i, s)
                for m in range(2):
                    e.wait_ge(pool_in, 2 * l + m + 1)
                    e.matmul(score[m][:], pool_w[:, m, :], ux[:, m, :], start=True, stop=True).then_inc(pool_done, 1)
                def cat_chunk(c):
                    if c < HEAD_PAIRS:
                        e.wait_ge(o2_taken, HEAD_PAIRS * l + c + 2)
                    else:
                        e.wait_ge(cat_ready, 4 * l + (3, 4, 1, 2)[c - HEAD_PAIRS])

                with e.Fori(0, DC // 2) as i:
                    unit(pm + MIX2_IN + i, 0, from_h, from_h_lo, EIGHT,
                         before=cat_chunk)
                    unit(pm + MIX2_IN + i, 1, from_h, from_h_lo, EIGHT)
                f_sum(3 * l + 1)

            e.wait_ge(consts_loaded, CONSTS)
            with e.Fori(0, 3) as g:
                e.wait_ge(ada_used, DC * g + DC)
                e.wait_ge(mod_ready, g + 1)
                for c in range(16):
                    mm = e.matmul(out_bank[:, c:c + 1], ada_acc[:, c * P:(c + 1) * P], tab("ones", 0, 1),
                                  start=True, stop=True)
                mm.then_inc(mod_sum, 1)
            for c in EIGHT:
                add_square(0, c)

            unit(IN1, 0, from_u, from_u_lo, EIGHT, before=u_chunk(0))
            in_unit(IN1, 1)
            e.wait_ge(B_padded, 1)
            for n in range(4):
                mm = e.transpose(out_bank[:, n * P:(n + 1) * P], slot(22, 1)[:, n * P:(n + 1) * P], tab("ident"))
            mm.then_inc(B_turned, 1)
            e.wait_ge(B_ready, 1)
            for s in range(2):
                e.wait_ge(taken[s], 2)
            for i in range(SSM_TILES):
                rows = slice(32 * (i % 4), 32 * (i % 4) + 32)
                for part in range(2):
                    n = 2 * i + part
                    if n >= 2:
                        e.wait_ge(bu_ready, n - 1)
                    e.matmul(score[part][:], B_t[rows, 2 * part + i // 4, :], us[rows, i // 4, :],
                             start=True, stop=True).then_inc(bu_done, 1)

            with e.Fori(0, HEAD_PAIRS) as j:
                def scores(n):
                    h, b = divmod(n, TB)
                    if n == 0:
                        for s in range(2):
                            e.wait_ge(taken[s], in_pair(j, 0) + 2)
                    if n >= 2:
                        e.wait_ge(s_biased, 8 * j + n - 1)
                    rows = slice(HD * h, HD * h + HD)
                    e.matmul(score[n % 2][:, 0:(b + 1) * P], q_st[rows, b * P:(b + 1) * P],
                             k_st[rows, 0:(b + 1) * P], start=True, stop=True).then_inc(s_done, 1)

                def turn_probs(n):
                    e.wait_ge(p_scaled, 8 * j + n + 1)
                    if n >= 2:
                        e.wait_ge(pT_ready, 8 * j + n - 1)
                    for i in range(n % TB + 1):
                        mm = e.transpose(mix[n % 2][:, i * P:(i + 1) * P], nsc[:, n % 2, i * P:(i + 1) * P],
                                         tab("ident"))
                    mm.then_inc(p_turned, 1)

                def values(h):
                    e.wait_ge(v_ready, j + 1)
                    e.wait_ge(pT_ready, 8 * j + TB * (h + 1))
                    rows = slice(HD * h, HD * h + HD)
                    for b in range(TB):
                        for i in range(b + 1):
                            mm = e.matmul(out_bank[rows, b * P:(b + 1) * P], v_nat[:, i, rows], pT(b)[:, i, :],
                                          start=i == 0, stop=i == b)
                    mm.then_inc(pv_done, 1)

                in_unit(in_pair(j, 0), 0)
                in_unit(in_pair(j, 0), 1)
                in_unit(in_pair(j, 1), 0)
                in_unit(in_pair(j, 1), 1)
                turn_v(o_taken, j + 1, taken[0], in_pair(j, 1) + 2, v_turned)
                scores(0)
                scores(1)
                in_unit(in_pair(j, 2), 0)
                turn_probs(0)
                scores(2)
                turn_probs(1)
                scores(3)
                in_unit(in_pair(j, 2), 1)
                for n in range(2, TB):
                    turn_probs(n)
                    scores(n + 2)
                values(0)
                for n in range(TB, 2 * TB):
                    turn_probs(n)
                    if n + 2 < 2 * TB:
                        scores(n + 2)
                values(1)
            with e.Fori(0, 2) as i:
                for s in range(2):
                    in_unit(in_pair(HEAD_PAIRS, 0) + i, s)
            e.wait_ge(scan_ready, SSM_TILES)
            for i in range(SSM_TILES):
                rows = slice(32 * (i % 4), 32 * (i % 4) + 32)
                e.matmul(mix[i // 4][rows, :], C_t[:, 0, i, :], bu_re[:, i, :], start=True, stop=False)
                e.matmul(mix[i // 4][rows, :], C_t[:, 1, i, :], bu_im[:, i, :], start=False,
                         stop=True).then_inc(y_done, 1)
            e.wait_ge(gelu_ready, 2)
            for m in range(2):
                for k in range(2):
                    mm = e.matmul(score[m][:], tab("w_glu", 256 * k + P * m, 256 * k + P * m + P),
                                  gelu_y[:, k, :], start=k == 0, stop=k == 1)
                mm.then_inc(glu_done, 1)
            e.wait_ge(y_split, 2)
            e.wait_ge(o_taken, HEAD_PAIRS + 1)
            with e.Fori(0, DC // 2) as i:
                for s in range(2):
                    p = MERGE1 + i
                    unit(p, s, lambda k: h_hi[:, 5 + k, :], lambda k: h_lo[:, 4 + k, :], range(2),
                         bank=score[s], signal="first")
                    unit(p, s, lambda k: h_hi[:, 7 + k, :], lambda k: h_lo[:, k, :], range(4), first=2,
                         signal="last")
            with e.Fori(0, DC // 2) as i:
                unit(OUT1 + i, 0, from_u, from_u_lo, EIGHT, before=lambda c: e.wait_ge(m_ready, c + 1))
                unit(OUT1 + i, 1, from_u, from_u_lo, EIGHT)

            for c in EIGHT:
                add_square(1, c)
            for half in range(2):
                p0 = FFN1 + half * FFN1_HALF
                with e.Fori(0, HALF1) as i:
                    unit(p0 + i, 0, from_u, from_u_lo, EIGHT, before=u_chunk(1))
                    in_unit(p0 + i, 1)
                down(p0 + HALF1, HALF1 * half, HALF1)
            for c in EIGHT:
                add_square(2, c)

            with e.Fori(0, LAYERS) as l:
                for s_ffn in range(2):
                    k_norm = 2 * s_ffn
                    for half in range(2):
                        p0 = ffn2(l, s_ffn) + half * FFN2_HALF
                        if half == 0:
                            unit(p0, 0, from_u, from_u_lo, EIGHT,
                                 before=u_chunk(2 + 3 * l + k_norm, 3 + 3 * l + k_norm))
                            in_unit(p0, 1)
                        with e.Fori(1 - half, HALF2) as i:
                            in_unit(p0 + i, 0)
                            in_unit(p0 + i, 1)
                        down(p0 + HALF2, 16 + 44 * l + 22 * s_ffn + HALF2 * half, HALF2)
                    f_sum(3 * l + k_norm)
                    if s_ffn == 0:
                        mixer2(l)


        @block.scalar
        def _(e):
            def settled():
                e.wait_ge(consts_loaded, CONSTS)

            def refill(p, s, n=D):
                if not isinstance(p, int) or p > 0:
                    e.wait_ge(unit_done, 2 * p + s - 1)
                e.wait_ge(raw_loaded[s], 16 * p + 16)
                e.activation(w_hi[:, s, 0:n], raw[:, s, 0:n], ACT.Copy).then_inc(hi_ready, 1)

            def square(q, c):
                if not (isinstance(q, int) and DC * q + c < 2):
                    e.wait_ge(sq_used, DC * q + c - 1)
                e.activation(sq[:, c % 2, :], x[:, c, :], ACT.Square).then_inc(sq_ready, 1)

            def root():
                e.activation(std, stat_bank[:], ACT.Sqrt, bias=eps[:], scale=1.0 / D).then_inc(std_ready, 1)

            def shifted(n, shift):
                for c in range(DC):
                    e.wait_ge(ux_ready, DC * n + c + 1)
                    e.activation(u_hi[:, c, :], ux[:, c % 2, :], ACT.Identity,
                                 bias=mod[:, shift + c:shift + c + 1]).then_inc(uhi_ready, 1)

            e.wait_ge(consts_loaded, CONSTS)
            refill(0, 0)
            refill(0, 1)
            e.activation(c_act[:], col("c", 0, 8), ACT.Silu).then_inc(cact_ready, 1)
            e.activation(co[:, 0, :], col("log_dt", 0, 8), ACT.Exp).then_inc(ssm_act, 1)
            e.wait_ge(ssm_vec, 1)
            e.activation(co[:, 3, :], co[:, 1, :], ACT.Exp)
            e.activation(co[:, 7, :], co[:, 5, :], ACT.Sin)
            e.activation(co[:, 8, :], co[:, 6, :], ACT.Sin).then_inc(ssm_act, 1)

            e.wait_ge(x_loaded, 16)
            e.wait_ge(prep_ready, 1)
            for c in range(DC):
                square(0, c)
            e.wait_ge(sq_used, DC)
            root()
            shifted(0, 0)
            for s in range(2):
                refill(IN1 + 1, s)
                e.activation(us[:, s, :], unit_bank[s][:], ACT.Copy).then_inc(taken[s], 1)
            for n in range(2 * SSM_TILES):
                e.wait_ge(bu_done, n + 1)
                e.activation((bu_re, bu_im)[n % 2][:, n // 2, :], score[n % 2][:], ACT.Copy).then_inc(bu_ready, 1)

            with e.Fori(0, HEAD_PAIRS) as j:
                def gate(s, g):
                    settled()
                    e.activation(gates[:, bass.ds(g, 1), :].rearrange("p a t -> p (a t)"), unit_bank[s][:],
                                 ACT.Identity, bias=col("b_gate", g)).then_inc(taken[s], 1)

                def exps(n):
                    W = (n % TB + 1) * P
                    e.wait_ge(s_biased, 8 * j + n + 1)
                    e.activation(nsc[:, n % 2, 0:W], nsc[:, n % 2, 0:W], ACT.Exp, bias=stat[:, n:n + 1],
                                 scale=-1.0).then_inc(p_ready, 1)

                def divide(n):
                    W = (n % TB + 1) * P
                    e.wait_ge(p_weighted, 8 * j + n + 1)
                    e.activation(nsc[:, n % 2, 0:W], nsc[:, n % 2, 0:W], ACT.Identity,
                                 scale=stat[:, 16 + n:17 + n]).then_inc(p_scaled, 1)

                refill(in_pair(j, 1), 0)
                e.activation(q_st, unit_bank[0][:], ACT.Copy, scale=-ATT_SCALE).then_inc(taken[0], 1)
                refill(in_pair(j, 1), 1)
                e.activation(k_st, unit_bank[1][:], ACT.Copy).then_inc(taken[1], 1)
                refill(in_pair(j, 2), 0)
                e.activation(vT_st, unit_bank[0][:], ACT.Copy).then_inc(taken[0], 1)
                refill(in_pair(j, 2), 1)
                gate(1, 3 * j)
                for n in (0, 1):
                    exps(n)
                for n in (0, 1):
                    divide(n)
                refill(in_pair(j, 3), 0)
                gate(0, 3 * j + 1)
                for n in (2, 3):
                    exps(n)
                for n in (2, 3):
                    divide(n)
                refill(in_pair(j, 3), 1)
                gate(1, 3 * j + 2)
                for n in (4, 5):
                    exps(n)
                for n in (4, 5):
                    divide(n)
                for n in (6, 7):
                    exps(n)
                for n in (6, 7):
                    divide(n)
                e.wait_ge(pv_done, 2 * j + 2)
                settled()
                e.activation(h_hi[:, bass.ds(7 + j, 1), :].rearrange("p a t -> p (a t)"), out_bank[:],
                             ACT.Copy).then_inc(ohi_ready, 1)
            for i in range(2):
                p = in_pair(HEAD_PAIRS, 0) + i
                for s in range(2):
                    refill(p + 1, s, D if i == 0 else 6 * P)
                    g = 3 * HEAD_PAIRS + 2 * i + s
                    e.activation(gates[:, g, :], unit_bank[s][:], ACT.Identity,
                                 bias=col("b_gate", g)).then_inc(taken[s], 1)
            for m in range(2):
                e.wait_ge(y_ready, m + 1)
                e.activation(gelu_y[:, m, :], ssm_y[:, m, :], ACT.Gelu_apprx_tanh).then_inc(gelu_ready, 1)
            for m in range(2):
                e.wait_ge(glu_done, m + 1)
                e.activation(glu_s[:, m, :], score[m][:], ACT.Sigmoid, bias=col("b_glu", m)).then_inc(glu_ready, 1)
            for m in range(2):
                e.wait_ge(yy_ready, m + 1)
                e.activation(h_hi[:, 5 + m, :], ssm_y[:, m, :], ACT.Copy).then_inc(yhi_ready, 1)
            by_branch = gates.rearrange("p (g c) t -> p g c t", g=2)

            def merge(i, n):
                for s in range(2):
                    g = by_branch[:, :, bass.ds(2 * i + s, 1), :].rearrange("p g a t -> p g (a t)")
                    settled()
                    e.activation(g, g, ACT.Sigmoid).then_inc(sig_ready, 1)
                for s in range(2):
                    refill(MERGE1 + i + 1, s, n)
                    e.wait_ge(merged_ready, 2 * i + s + 1)
                    settled()
                    e.activation(u_hi[:, bass.ds(2 * i + s, 1), :].rearrange("p a t -> p (a t)"),
                                 slot(22 + s), ACT.Copy).then_inc(mhi_ready, 1)

            with e.Fori(0, DC // 2 - 1) as i:
                merge(i, 6 * P)
            merge(DC // 2 - 1, D)
            with e.Fori(0, DC // 2) as i:
                for s in range(2):
                    refill(OUT1 + i + 1, s)

            for c in range(DC):
                e.wait_ge(taken[c % 2], OUT1 + c // 2 + 2)
                square(1, c)
            e.wait_ge(sq_used, 2 * DC)
            root()
            shifted(1, 24)
            for half in range(2):
                p0 = FFN1 + half * FFN1_HALF
                with e.Fori(0, HALF1) as i:
                    refill(p0 + i + 1, 0)
                    e.wait_ge(prep_ready, 2)
                    e.activation(a_pad[:, 2:T + 2], unit_bank[0][:], ACT.Copy).then_inc(taken[0], 1)
                    e.wait_ge(conv_ready, HALF1 * half + i + 1)
                    e.activation(ffn_s, ffn_u, ACT.Silu).then_inc(silu_ready, 1)
                    refill(p0 + i + 1, 1)
                    e.wait_ge(taken[1], p0 + i + 2)
                    settled()
                    e.activation(h_hi[:, bass.ds(i, 1), :].rearrange("p a t -> p (a t)"), ffn_h,
                                 ACT.Copy).then_inc(hhi_ready, 1)
                with e.Fori(0, DC // 2 - half) as i:
                    for s in range(2):
                        refill(p0 + HALF1 + i + 1, s)
            for c in range(DC):
                e.wait_ge(taken[c % 2], LAYER0 - DC // 2 + c // 2 + 2)
                square(2, c)
            e.wait_ge(sq_used, 3 * DC)
            root()

            with e.Fori(0, LAYERS) as l:
                def pre_norm(k):
                    for c in range(DC):
                        e.wait_ge(x_ready, DC * (3 * l + k) + c + 1)
                        settled()
                        e.activation(u_hi[:, c, :], x[:, c, :], ACT.Identity,
                                     scale=col("norm_g", (6 * l + 2 * k) * DC + c)).then_inc(uhi_ready, 1)
                        square(3 + 3 * l + k, c)
                    e.wait_ge(sq_used, DC * (4 + 3 * l + k))
                    root()

                def f_squares(p, s, r, c):
                    e.wait_ge(taken[s], p + 2)
                    settled()
                    e.activation(sq[:, 0, :], f[:, bass.ds(c, 1), :].rearrange("p a t -> p (a t)"),
                                 ACT.Square).then_inc(fsq_ready, 1)

                def f_root(r):
                    e.wait_ge(fsum_ready, r + 1)
                    root()

                for s in range(2):
                    refill(layer(l), s)
                for s_ffn in range(2):
                    k_norm = 2 * s_ffn
                    pre_norm(k_norm)
                    for half in range(2):
                        p0 = ffn2(l, s_ffn) + half * FFN2_HALF
                        h0 = 16 + 44 * l + 22 * s_ffn + HALF2 * half

                        def hidden(i, n):
                            refill(p0 + i + 1, 0, n)
                            e.wait_ge(taken[0], p0 + i + 2)
                            e.activation(ffn_s, ffn_g, ACT.Silu).then_inc(silu_ready, 1)
                            refill(p0 + i + 1, 1, n)
                            e.wait_ge(hidden_ready, h0 - 16 + i + 1)
                            settled()
                            e.activation(h_hi[:, bass.ds(i, 1), :].rearrange("p a t -> p (a t)"), ffn_h,
                                         ACT.Copy).then_inc(hhi_ready, 1)

                        def out(i, n):
                            for s in range(2):
                                p = p0 + HALF2 + i
                                if n:
                                    refill(p + 1, s, n)
                                if half == 1:
                                    f_squares(p, s, 3 * l + k_norm, 2 * i + s)

                        with e.Fori(0, HALF2 - 1) as i:
                            hidden(i, D)
                        hidden(HALF2 - 1, RING)
                        with e.Fori(0, DC // 2 - 1) as i:
                            out(i, RING)
                        out(DC // 2 - 1, D if half == 0 or s_ffn == 0 else 0)
                    f_root(3 * l + k_norm)
                    if s_ffn:
                        continue
                    pm = layer(l) + MIX2
                    pre_norm(1)
                    with e.Fori(0, HEAD_PAIRS) as j:
                        J = HEAD_PAIRS * l + j

                        def softplus(n):
                            i = TB - 1 - n % TB
                            az = softp[:, n % 2, 0:T - i * P]
                            e.wait_ge(z_done, 8 * J + n + 1)
                            if n >= 2:
                                e.wait_ge(sp_ready, 8 * J + n - 1)
                            e.activation(az, score[n % 2][:, 0:T - i * P], ACT.Abs).then_inc(act_step, 1)
                            e.wait_ge(act_step, 16 * J + 2 * n + 1)
                            e.activation(az, az, ACT.Exp, scale=-1.0).then_inc(act_step, 1)
                            e.wait_ge(act_step, 16 * J + 2 * n + 2)
                            e.activation(az, az, ACT.Ln, bias=1.0).then_inc(softp_ready, 1)

                        def weights(n):
                            i = TB - 1 - n % TB
                            e.wait_ge(R_done, 8 * J + n + 1)
                            if n == TB:
                                e.wait_ge(pv2_done, 2 * J + 1)
                            e.activation(a_keys[:, i, 0:T - i * P], mix[n % 2][:, 0:T - i * P], ACT.Exp,
                                         scale=-1.0).then_inc(a_ready, 1)

                        refill(pm + 2 * j + 1, 0)
                        refill(pm + 2 * j + 1, 1)
                        refill(pm + 2 * j + 2, 0)
                        softplus(0)
                        softplus(1)
                        refill(pm + 2 * j + 2, 1)
                        for n in range(2 * TB):
                            weights(n)
                            if n + 2 < 2 * TB:
                                softplus(n + 2)
                        e.wait_ge(pv2_done, 2 * J + 2)
                        settled()
                        e.activation(h_hi[:, bass.ds(j, 1), :].rearrange("p a t -> p (a t)"), out_bank[:],
                                     ACT.Copy).then_inc(ohi2_ready, 1)
                    for i in range(2):
                        for s in range(2):
                            refill(pm + 2 * HEAD_PAIRS + i + 1, s)
                    for m in range(2):
                        e.wait_ge(pool_done, 2 * l + m + 1)
                        settled()
                        e.activation(h_hi[:, 6 + m, :], score[m][:], ACT.Identity,
                                     scale=col("pool_scale", 2 * l + m)).then_inc(phi_ready, 1)
                    for m in range(2):
                        e.wait_ge(conv2_ready, 2 * l + m + 1)
                        e.activation(h_hi[:, 4 + m, :], cx[:, 2 + m, :], ACT.Copy).then_inc(chi_ready, 1)
                    with e.Fori(0, DC // 2) as i:
                        for s in range(2):
                            refill(pm + MIX2_IN + i + 1, s)
                            f_squares(pm + MIX2_IN + i, s, 3 * l + 1, 2 * i + s)
                    f_root(3 * l + 1)

        @block.vector
        def _(e):
            step = Steps(e, vec_step)

            def settled():
                e.wait_ge(consts_loaded, CONSTS)

            def passed():
                e.sem_inc(vec_passed, 1)

            def flat(ap):
                return ap.rearrange("p a t -> p (a t)")

            for free in (*taken, mod_ready, o_taken, o2_taken):
                e.sem_inc(free, 1)
            settled()
            e.memset(eps[:], EPS)
            e.tensor_copy(ident_b[:], tab("ident"))
            e.tensor_scalar(mask_b[:], tab("strict"), -1e30, 1e30, ALU.mult, ALU.add)
            e.memset(C_t[:], 0.0)
            e.memset(pool_w[:], 0.0)
            e.memset(slot(22, 1), 0.0)
            step(e.tensor_scalar(half_g[:], col("norm_g", 0, 96), 0.5, None, ALU.mult))
            e.sem_inc(prep_ready, 1)

            def cc(n):
                return co[:, n, :]

            def tt(out, a, b, op):
                step(e.tensor_tensor(out, a, b, op))

            lr, li = col("a_re", 0, 8), col("a_im", 0, 8)
            dt, lrdt, ang, mag, turns, red, red_c, sin, cos, abr, abi, den, rden, fre, fim, t1, t2, zr, zi = (
                cc(n) for n in range(19))
            e.wait_ge(ssm_act, 1)
            tt(lrdt, lr, dt, ALU.mult)
            tt(ang, li, dt, ALU.mult)
            step(e.tensor_scalar(turns, ang, INV_TWO_PI, ROUND_MAGIC, ALU.mult, ALU.add))
            step(e.tensor_scalar(turns, turns, ROUND_MAGIC, None, ALU.subtract))
            step(e.scalar_tensor_tensor(red, turns, -TWO_PI_1, ang, ALU.mult, ALU.add))
            step(e.scalar_tensor_tensor(red, turns, -TWO_PI_2, red, ALU.mult, ALU.add))
            step(e.scalar_tensor_tensor(red, turns, -TWO_PI_3, red, ALU.mult, ALU.add))
            step(e.tensor_scalar(red, red, PI_SAFE, -PI_SAFE, ALU.min, ALU.max))
            step(e.scalar_tensor_tensor(t1, red, -1.0, red, ALU.mult, ALU.max))
            e.tensor_scalar(red_c, t1, -1.0, HALF_PI, ALU.mult, ALU.add).then_inc(ssm_vec, 1)
            e.wait_ge(ssm_act, 2)
            tt(abr, mag, cos, ALU.mult)
            tt(abi, mag, sin, ALU.mult)
            tt(t1, lr, lr, ALU.mult)
            tt(t2, li, li, ALU.mult)
            tt(den, t1, t2, ALU.add)
            step(e.reciprocal(rden, den))
            step(e.tensor_scalar(zr, abr, -1.0, None, ALU.add))
            tt(t1, zr, lr, ALU.mult)
            tt(t2, abi, li, ALU.mult)
            tt(t1, t1, t2, ALU.add)
            tt(fre, t1, rden, ALU.mult)
            tt(t1, abi, lr, ALU.mult)
            tt(t2, zr, li, ALU.mult)
            tt(t1, t1, t2, ALU.subtract)
            tt(fim, t1, rden, ALU.mult)

            def per_state(name):
                return col(name, 0, SSM_TILES * SSM_CH).rearrange("p (i c) -> p i c", c=SSM_CH)

            def wide(ap, n):
                return ap[:, :, None].broadcast_to([P, SSM_TILES, n])

            b1 = slot(23)[:, 0:P].rearrange("p (i c) -> p i c", c=SSM_CH)
            b2 = slot(24)[:, 0:P].rearrange("p (i c) -> p i c", c=SSM_CH)
            B_pad = slot(22).rearrange("p (k i c) -> p k i c", k=2, c=32)
            for part, (x1, x2, op) in enumerate(((fre, fim, ALU.subtract), (fim, fre, ALU.add))):
                tt(b1, per_state("b_re"), wide(x1, SSM_CH), ALU.mult)
                tt(b2, per_state("b_im"), wide(x2, SSM_CH), ALU.mult)
                for h in range(2):
                    rows, ch = slice(64 * h, 64 * h + 64), slice(SSM_CH * h, SSM_CH * h + SSM_CH)
                    tt(B_pad[rows, part, :, ch], b1[rows], b2[rows], op)
            for h in range(2):
                rows, ch = slice(64 * h, 64 * h + 64), slice(SSM_CH * h, SSM_CH * h + SSM_CH)
                step(e.tensor_copy(C_t[rows, 0, :, ch], per_state("c_re")[rows]))
                step(e.tensor_scalar(C_t[rows, 1, :, ch], per_state("c_im")[rows], -1.0, None, ALU.mult))
            e.sem_inc(B_padded, 1)

            e.memset(E1[:, 0, :, 0:1], 1.0)
            e.memset(E1[:, 1, :, 0:1], 0.0)
            e.memset(E16[:, 0, :, 0:1], 1.0)
            e.memset(E16[:, 1, :, 0:1], 0.0)
            step(e.tensor_copy(zr, cos))
            step(e.tensor_copy(zi, sin))
            for E, top in ((E1, 16), (E16, 32)):
                n = 1
                while n < top:
                    re, im = E[:, 0, :, 0:n], E[:, 1, :, 0:n]
                    p1 = slot(23)[:, 0:8 * n].rearrange("p (i c) -> p i c", c=n)
                    p2 = slot(24)[:, 0:8 * n].rearrange("p (i c) -> p i c", c=n)
                    tt(p1, re, wide(zr, n), ALU.mult)
                    tt(p2, im, wide(zi, n), ALU.mult)
                    tt(E[:, 0, :, n:2 * n], p1, p2, ALU.subtract)
                    tt(p1, re, wide(zi, n), ALU.mult)
                    tt(p2, im, wide(zr, n), ALU.mult)
                    tt(E[:, 1, :, n:2 * n], p1, p2, ALU.add)
                    tt(t1, zr, zr, ALU.mult)
                    tt(t2, zi, zi, ALU.mult)
                    step(e.scalar_tensor_tensor(zi, zr, 2.0, zi, ALU.mult, ALU.mult))
                    tt(zr, t1, t2, ALU.subtract)
                    n *= 2

            e.wait_ge(cact_ready, 1)
            with e.Fori(0, 3) as g:
                for k in range(DC):
                    e.wait_ge(ada_loaded[k % 2], 64 * g + 16 * (k // 2) + 16)
                    if k == 0:
                        e.tensor_scalar(ada_acc[:], ada_w[:, 0, :], c_act[:, 0:1], None,
                                        ALU.mult).then_inc(ada_used, 1)
                    else:
                        e.wait_ge(ada_used, DC * g + k)
                        e.scalar_tensor_tensor(ada_acc[:], ada_w[:, k % 2, :], c_act[:, k:k + 1], ada_acc[:],
                                               ALU.mult, ALU.add).then_inc(ada_used, 1)
                e.wait_ge(mod_sum, g + 1)
                e.tensor_tensor(mod[:, bass.ds(16 * g, 16)], out_bank[:, 0:16], col("b_ada", 16 * g, 16),
                                ALU.add).then_inc(mod_ready, 1)
            e.wait_ge(mod_ready, 4)
            for n, (g_name, scale) in enumerate((("g_mix", 8), ("g_ffn", 32))):
                step(e.scalar_tensor_tensor(amp[:, 8 * n:8 * n + 8], mod[:, scale:scale + 8], 1.0,
                                            col(g_name, 0, 8), ALU.add, ALU.mult))

            def invert(st):
                e.wait_ge(std_ready, st + 1)
                step(e.reciprocal(rstd[:], std))

            def modulate(n, st, shift):
                invert(st)
                for c in range(DC):
                    if c >= 2:
                        e.wait_ge(u_ready, DC * n + c - 1)
                    e.scalar_tensor_tensor(ux[:, c % 2, :], x[:, c, :], amp[:, 8 * n + c:8 * n + c + 1], rstd[:],
                                           ALU.mult, ALU.mult).then_inc(ux_ready, 1)
                    if c:
                        shift_lo(n, c - 1, shift)
                shift_lo(n, DC - 1, shift)

            def shift_lo(n, c, shift):
                e.wait_ge(uhi_ready, DC * n + c + 1)
                e.scalar_tensor_tensor(u_lo[:, c, :], ux[:, c % 2, :], mod[:, shift + c:shift + c + 1],
                                       as32(u_hi[:, c, :]), ALU.add, ALU.subtract).then_inc(u_ready, 1)

            modulate(0, 0, 0)
            e.wait_ge(B_turned, 1)
            e.tensor_copy(B_t[:].rearrange("p k n -> p (k n)"), out_bank[:]).then_inc(B_ready, 1)
            e.wait_ge(bu_ready, 2 * SSM_TILES)

            def scan_tile(i):
                c_t, s_t, p1, p2, wr, wi = (ssm_tmp[:, n, :] for n in range(6))
                br, bi = flat(bu_re[:, bass.ds(i, 1), :]), flat(bu_im[:, bass.ds(i, 1), :])
                r = co[:, 3, bass.ds(i, 1)].broadcast_to([P, T])

                def power(part, b_part, out, op):
                    grid = out.rearrange("p (a b) -> p a b", b=16)
                    big = flat(E16[:, part, bass.ds(i, 1), :])[:, :, None].broadcast_to([P, 32, 16])
                    small = flat(E1[:, b_part, bass.ds(i, 1), :])[:, None, :].broadcast_to([P, 32, 16])
                    tt(grid, big, small, op)

                power(0, 0, p1, ALU.mult)
                power(1, 1, p2, ALU.mult)
                tt(c_t, p1, p2, ALU.subtract)
                power(0, 1, p1, ALU.mult)
                power(1, 0, p2, ALU.mult)
                tt(s_t, p1, p2, ALU.add)
                tt(p1, c_t, br, ALU.mult)
                tt(p2, s_t, bi, ALU.mult)
                tt(wr, p1, p2, ALU.add)
                tt(p1, c_t, bi, ALU.mult)
                tt(p2, s_t, br, ALU.mult)
                tt(wi, p1, p2, ALU.subtract)
                step(e.tensor_tensor_scan(br, r, wr, 0.0, ALU.mult, ALU.add))
                step(e.tensor_tensor_scan(bi, r, wi, 0.0, ALU.mult, ALU.add))
                tt(p1, c_t, br, ALU.mult)
                tt(p2, s_t, bi, ALU.mult)
                tt(wr, s_t, br, ALU.mult)
                tt(wi, c_t, bi, ALU.mult)
                tt(br, p1, p2, ALU.subtract)
                e.tensor_tensor(bi, wr, wi, ALU.add).then_inc(scan_ready, 1)

            with e.Fori(0, HEAD_PAIRS) as j:
                start = step.enter(j, HEADS1_STEPS)

                def bias(h):
                    step(e.tensor_scalar(bias_h, tab("dist"), col("slopes", 2 * j + h), None, ALU.mult))

                def score_bias(n):
                    b = n % TB
                    W = (b + 1) * P
                    e.wait_ge(s_done, 8 * j + n + 1)
                    passed()
                    e.tensor_tensor_reduce(nsc[:, n % 2, 0:W], score[n % 2][:, 0:W], bias_h[:, T - W:T], 1.0, 3e38,
                                           ALU.add, ALU.min, stat[:, n:n + 1]).then_inc(s_biased, 1)

                def weigh(n):
                    W = (n % TB + 1) * P
                    e.wait_ge(p_ready, 8 * j + n + 1)
                    step(e.tensor_tensor_reduce(nsc[:, n % 2, 0:W], nsc[:, n % 2, 0:W], tab("count", T - W, T),
                                                1.0, 0.0, ALU.mult, ALU.add, stat[:, 8 + n:9 + n]))
                    e.reciprocal(stat[:, 16 + n:17 + n], stat[:, 8 + n:9 + n]).then_inc(p_weighted, 1)

                def take_probs(n):
                    b = n % TB
                    e.wait_ge(p_turned, 8 * j + n + 1)
                    if n == TB:
                        e.wait_ge(pv_done, 2 * j + 1)
                    e.tensor_copy(pT(b).rearrange("p i t -> p (i t)"), mix[n % 2][:, 0:(b + 1) * P]).then_inc(
                        pT_ready, 1)

                scan_tile(2 * j)
                scan_tile(2 * j + 1)
                bias(0)
                e.wait_ge(v_turned, j + 1)
                e.tensor_copy(v_nat.rearrange("p i d -> p (i d)"), out_bank[:]).then_inc(v_ready, 1)
                score_bias(0)
                score_bias(1)
                weigh(0)
                weigh(1)
                for n in range(0, 2 * TB, 2):
                    take_probs(n)
                    if n + 2 == TB:
                        bias(1)
                    if n + 2 < 2 * TB:
                        score_bias(n + 2)
                    take_probs(n + 1)
                    if n + 2 < 2 * TB:
                        score_bias(n + 3)
                        weigh(n + 2)
                        weigh(n + 3)
                e.wait_ge(ohi_ready, j + 1)
                e.tensor_tensor(flat(h_lo[:, bass.ds(j, 1), :]), out_bank[:],
                                as32(flat(h_hi[:, bass.ds(7 + j, 1), :])), ALU.subtract).then_inc(o_taken, 1)
            step.at = start + HEAD_PAIRS * HEADS1_STEPS
            for m in range(2):
                e.wait_ge(y_done, TB * (m + 1))
                e.scalar_tensor_tensor(ssm_y[:, m, :], us[:, m, :], col("d_skip", m), mix[m][:], ALU.mult,
                                       ALU.add).then_inc(y_ready, 1)
            for m in range(2):
                e.wait_ge(glu_ready, m + 1)
                e.tensor_tensor(ssm_y[:, m, :], gelu_y[:, m, :], glu_s[:, m, :], ALU.mult).then_inc(yy_ready, 1)
            for m in range(2):
                e.wait_ge(yhi_ready, m + 1)
                e.tensor_tensor(h_lo[:, 4 + m, :], ssm_y[:, m, :], as32(h_hi[:, 5 + m, :]),
                                ALU.subtract).then_inc(y_split, 1)
            with e.Fori(0, DC // 2) as i:
                start = step.enter(i, MERGE_STEPS)
                for s in range(2):
                    p, c = MERGE1 + i, 2 * i + s
                    g_att = flat(gates[:, bass.ds(c, 1), :])
                    g_ssm = flat(gates[:, bass.ds(c + DC, 1), :])
                    e.wait_ge(sig_ready, c + 1)
                    e.wait_ge(unit_done, 2 * p + s + 1)
                    step(e.tensor_tensor(slot(24), score[s][:], g_ssm, ALU.mult))
                    e.tensor_tensor(slot(25), unit_bank[s][:], g_att, ALU.mult).then_inc(taken[s], 1)
                    e.wait_ge(taken[s], p + 2)
                    e.tensor_tensor(slot(22 + s), slot(24), slot(25), ALU.add).then_inc(merged_ready, 1)
                    e.wait_ge(mhi_ready, c + 1)
                    e.tensor_tensor(flat(u_lo[:, bass.ds(c, 1), :]), slot(22 + s),
                                    as32(flat(u_hi[:, bass.ds(c, 1), :])), ALU.subtract).then_inc(m_ready, 1)
            step.at = start + (DC // 2) * MERGE_STEPS

            def gated_update(p0, gate):
                with e.Fori(0, DC // 2) as i:
                    for s in range(2):
                        xc = flat(x[:, bass.ds(2 * i + s, 1), :])
                        e.wait_ge(unit_done, 2 * (p0 + i) + s + 1)
                        e.scalar_tensor_tensor(xc, unit_bank[s][:], mod[:, bass.ds(gate + 2 * i + s, 1)], xc,
                                               ALU.mult, ALU.add).then_inc(taken[s], 1)

            gated_update(OUT1, 16)

            modulate(1, 1, 24)
            step(e.memset(a_pad[:, 0:2], 0.0))
            e.sem_inc(prep_ready, 1)
            for half in range(2):
                p0 = FFN1 + half * FFN1_HALF
                with e.Fori(0, HALF1) as i:
                    start = step.enter(i, CONV_STEPS)
                    c = HALF1 * half + i
                    e.wait_ge(taken[0], p0 + i + 2)
                    settled()
                    step(e.tensor_scalar(ffn_u, a_pad[:, 2:T + 2], col("w_conv", c), col("b_conv", c),
                                         ALU.mult, ALU.add))
                    step(e.scalar_tensor_tensor(ffn_u, a_pad[:, 1:T + 1], col("w_conv", 16 + c), ffn_u,
                                                ALU.mult, ALU.add))
                    e.scalar_tensor_tensor(ffn_u, a_pad[:, 0:T], col("w_conv", 32 + c), ffn_u,
                                           ALU.mult, ALU.add).then_inc(conv_ready, 1)
                    e.wait_ge(silu_ready, c + 1)
                    e.wait_ge(unit_done, 2 * (p0 + i) + 2)
                    e.tensor_tensor(ffn_h, unit_bank[1][:], ffn_s, ALU.mult).then_inc(taken[1], 1)
                    e.wait_ge(hhi_ready, c + 1)
                    e.tensor_tensor(flat(h_lo[:, bass.ds(i, 1), :]), ffn_h, as32(flat(h_hi[:, bass.ds(i, 1), :])),
                                    ALU.subtract).then_inc(h_ready, 1)
                step.at = start + HALF1 * CONV_STEPS
                gated_update(p0 + HALF1, 40)
            invert(2)
            for c in range(DC):
                e.scalar_tensor_tensor(x[:, c, :], x[:, c, :], col("g_final", c), rstd[:], ALU.mult,
                                       ALU.mult).then_inc(x_ready, 1)

            with e.Fori(0, LAYERS) as l:
                step.enter(l, LAYER_STEPS)
                calls = step.calls

                def pre_norm(k):
                    for c in range(DC):
                        e.wait_ge(uhi_ready, DC * (2 + 3 * l + k) + c + 1)
                        e.scalar_tensor_tensor(u_lo[:, c, :], x[:, c, :], col("norm_g", (6 * l + 2 * k) * DC + c),
                                               as32(u_hi[:, c, :]), ALU.mult, ALU.subtract).then_inc(u_ready, 1)
                    invert(3 + 6 * l + 2 * k)
                    passed()

                def post_norm(k):
                    invert(4 + 6 * l + 2 * k)
                    for c in range(DC):
                        at = (6 * l + 2 * k + 1) * DC + c
                        g = col("norm_g", at) if k == 1 else half_g[:, bass.ds(at, 1)]
                        step(e.scalar_tensor_tensor(ux[:, c % 2, :], f[:, c, :], g, rstd[:], ALU.mult, ALU.mult))
                        e.tensor_tensor(x[:, c, :], x[:, c, :], ux[:, c % 2, :], ALU.add).then_inc(x_ready, 1)

                def f_out(p0, r, add, squares):
                    if squares:
                        e.memset(acc, 0.0).then_inc(fsq_added, 1)
                    with e.Fori(0, DC // 2) as i:
                        for s in range(2):
                            fc = flat(f[:, bass.ds(2 * i + s, 1), :])
                            e.wait_ge(unit_done, 2 * (p0 + i) + s + 1)
                            if add:
                                e.tensor_tensor(fc, unit_bank[s][:], fc, ALU.add).then_inc(taken[s], 1)
                            else:
                                settled()
                                e.tensor_copy(fc, unit_bank[s][:]).then_inc(taken[s], 1)
                            if squares:
                                e.wait_ge(fsq_ready, DC * r + 2 * i + s + 1)
                                e.wait_ge(fsq_added, (DC + 1) * r + 2 * i + s + 1)
                                e.tensor_tensor(acc, acc, sq[:, 0, :], ALU.add).then_inc(fsq_added, 1)

                for s_ffn in range(2):
                    k_norm = 2 * s_ffn
                    pre_norm(k_norm)
                    for half in range(2):
                        p0 = ffn2(l, s_ffn) + half * FFN2_HALF
                        h0 = 16 + 44 * l + 22 * s_ffn + HALF2 * half
                        with e.Fori(0, HALF2) as i:
                            p = p0 + i
                            e.wait_ge(unit_done, 2 * p + 1)
                            e.tensor_tensor(ffn_g, unit_bank[0][:], rstd[:], ALU.mult).then_inc(taken[0], 1)
                            e.wait_ge(unit_done, 2 * p + 2)
                            e.tensor_tensor(ffn_u, unit_bank[1][:], rstd[:], ALU.mult).then_inc(taken[1], 1)
                            e.wait_ge(silu_ready, h0 + i + 1)
                            e.wait_ge(taken[1], p + 2)
                            e.tensor_tensor(ffn_h, ffn_s, ffn_u, ALU.mult).then_inc(hidden_ready, 1)
                            e.wait_ge(hhi_ready, h0 + i + 1)
                            e.tensor_tensor(flat(h_lo[:, bass.ds(i, 1), :]), ffn_h,
                                            as32(flat(h_hi[:, bass.ds(i, 1), :])), ALU.subtract).then_inc(h_ready, 1)
                        f_out(p0 + HALF2, 3 * l + k_norm, half == 1, half == 1)
                    post_norm(k_norm)
                    if s_ffn:
                        continue
                    pm = layer(l) + MIX2
                    pre_norm(1)
                    for g in range(2):
                        rows = slice(64 * g, 64 * g + 64)
                        step(e.tensor_copy(pool_w[rows, :, rows], tabs[rows, bass.ds(
                            l * P + TABS["pool_w"][0], P)].rearrange("p (m n) -> p m n", m=2)))
                    passed()
                    with e.Fori(0, HEAD_PAIRS) as j:
                        J = HEAD_PAIRS * l + j
                        start = step.enter(j, HEADS2_STEPS)

                        def take(p, s, out):
                            e.wait_ge(unit_done, 2 * p + s + 1)
                            e.tensor_tensor(out, unit_bank[s][:], rstd[:], ALU.mult).then_inc(taken[s], 1)

                        def keep_logs(n):
                            h, i = n // TB, TB - 1 - n % TB
                            W = T - i * P
                            e.wait_ge(softp_ready, 8 * J + n + 1)
                            step(e.scalar_tensor_tensor(sp[:, h, i, 0:W], score[n % 2][:, 0:W], 0.0,
                                                        softp[:, n % 2, 0:W], ALU.max, ALU.add))
                            e.tensor_tensor(sp[:, h, i, 0:P], sp[:, h, i, 0:P], tab("strict"),
                                            ALU.mult).then_inc(sp_ready, 1)

                        pq = pm + 2 * j
                        e.wait_ge(unit_done, 2 * pq + 1)
                        e.scalar_tensor_tensor(nq_st, unit_bank[0][:], -ATT_SCALE, rstd[:], ALU.mult, ALU.mult)
                        e.scalar_tensor_tensor(q_st, unit_bank[0][:], ATT_SCALE, rstd[:], ALU.mult,
                                               ALU.mult).then_inc(taken[0], 1)
                        take(pq, 1, k_st)
                        take(pq + 1, 0, vT_st)
                        keep_logs(0)
                        keep_logs(1)
                        take(pq + 1, 1, flat(f[:, bass.ds(j, 1), :]))
                        e.wait_ge(v2_turned, J + 1)
                        e.tensor_copy(v_nat.rearrange("p i d -> p (i d)"), out_bank[:]).then_inc(v2_ready, 1)
                        for n in range(2, 2 * TB):
                            keep_logs(n)
                        e.wait_ge(ohi2_ready, J + 1)
                        e.tensor_tensor(flat(h_lo[:, bass.ds(j, 1), :]), out_bank[:],
                                        as32(flat(h_hi[:, bass.ds(j, 1), :])), ALU.subtract).then_inc(o2_taken, 1)
                    step.at = start + HEAD_PAIRS * HEADS2_STEPS

                    A, B = padded[:, 0, :], padded[:, 1, :]
                    Z = 16
                    lower, upper = slice(0, 64), slice(64, P)

                    def trailing(dst, src, lag, rows=slice(0, P)):
                        tt(dst[rows, Z:], src[rows, Z:], src[rows, Z - lag:T + Z - lag], ALU.add)

                    def pool(m):
                        step(e.tensor_copy(A[:, Z:], f[:, m, :]))
                        trailing(B, A, 1)
                        if m:
                            trailing(A, B, 2)
                            trailing(B, A, 4)
                        trailing(A, B, 8 if m else 2, upper)
                        head = col("inv_head", 16 * m, 16)
                        for rows, src in ((lower, B), (upper, A)):
                            step(e.tensor_scalar(cx[rows, m, :], src[rows, Z:], col("inv_w", m)[rows], None, ALU.mult))
                            tt(cx[rows, m, 0:16], src[rows, Z:Z + 16], head[rows], ALU.mult)
                        e.tensor_tensor(ux[:, m, :], cx[:, m, :], f[:, m, :], ALU.subtract).then_inc(pool_in, 1)

                    def take_extra(i):
                        p, s = pm + 2 * HEAD_PAIRS + i // 2, i % 2
                        e.wait_ge(unit_done, 2 * p + s + 1)
                        e.tensor_tensor(f[:, 4 + i, :], unit_bank[s][:], rstd[:], ALU.mult).then_inc(taken[s], 1)

                    step(e.memset(padded[:, :, 0:Z], 0.0))
                    pool(0)
                    take_extra(0)
                    pool(1)
                    take_extra(1)
                    take_extra(2)
                    take_extra(3)
                    for m in range(2):
                        tt(A[:, Z:], f[:, 2 + m, :], f[:, 4 + m, :], ALU.mult)
                        y = cx[:, m, :]

                        def tap(n):
                            return col("conv_w2", 6 * l + 2 * n + m)

                        step(e.tensor_scalar(y, A[:, Z - 2:T + Z - 2], tap(0), None, ALU.mult))
                        for n in (1, 2):
                            step(e.scalar_tensor_tensor(y, A[:, Z - 2 + n:T + Z - 2 + n], tap(n), y, ALU.mult, ALU.add))
                        e.tensor_tensor(cx[:, 2 + m, :], y, f[:, 6 + m, :], ALU.mult).then_inc(conv2_ready, 1)
                    for m in range(2):
                        e.wait_ge(phi_ready, 2 * l + m + 1)
                        e.scalar_tensor_tensor(h_lo[:, 6 + m, :], score[m][:], col("pool_scale", 2 * l + m),
                                               as32(h_hi[:, 6 + m, :]), ALU.mult, ALU.subtract).then_inc(cat_ready, 1)
                    for m in range(2):
                        e.wait_ge(chi_ready, 2 * l + m + 1)
                        e.tensor_tensor(h_lo[:, 4 + m, :], cx[:, 2 + m, :], as32(h_hi[:, 4 + m, :]),
                                        ALU.subtract).then_inc(cat_ready, 1)
                    f_out(pm + MIX2_IN, 3 * l + 1, False, True)
                    post_norm(1)
                assert step.calls - calls + (HEAD_PAIRS - 1) * HEADS2_STEPS == LAYER_STEPS, step.calls - calls


def _tiles(w):
    K, F = w.shape
    return w.reshape(K // P, P, F // P, P).transpose(2, 1, 0, 3).reshape(F // P, P, K)


def _cols(v):
    return v.reshape(-1, P).T


def _layout(a):
    import numpy as np

    lead = {k: v[0] for k, v in a.items() if not k.endswith("_2") and k != "g_final"}
    out = {"x": lead["x"].T.reshape(DC, P, T).transpose(1, 0, 2)}
    t_s = np.arange(P)[:, None] + (T - P) - np.arange(T)[None, :]
    seen = t_s >= 0
    count = (seen * ((t_s <= P) * 1 + (t_s % 4 == 0) + (t_s % 16 == 0))).astype(np.float32)
    dist = np.where(count > 0, t_s, 1e35).astype(np.float32)
    row, colm = np.arange(P)[:, None], np.arange(P)[None, :]
    eye = (row == colm).astype(np.float32)
    windows = np.repeat(np.array([[2, 8], [4, 16]], np.float32), 64, axis=0)
    inv_head = 1.0 / np.minimum(np.arange(1, 17, dtype=np.float32)[None, None, :], windows[:, :, None])
    slopes = np.array([2.0 ** (-8.0 * (h + 1) / HEADS) for h in range(HEADS)], np.float32)

    def state(v):
        return v.reshape(SSM_TILES, P).T

    def state_ch(v):
        return v.reshape(SSM_TILES, P, SSM_CH).transpose(1, 0, 2).reshape(P, -1)

    parts = {
        "c": _cols(lead["c"]), "b_ada": _cols(lead["b_ada"]), "g_mix": _cols(lead["g_mix"]),
        "g_ffn": _cols(lead["g_ffn"]), "g_final": _cols(a["g_final"]), "norm_g": _cols(a["norm_g_2"]),
        "b_gate": _cols(lead["b_gate"]), "d_skip": _cols(lead["d_skip"]), "b_glu": _cols(lead["b_glu"]),
        "w_conv": _cols(lead["w_conv"]), "b_conv": _cols(lead["b_conv"]), "conv_w2": _cols(a["conv_w_2"]),
        "pool_scale": _cols(a["pool_scale_2"]), "slopes": np.broadcast_to(slopes, (P, HEADS)),
        "a_re": state(lead["a_re"]), "a_im": state(lead["a_im"]), "log_dt": state(np.repeat(lead["log_dt"], 64)),
        "inv_head": inv_head.reshape(P, 32).astype(np.float32), "inv_w": (1.0 / windows).astype(np.float32),
        "b_re": state_ch(lead["b_re"]), "b_im": state_ch(lead["b_im"]),
        "c_re": state_ch(lead["c_re"].transpose(0, 2, 1)), "c_im": state_ch(lead["c_im"].transpose(0, 2, 1)),
    }
    out["cols"] = np.concatenate([parts[n] for n in COLS], axis=1)
    tabs = {
        "ident": eye, "tri": (row >= colm).astype(np.float32), "ones": np.ones((P, P), np.float32),
        "strict": (colm > row).astype(np.float32), "dist": dist, "count": count,
        "w_glu": lead["w_glu"].reshape(2, P, 256).transpose(1, 0, 2).reshape(P, 512),
        "pool_w": a["pool_w_2"].reshape(2, 2, P, 64).transpose(2, 0, 1, 3).reshape(P, 256),
    }
    out["tabs"] = np.concatenate([tabs[n] for n in TABS], axis=1)
    out["w_ada"] = lead["w_ada"].reshape(DC, P, 3, 2 * D).transpose(2, 0, 1, 3).reshape(3 * DC, P, 2 * D)

    w_in = _tiles(lead["w_in"])
    q0, k0, v0, us0, g0 = 0, 4, 8, 12, 14
    order = [us0, us0 + 1]
    for j in range(HEAD_PAIRS):
        order += [q0 + j, k0 + j, v0 + j, g0 + 3 * j, g0 + 3 * j + 1, g0 + 3 * j + 2]
    order += [g0 + n for n in range(12, 16)]
    out["w_in"] = w_in[order]
    out["w_merge"] = np.concatenate([_tiles(lead["w_proj_ssm"]), _tiles(lead["w_proj_att"])], axis=2)
    out["w_out"] = _tiles(lead["w_out"])
    up = _tiles(lead["w_up"]).reshape(2, 16, P, D)
    out["w_up"] = up.transpose(1, 0, 2, 3).reshape(32, P, D)
    out["w_down"] = np.concatenate([_tiles(w) for w in lead["w_down"].reshape(2, D, D)])

    gu, dn, in2, out2 = [], [], [], []
    for l in range(LAYERS):
        for s in range(2):
            pair = np.stack([_tiles(a["ffn_w_gate_2"][l, s]), _tiles(a["ffn_w_up_2"][l, s])], axis=1)
            gu.append(pair.reshape(4 * HALF2, P, D))
            dn += [_tiles(w) for w in a["ffn_w_down_2"][l, s].reshape(2, RING, D)]
        w = _tiles(a["w_in_2"][l])
        q0, k0, v0, gb, gc, ch, pl = 0, 4, 8, 12, 14, 16, 18
        extra = [pl, pl + 1, ch, ch + 1, gc, gc + 1, gb, gb + 1]
        order = []
        for j in range(HEAD_PAIRS):
            order += [q0 + j, k0 + j, v0 + j, extra[j]]
        in2.append(w[order + extra[4:]])
        out2.append(_tiles(a["w_out_2"][l]))
    out["w_gate_up"], out["w_down2"] = np.concatenate(gu), np.concatenate(dn)
    out["w_in2"], out["w_out2"] = np.concatenate(in2), np.concatenate(out2)
    return {k: np.ascontiguousarray(v) for k, v in out.items()}


def kernel(**inputs):
    import numpy as np
    import concourse.bacc as bacc
    from concourse.bass_utils import run_bass_kernel_spmd

    arrays = _layout({k: np.asarray(v) for k, v in inputs.items()})
    nc = bacc.Bacc("TRN2", target_bir_lowering=False, num_devices=1, dynamic_dma_scratch_size=256)
    d = {k: nc.dram_tensor(f"in_{k}", v.shape, F32, kind="ExternalInput").ap() for k, v in arrays.items()}
    d["out"] = nc.dram_tensor("out", (DC, P, T), F32, kind="ExternalOutput").ap()
    program(nc, d)
    r = run_bass_kernel_spmd(nc, [{f"in_{k}": v for k, v in arrays.items()}], core_ids=[0])
    return np.ascontiguousarray(r.results[0]["out"].reshape(D, T).T)[None]
```

```python
from contextlib import ExitStack

import concourse.bass as bass
from concourse import mybir

F32 = mybir.dt.float32
F32R = mybir.dt.float32r
BF16 = mybir.dt.bfloat16
ALU = mybir.AluOpType
ACT = mybir.ActivationFunctionType

P = 128
T = 512
D = 1024
DC = D // P
EPS = 1e-6
HEADS, HD = 8, 64
HEAD_PAIRS = HEADS // 2
TB = T // P
ATT_SCALE = HD ** -0.5
LAYERS = 2
SSM_TILES = 8
SSM_CH = 16
HALF1 = 8
HALF2 = 11
RING = HALF2 * P

IN1, MERGE1, OUT1 = 0, 15, 19
FFN1 = 23
FFN1_HALF = HALF1 + DC // 2
LAYER0 = FFN1 + 2 * FFN1_HALF
FFN2_HALF = HALF2 + DC // 2
MIX2 = 2 * FFN2_HALF
MIX2_IN = 10
PAIRS_PER_LAYER = 2 * MIX2 + MIX2_IN + DC // 2

COLS = {}
_at = 0
for _name, _n in (("c", 8), ("b_ada", 48), ("g_mix", 8), ("g_ffn", 8), ("g_final", 8), ("norm_g", 96),
                  ("b_gate", 16), ("d_skip", 2), ("b_glu", 2), ("w_conv", 48), ("b_conv", 16),
                  ("conv_w2", 12), ("pool_scale", 4), ("slopes", 8), ("a_re", 8), ("a_im", 8), ("log_dt", 8),
                  ("inv_head", 32), ("inv_w", 2),
                  ("b_re", 128), ("b_im", 128), ("c_re", 128), ("c_im", 128)):
    COLS[_name] = (_at, _n)
    _at += _n
N_COLS = _at
TABS = {}
_at = 0
for _name, _n in (("ident", 128), ("after", 128), ("ones", 128), ("strict", 128), ("dist", 512), ("count", 512),
                  ("w_glu", 512), ("pool_w", 256)):
    TABS[_name] = (_at, _n)
    _at += _n
N_TABS = _at
HEADS1_STEPS, CONV_STEPS, HEADS2_STEPS = 2 * 19 + 2 + 8, 2, 10
LAYER_STEPS = 3 + 3 * 9 + 2 + HEAD_PAIRS * HEADS2_STEPS + 1 + 7 + 9 + 8

TWO_PI_1, TWO_PI_2, TWO_PI_3 = 6.28125, 0.0019350051879882812, 3.0199159819567e-07
INV_TWO_PI = 0.15915494309189535
ROUND_MAGIC = 12582912.0
PI_SAFE, HALF_PI = 3.1415925, 1.5707963267948966


class Steps:

    def __init__(self, eng, sem):
        self.eng, self.sem, self.at, self.calls = eng, sem, 0, 0

    def __call__(self, ins):
        ins.then_inc(self.sem, 1)
        self.at = self.at + 1
        self.calls += 1
        self.eng.wait_ge(self.sem, self.at)

    def enter(self, i, per_turn):
        start = self.at
        self.at = i * per_turn + start
        return start


def program(nc, d):
    ctx = ExitStack()
    with ctx:
        def sb(name, shape, dt=F32):
            return ctx.enter_context(nc.sbuf_tensor(name, shape, dt))

        def sem(name):
            return ctx.enter_context(nc.semaphore(name))

        cols = sb("cols", [P, N_COLS])
        tabs = sb("tabs", [P, N_TABS])
        x = sb("x", [P, DC, T])
        u_hi = sb("u_hi", [P, DC, T], F32R)
        u_lo = sb("u_lo", [P, DC, T], F32R)
        h_at = nc.sbuf_base
        h_hi = sb("h_hi", [P, HALF2, T], F32R)
        h_lo = sb("h_lo", [P, HALF2 + 1, T], F32R)
        f = sb("f", [P, DC, T])
        raw = sb("raw", [P, 2, RING])
        w_hi = sb("w_hi", [P, 2, RING], F32R)
        w_lo = sb("w_lo", [P, 2, RING], F32R)
        arena = sb("arena", [P, 26 * T])
        rstd = sb("rstd", [P, T])
        mod = sb("mod", [P, 48])
        amp = sb("amp", [P, 16])
        c_act = sb("c_act", [P, 8])
        half_g = sb("half_g", [P, 96])
        eps = sb("eps", [P, 1])
        mask_b = sb("mask_b", [P, P], BF16)
        stat = sb("stat", [P, 32])
        us = sb("us", [P, 2, T])
        B_t = sb("B_t", [P, 4, P])
        C_t = sb("C_t", [P, 2, SSM_TILES, 32])
        co = sb("co", [P, 26, 8])
        E1 = sb("E1", [P, 2, SSM_TILES, 16])
        E16 = sb("E16", [P, 2, SSM_TILES, 32])
        pool_w = sb("pool_w", [P, 2, P])

        def slot(n, k=1):
            return arena[:, n * T:(n + k) * T]

        def slots(n, k):
            return slot(n, k).rearrange("p (c t) -> p c t", t=T)

        gates = slots(0, 16)
        sq, acc, std, ux = slots(0, 2), slot(2), slot(3), slots(4, 2)
        ffn_g, ffn_s, ffn_u, ffn_h = slot(6), slot(7), slot(8), slot(9)
        a_pad = arena[:, 10 * T:10 * T + T + 2]
        q_st, k_st, vT_st = slot(16), slot(17), slot(18)
        v_nat = slots(19, 1)[:, 0, :].rearrange("p (i d) -> p i d", d=P)
        nsc, bias_h = slots(20, 2), slot(25)
        pt_all = arena[:, 22 * T:24 * T + 2 * P]
        kept, own = slots(0, 4), slots(4, 4)
        pooled = slots(23, 2)
        a_keys, softp = slots(8, 4), slots(12, 4)
        padded = arena[:, 20 * T:20 * T + 2 * (T + 16)].rearrange("p (a t) -> p a t", a=2)
        cx = slots(6, 4)
        gelu_y, glu_s, ssm_y = slots(16, 2), slots(18, 2), slots(20, 2)
        ssm_tmp = nc.alloc_sbuf_tensor_at("ssm_tmp", [P, 7, T], F32, offset=h_at)
        bu_im = nc.alloc_sbuf_tensor_at("bu_im", [P, SSM_TILES, T], F32, offset=h_at + 15 * T * 4)
        ada_acc = nc.alloc_sbuf_tensor_at("ada_acc", [P, 2 * D], F32, offset=h_at)
        ada_w = nc.alloc_sbuf_tensor_at("ada_w", [P, 2, 2 * D], F32, offset=h_at + 2 * D * 4)
        bu_re = f
        ada_rows = f.rearrange("p (n c) t -> p n (c t)", c=2)
        ada_sums = nc.alloc_sbuf_tensor_at("ada_sums", [P, 3 * D], F32, offset=h_at + (HALF2 + 6) * T * 4)
        gate_sum = slot(20, 2)
        banks = [ctx.enter_context(nc.psum_tensor(n, [P, T], F32)) for n in
                 ("unit_bank0", "unit_bank1", "stat_bank", "score0", "score1", "mix0", "mix1", "out_bank")]
        unit_bank, stat_bank, score, mix, out_bank = banks[0:2], banks[2], banks[3:5], banks[5:7], banks[7]
        z_bank = banks[3:7]

        consts_loaded = sem("consts_loaded")
        x_loaded = sem("x_loaded")
        ada_loaded = [sem(f"ada_loaded{i}") for i in range(2)]
        ada_rows_loaded = [sem(f"ada_rows_loaded{i}") for i in range(4)]
        raw_loaded = [sem(f"raw_loaded{i}") for i in range(2)]
        hi_ready = sem("hi_ready")
        lo_ready = sem("lo_ready")
        unit_done = sem("unit_done")
        taken = [sem(f"taken{i}") for i in range(2)]
        cact_ready = sem("cact_ready")
        ada_used = sem("ada_used")
        mod_sum = sem("mod_sum")
        mod_ready = sem("mod_ready")
        prep_ready = sem("prep_ready")
        sq_ready = sem("sq_ready")
        sq_used = sem("sq_used")
        fsq_ready = sem("fsq_ready")
        fsq_added = sem("fsq_added")
        fsum_ready = sem("fsum_ready")
        std_ready = sem("std_ready")
        ux_ready = sem("ux_ready")
        uhi_ready = sem("uhi_ready")
        u_ready = sem("u_ready")
        x_ready = sem("x_ready")
        conv_ready = sem("conv_ready")
        silu_ready = sem("silu_ready")
        hidden_ready = sem("hidden_ready")
        hhi_ready = sem("hhi_ready")
        h_ready = sem("h_ready")
        ssm_act, ssm_vec = sem("ssm_act"), sem("ssm_vec")
        B_padded, B_turned, B_ready = sem("B_padded"), sem("B_turned"), sem("B_ready")
        bu_done, bu_ready = sem("bu_done"), sem("bu_ready")
        scan_ready = sem("scan_ready")
        y_done, y_ready, gelu_ready, glu_done, glu_ready, yy_ready, yhi_ready, y_split = (
            sem(n) for n in ("y_done", "y_ready", "gelu_ready", "glu_done", "glu_ready", "yy_ready",
                             "yhi_ready", "y_split"))
        v_turned, v_ready = sem("v_turned"), sem("v_ready")
        s_done, s_biased, p_ready, p_weighted, p_scaled, p_turned, pT_ready, pv_done = (
            sem(n) for n in ("s_done", "s_biased", "p_ready", "p_weighted", "p_scaled", "p_turned",
                             "pT_ready", "pv_done"))
        ohi_ready, o_taken = sem("ohi_ready"), sem("o_taken")
        sig_ready, ym_done, merged_ready, mhi_ready, m_ready = (
            sem(n) for n in ("sig_ready", "ym_done", "merged_ready", "mhi_ready", "m_ready"))
        v2_turned, v2_ready = sem("v2_turned"), sem("v2_ready")
        sums_taken = sem("sums_taken")
        z_done, softp_ready, sp_ready, R_done, a_ready, pv2_done, ohi2_ready, o2_taken = (
            sem(n) for n in ("z_done", "softp_ready", "sp_ready", "R_done", "a_ready", "pv2_done",
                             "ohi2_ready", "o2_taken"))
        pool_in, pool_done, phi_ready, conv2_ready, chi_ready, cat_ready = (
            sem(n) for n in ("pool_in", "pool_done", "phi_ready", "conv2_ready", "chi_ready", "cat_ready"))
        vec_step, act_step = sem("vec_step"), sem("act_step")
        vec_passed = sem("vec_passed")
        out_stored = sem("out_stored")

        def col(name, i=0, n=1):
            return cols[:, bass.ds(COLS[name][0] + i, n)]

        def tab(name, a=0, b=None):
            at, n = TABS[name]
            return tabs[:, at + a:at + (n if b is None else b)]

        def as32(ap):
            return ap.bitcast(F32)

        def in_pair(j, n):
            return IN1 + 1 + 3 * j + n

        def layer(l):
            return LAYER0 + PAIRS_PER_LAYER * l

        def ffn2(l, s):
            return layer(l) + s * (MIX2 + MIX2_IN + DC // 2)

        def pT(b):
            return pt_all[:, P * b * (b + 1) // 2:P * (b + 1) * (b + 2) // 2].rearrange("p (i t) -> p i t", t=P)

        CONSTS = 32
        LAST_PAIR = LAYER0 + LAYERS * PAIRS_PER_LAYER
        block = ctx.enter_context(nc.Block())

        @block.sync
        def _(sp_eng):
            e = sp_eng
            e.dma_start(cols[:], d["cols"]).then_inc(consts_loaded, 16)
            e.dma_start(tabs[:], d["tabs"]).then_inc(consts_loaded, 16)

            def load(p, s, src, n):
                if not isinstance(p, int) or p > 0:
                    e.wait_ge(lo_ready, 2 * p + s - 1)
                e.dma_start(raw[:, s, 0:n], src).then_inc(raw_loaded[s], 16)

            def load_pairs(p0, w, first, pairs):
                n = w.shape[2]
                with e.Fori(0, pairs) as i:
                    for s in range(2):
                        load(p0 + i, s, w[bass.ds(first + 2 * i + s, 1), :, :].rearrange("a p n -> p (a n)"), n)

            for k in range(DC):
                if k >= 2:
                    e.wait_ge(ada_used, k - 1)
                e.dma_start(ada_w[:, k % 2, :], d["w_ada"][k]).then_inc(ada_loaded[k % 2], 16)
                if k == 1:
                    e.dma_start(x[:], d["x"]).then_inc(x_loaded, 16)
                if k == 3:
                    for s in range(2):
                        load(0, s, d["w_in"][s], D)
            load_pairs(1, d["w_in"], 2, MERGE1 - 1)

            def load_rows(a):
                if a >= 4:
                    e.wait_ge(ada_used, DC + a - 3)
                else:
                    e.wait_ge(y_done, SSM_TILES)
                e.dma_start(ada_rows[:, a % 4, :], d["w_ada_rows"][a]).then_inc(ada_rows_loaded[a % 4], 16)

            rows = [[u] for u in range(DC)] + [[DC + 3 * u + m for m in range(3)] for u in range(DC)]
            for u in range(2 * DC):
                w, p = (d["w_merge"], MERGE1) if u < DC else (d["w_out"], OUT1)
                load(p + u % DC // 2, u % 2, w[u % DC], w.shape[2])
                if u >= 2:
                    for a in rows[u - 2]:
                        load_rows(a)
            for a in rows[-2] + rows[-1]:
                load_rows(a)
            for half in range(2):
                load_pairs(FFN1 + half * FFN1_HALF, d["w_up"], 2 * HALF1 * half, HALF1)
                load_pairs(FFN1 + half * FFN1_HALF + HALF1, d["w_down"], DC * half, DC // 2)
            with e.Fori(0, LAYERS) as l:
                for s in range(2):
                    for half in range(2):
                        n = 2 * (2 * l + s) + half
                        load_pairs(ffn2(l, s) + half * FFN2_HALF, d["w_gate_up"], 2 * HALF2 * n, HALF2)
                        load_pairs(ffn2(l, s) + half * FFN2_HALF + HALF2, d["w_down2"], DC * n, DC // 2)
                    if s == 0:
                        load_pairs(layer(l) + MIX2, d["w_in2"], 2 * MIX2_IN * l, MIX2_IN)
                        load_pairs(layer(l) + MIX2 + MIX2_IN, d["w_out2"], DC * l, DC // 2)
            for c in range(DC):
                e.wait_ge(x_ready, DC * 3 * LAYERS + c + 1)
                e.dma_start(d["out"][c], x[:, c, :]).then_inc(out_stored, 16)
            e.wait_ge(out_stored, 16 * DC)

        @block.gpsimd
        def _(e):
            def split_pairs(p0, pairs, n):
                with e.Fori(0, pairs) as i:
                    for s in range(2):
                        e.wait_ge(hi_ready, 2 * (p0 + i) + s + 1)
                        e.tensor_tensor(w_lo[:, s, 0:n], raw[:, s, 0:n], as32(w_hi[:, s, 0:n]),
                                        ALU.subtract).then_inc(lo_ready, 1)

            split_pairs(IN1, MERGE1 - IN1, D)
            split_pairs(MERGE1, DC // 2, 6 * P)
            split_pairs(OUT1, LAYER0 - OUT1, D)
            with e.Fori(0, LAYERS) as l:
                for s in range(2):
                    for half in range(2):
                        split_pairs(ffn2(l, s) + half * FFN2_HALF, HALF2, D)
                        split_pairs(ffn2(l, s) + half * FFN2_HALF + HALF2, DC // 2, RING)
                    if s == 0:
                        split_pairs(layer(l) + MIX2, MIX2_IN + DC // 2, D)

        @block.tensor
        def _(e):
            def unit(p, s, hi, lo, ks, bank=None, first=0, before=None, signal=True):
                bank = unit_bank[s] if bank is None else bank
                if signal is True or signal == "first":
                    e.wait_ge(lo_ready, 2 * p + s + 1)
                    e.wait_ge(taken[s], p + 1)
                for n, k in enumerate(ks):
                    if before:
                        before(n)
                    wh = w_hi[:, s, (first + n) * P:(first + n + 1) * P]
                    wl = w_lo[:, s, (first + n) * P:(first + n + 1) * P]
                    last = n == len(ks) - 1
                    e.matmul(bank[:], wh, hi(k), start=n == 0, stop=False)
                    e.matmul(bank[:], wh, lo(k), start=False, stop=False)
                    mm = e.matmul(bank[:], wl, hi(k), start=False, stop=last)
                if signal is True or signal == "last":
                    mm.then_inc(unit_done, 1)

            def from_u(k):
                return u_hi[:, k, :]

            def from_u_lo(k):
                return u_lo[:, k, :]

            def from_h(k):
                return h_hi[:, k, :]

            def from_h_lo(k):
                return h_lo[:, k, :]

            EIGHT = range(DC)

            def in_unit(p, s):
                unit(p, s, from_u, from_u_lo, EIGHT)

            def add_square(q, c):
                e.wait_ge(sq_ready, DC * q + c + 1)
                e.matmul(stat_bank[:], tab("ones"), sq[:, c % 2, :], start=c == 0,
                         stop=c == DC - 1).then_inc(sq_used, 1)

            def u_chunk(n, q=None):
                def wait(c):
                    if q is not None:
                        add_square(q, c)
                    e.wait_ge(u_ready, DC * n + c + 1)
                return wait

            def h_chunk(h0):
                return lambda c: e.wait_ge(h_ready, h0 + c + 1)

            def down(p0, h0, n_k):
                with e.Fori(0, DC // 2) as i:
                    unit(p0 + i, 0, from_h, from_h_lo, range(n_k), before=h_chunk(h0))
                    unit(p0 + i, 1, from_h, from_h_lo, range(n_k))

            def f_sum(r):
                e.wait_ge(fsq_added, (DC + 1) * (r + 1))
                e.matmul(stat_bank[:], tab("ones"), acc, start=True, stop=True).then_inc(fsum_ready, 1)

            def turn_v(free, free_at, src_sem, src_at, done):
                e.wait_ge(free, free_at)
                e.wait_ge(src_sem, src_at)
                for i in range(TB):
                    mm = e.transpose(out_bank[:, i * P:(i + 1) * P], vT_st[:, i * P:(i + 1) * P], tab("ident"))
                mm.then_inc(done, 1)

            def mixer2(l):
                pm = layer(l) + MIX2

                def head_pair(j):
                    J = HEAD_PAIRS * l + j

                    def z(h):
                        if h == 0:
                            for s in range(2):
                                e.wait_ge(taken[s], pm + 2 * j + 2)
                        rows = slice(HD * h, HD * h + HD)
                        for n in range(TB):
                            i = TB - 1 - n
                            e.wait_ge(sums_taken, 8 * J + TB * h + n + 1)
                            e.matmul(z_bank[i][:, 0:T - i * P], k_st[rows, i * P:(i + 1) * P], q_st[rows, i * P:T],
                                     start=True, stop=True).then_inc(z_done, 1)

                    def keep_sums(h):
                        for n in range(TB):
                            i = TB - 1 - n
                            e.wait_ge(sp_ready, 8 * J + TB * h + n + 1)
                            R = z_bank[i]
                            mm = e.matmul(R[:, 0:T - i * P], tab("after"), kept[:, i, 0:T - i * P], start=True,
                                          stop=n == 0)
                            for m in range(i + 1, TB):
                                mm = e.matmul(R[:, (m - i) * P:T - i * P], tab("ones"), kept[:, m, 0:T - m * P],
                                              start=False, stop=m == TB - 1)
                            mm.then_inc(R_done, 1)

                    def values(h):
                        if h == 0:
                            e.wait_ge(v2_ready, J + 1)
                        e.wait_ge(a_ready, 8 * J + TB * (h + 1))
                        rows = slice(HD * h, HD * h + HD)
                        for i in range(TB):
                            mm = e.matmul(out_bank[rows, i * P:T], v_nat[:, i, rows], a_keys[:, i, 0:T - i * P],
                                          start=i == 0, stop=i == TB - 1)
                        mm.then_inc(pv2_done, 1)

                    z(0)
                    in_unit(pm + 2 * j + 1, 0)
                    keep_sums(0)
                    in_unit(pm + 2 * j + 1, 1)
                    turn_v(o2_taken, J + 1, taken[0], pm + 2 * j + 3, v2_turned)
                    z(1)
                    values(0)
                    in_unit(pm + 2 * j + 2, 0)
                    keep_sums(1)
                    in_unit(pm + 2 * j + 2, 1)
                    values(1)

                unit(pm, 0, from_u, from_u_lo, EIGHT, before=u_chunk(3 + 3 * l, 4 + 3 * l))
                in_unit(pm, 1)
                with e.Fori(0, HEAD_PAIRS) as j:
                    head_pair(j)
                for s in range(2):
                    in_unit(pm + 2 * HEAD_PAIRS + 1, s)
                for m in range(2):
                    e.wait_ge(pool_in, 2 * l + m + 1)
                    e.matmul(score[m][:], pool_w[:, m, :], pooled[:, m, :], start=True, stop=True).then_inc(pool_done, 1)
                def cat_chunk(c):
                    if c < HEAD_PAIRS:
                        e.wait_ge(o2_taken, HEAD_PAIRS * l + c + 2)
                    else:
                        e.wait_ge(cat_ready, 4 * l + (3, 4, 1, 2)[c - HEAD_PAIRS])

                with e.Fori(0, DC // 2) as i:
                    unit(pm + MIX2_IN + i, 0, from_h, from_h_lo, EIGHT,
                         before=cat_chunk)
                    unit(pm + MIX2_IN + i, 1, from_h, from_h_lo, EIGHT)
                f_sum(3 * l + 1)

            e.wait_ge(consts_loaded, CONSTS)
            for c in EIGHT:
                add_square(0, c)
            e.wait_ge(ada_used, DC)
            for c in range(16):
                mm = e.matmul(out_bank[:, c:c + 1], ada_acc[:, c * P:(c + 1) * P], tab("ones", 0, 1),
                              start=True, stop=True)
            mm.then_inc(mod_sum, 1)

            def sum_rows(n, src, at):
                e.wait_ge(ada_used, at)
                for c in range(DC):
                    mm = e.matmul(out_bank[:, DC * n + c:DC * n + c + 1], src[:, c * P:(c + 1) * P],
                                  tab("ones", 0, 1), start=True, stop=True)
                mm.then_inc(mod_sum, 1)

            unit(IN1, 0, from_u, from_u_lo, EIGHT, before=u_chunk(0))
            in_unit(IN1, 1)
            e.wait_ge(B_padded, 1)
            for n in range(4):
                mm = e.transpose(out_bank[:, n * P:(n + 1) * P], slot(22, 1)[:, n * P:(n + 1) * P], tab("ident"))
            mm.then_inc(B_turned, 1)
            e.wait_ge(B_ready, 1)
            for s in range(2):
                e.wait_ge(taken[s], 2)
            for i in range(SSM_TILES):
                rows = slice(32 * (i % 4), 32 * (i % 4) + 32)
                for part in range(2):
                    n = 2 * i + part
                    if n >= 2:
                        e.wait_ge(bu_ready, n - 1)
                    e.matmul(score[part][:], B_t[rows, 2 * part + i // 4, :], us[rows, i // 4, :],
                             start=True, stop=True).then_inc(bu_done, 1)

            with e.Fori(0, HEAD_PAIRS) as j:
                def scores(n):
                    h, b = divmod(n, TB)
                    if n == 0:
                        for s in range(2):
                            e.wait_ge(taken[s], in_pair(j, 0) + 2)
                    if n >= 2:
                        e.wait_ge(s_biased, 8 * j + n - 1)
                    rows = slice(HD * h, HD * h + HD)
                    e.matmul(score[n % 2][:, 0:(b + 1) * P], q_st[rows, b * P:(b + 1) * P],
                             k_st[rows, 0:(b + 1) * P], start=True, stop=True).then_inc(s_done, 1)

                def turn_probs(n):
                    e.wait_ge(p_scaled, 8 * j + n + 1)
                    if n >= 2:
                        e.wait_ge(pT_ready, 8 * j + n - 1)
                    for i in range(n % TB + 1):
                        mm = e.transpose(mix[n % 2][:, i * P:(i + 1) * P], nsc[:, n % 2, i * P:(i + 1) * P],
                                         tab("ident"))
                    mm.then_inc(p_turned, 1)

                def values(h):
                    e.wait_ge(v_ready, j + 1)
                    e.wait_ge(pT_ready, 8 * j + TB * (h + 1))
                    rows = slice(HD * h, HD * h + HD)
                    for b in range(TB):
                        for i in range(b + 1):
                            mm = e.matmul(out_bank[rows, b * P:(b + 1) * P], v_nat[:, i, rows], pT(b)[:, i, :],
                                          start=i == 0, stop=i == b)
                    mm.then_inc(pv_done, 1)

                in_unit(in_pair(j, 0), 0)
                in_unit(in_pair(j, 0), 1)
                in_unit(in_pair(j, 1), 0)
                in_unit(in_pair(j, 1), 1)
                turn_v(o_taken, j + 1, taken[0], in_pair(j, 1) + 2, v_turned)
                scores(0)
                scores(1)
                in_unit(in_pair(j, 2), 0)
                turn_probs(0)
                scores(2)
                turn_probs(1)
                scores(3)
                in_unit(in_pair(j, 2), 1)
                for n in range(2, TB):
                    turn_probs(n)
                    scores(n + 2)
                values(0)
                for n in range(TB, 2 * TB):
                    turn_probs(n)
                    if n + 2 < 2 * TB:
                        scores(n + 2)
                values(1)
            with e.Fori(0, 2) as i:
                for s in range(2):
                    in_unit(in_pair(HEAD_PAIRS, 0) + i, s)
            e.wait_ge(scan_ready, SSM_TILES)
            for i in range(SSM_TILES):
                rows = slice(32 * (i % 4), 32 * (i % 4) + 32)
                e.matmul(mix[i // 4][rows, :], C_t[:, 0, i, :], bu_re[:, i, :], start=True, stop=False)
                e.matmul(mix[i // 4][rows, :], C_t[:, 1, i, :], bu_im[:, i, :], start=False,
                         stop=True).then_inc(y_done, 1)
            e.wait_ge(gelu_ready, 2)
            for m in range(2):
                for k in range(2):
                    mm = e.matmul(score[m][:], tab("w_glu", 256 * k + P * m, 256 * k + P * m + P),
                                  gelu_y[:, k, :], start=k == 0, stop=k == 1)
                mm.then_inc(glu_done, 1)
            e.wait_ge(y_split, 2)
            e.wait_ge(o_taken, HEAD_PAIRS + 1)
            with e.Fori(0, DC // 2) as i:
                for s in range(2):
                    p = MERGE1 + i
                    unit(p, s, lambda k: h_hi[:, 5 + k, :], lambda k: h_lo[:, 4 + k, :], range(2),
                         bank=score[s], signal="first")
                    unit(p, s, lambda k: h_hi[:, 7 + k, :], lambda k: h_lo[:, k, :], range(4), first=2,
                         signal="last")
            sum_rows(0, gate_sum, 2 * DC)
            with e.Fori(0, DC // 2) as i:
                unit(OUT1 + i, 0, from_u, from_u_lo, EIGHT, before=lambda c: e.wait_ge(m_ready, c + 1))
                unit(OUT1 + i, 1, from_u, from_u_lo, EIGHT)

            for n in range(1, 4):
                sum_rows(n, ada_sums[:, (n - 1) * D:n * D], 5 * DC)
            for c in EIGHT:
                add_square(1, c)
            for half in range(2):
                p0 = FFN1 + half * FFN1_HALF
                with e.Fori(0, HALF1) as i:
                    unit(p0 + i, 0, from_u, from_u_lo, EIGHT, before=u_chunk(1))
                    in_unit(p0 + i, 1)
                down(p0 + HALF1, HALF1 * half, HALF1)
            for c in EIGHT:
                add_square(2, c)

            with e.Fori(0, LAYERS) as l:
                for s_ffn in range(2):
                    k_norm = 2 * s_ffn
                    for half in range(2):
                        p0 = ffn2(l, s_ffn) + half * FFN2_HALF
                        if half == 0:
                            unit(p0, 0, from_u, from_u_lo, EIGHT,
                                 before=u_chunk(2 + 3 * l + k_norm, 3 + 3 * l + k_norm))
                            in_unit(p0, 1)
                        with e.Fori(1 - half, HALF2) as i:
                            in_unit(p0 + i, 0)
                            in_unit(p0 + i, 1)
                        down(p0 + HALF2, 16 + 44 * l + 22 * s_ffn + HALF2 * half, HALF2)
                    f_sum(3 * l + k_norm)
                    if s_ffn == 0:
                        mixer2(l)


        @block.scalar
        def _(e):
            def settled():
                e.wait_ge(consts_loaded, CONSTS)

            def refill(p, s, n=D):
                if not isinstance(p, int) or p > 0:
                    e.wait_ge(unit_done, 2 * p + s - 1)
                e.wait_ge(raw_loaded[s], 16 * p + 16)
                e.activation(w_hi[:, s, 0:n], raw[:, s, 0:n], ACT.Copy).then_inc(hi_ready, 1)

            def square(q, c):
                if not (isinstance(q, int) and DC * q + c < 2):
                    e.wait_ge(sq_used, DC * q + c - 1)
                e.activation(sq[:, c % 2, :], x[:, c, :], ACT.Square).then_inc(sq_ready, 1)

            def root():
                e.activation(std, stat_bank[:], ACT.Sqrt, bias=eps[:], scale=1.0 / D).then_inc(std_ready, 1)

            def shifted(n, shift):
                e.wait_ge(mod_ready, n + 1)
                for c in range(DC):
                    e.wait_ge(ux_ready, DC * n + c + 1)
                    e.activation(u_hi[:, c, :], ux[:, c % 2, :], ACT.Identity,
                                 bias=mod[:, shift + c:shift + c + 1]).then_inc(uhi_ready, 1)

            e.wait_ge(consts_loaded, CONSTS)
            e.activation(c_act[:], col("c", 0, 8), ACT.Silu).then_inc(cact_ready, 1)
            e.activation(co[:, 0, :], col("log_dt", 0, 8), ACT.Exp).then_inc(ssm_act, 1)
            e.wait_ge(ssm_vec, 1)
            e.activation(co[:, 3, :], co[:, 1, :], ACT.Exp)
            e.activation(co[:, 7, :], co[:, 5, :], ACT.Sin)
            e.activation(co[:, 8, :], co[:, 6, :], ACT.Sin).then_inc(ssm_act, 1)

            e.wait_ge(x_loaded, 16)
            e.wait_ge(prep_ready, 1)
            for c in range(DC):
                square(0, c)
            for s in range(2):
                refill(0, s)
            e.wait_ge(sq_used, DC)
            root()
            shifted(0, 0)
            for s in range(2):
                refill(IN1 + 1, s)
                e.activation(us[:, s, :], unit_bank[s][:], ACT.Copy).then_inc(taken[s], 1)
            for n in range(2 * SSM_TILES):
                e.wait_ge(bu_done, n + 1)
                e.activation((bu_re, bu_im)[n % 2][:, n // 2, :], score[n % 2][:], ACT.Copy).then_inc(bu_ready, 1)

            with e.Fori(0, HEAD_PAIRS) as j:
                def gate(s, g):
                    settled()
                    e.activation(gates[:, bass.ds(g, 1), :].rearrange("p a t -> p (a t)"), unit_bank[s][:],
                                 ACT.Identity, bias=col("b_gate", g)).then_inc(taken[s], 1)

                def exps(n):
                    W = (n % TB + 1) * P
                    e.wait_ge(s_biased, 8 * j + n + 1)
                    e.activation(nsc[:, n % 2, 0:W], nsc[:, n % 2, 0:W], ACT.Exp, bias=stat[:, n:n + 1],
                                 scale=-1.0).then_inc(p_ready, 1)

                def divide(n):
                    W = (n % TB + 1) * P
                    e.wait_ge(p_weighted, 8 * j + n + 1)
                    e.activation(nsc[:, n % 2, 0:W], nsc[:, n % 2, 0:W], ACT.Identity,
                                 scale=stat[:, 16 + n:17 + n]).then_inc(p_scaled, 1)

                refill(in_pair(j, 1), 0)
                e.activation(q_st, unit_bank[0][:], ACT.Copy, scale=-ATT_SCALE).then_inc(taken[0], 1)
                refill(in_pair(j, 1), 1)
                e.activation(k_st, unit_bank[1][:], ACT.Copy).then_inc(taken[1], 1)
                refill(in_pair(j, 2), 0)
                e.activation(vT_st, unit_bank[0][:], ACT.Copy).then_inc(taken[0], 1)
                refill(in_pair(j, 2), 1)
                gate(1, 3 * j)
                for n in (0, 1):
                    exps(n)
                for n in (0, 1):
                    divide(n)
                refill(in_pair(j, 3), 0)
                gate(0, 3 * j + 1)
                for n in (2, 3):
                    exps(n)
                for n in (2, 3):
                    divide(n)
                refill(in_pair(j, 3), 1)
                gate(1, 3 * j + 2)
                for n in (4, 5):
                    exps(n)
                for n in (4, 5):
                    divide(n)
                for n in (6, 7):
                    exps(n)
                for n in (6, 7):
                    divide(n)
                e.wait_ge(pv_done, 2 * j + 2)
                settled()
                e.activation(h_hi[:, bass.ds(7 + j, 1), :].rearrange("p a t -> p (a t)"), out_bank[:],
                             ACT.Copy).then_inc(ohi_ready, 1)
            for i in range(2):
                p = in_pair(HEAD_PAIRS, 0) + i
                for s in range(2):
                    refill(p + 1, s, D if i == 0 else 6 * P)
                    g = 3 * HEAD_PAIRS + 2 * i + s
                    e.activation(gates[:, g, :], unit_bank[s][:], ACT.Identity,
                                 bias=col("b_gate", g)).then_inc(taken[s], 1)
            for m in range(2):
                e.wait_ge(y_ready, m + 1)
                e.activation(gelu_y[:, m, :], ssm_y[:, m, :], ACT.Gelu_apprx_tanh).then_inc(gelu_ready, 1)
            for m in range(2):
                e.wait_ge(glu_done, m + 1)
                e.activation(glu_s[:, m, :], score[m][:], ACT.Sigmoid, bias=col("b_glu", m)).then_inc(glu_ready, 1)
            for m in range(2):
                e.wait_ge(yy_ready, m + 1)
                e.activation(h_hi[:, 5 + m, :], ssm_y[:, m, :], ACT.Copy).then_inc(yhi_ready, 1)
            by_branch = gates.rearrange("p (g c) t -> p g c t", g=2)

            def merge(i, n):
                for s in range(2):
                    g = by_branch[:, :, bass.ds(2 * i + s, 1), :].rearrange("p g a t -> p g (a t)")
                    settled()
                    e.activation(g, g, ACT.Sigmoid).then_inc(sig_ready, 1)
                for s in range(2):
                    refill(MERGE1 + i + 1, s, n)
                    e.wait_ge(merged_ready, 2 * i + s + 1)
                    settled()
                    e.activation(u_hi[:, bass.ds(2 * i + s, 1), :].rearrange("p a t -> p (a t)"),
                                 slot(22 + s), ACT.Copy).then_inc(mhi_ready, 1)

            with e.Fori(0, DC // 2 - 1) as i:
                merge(i, 6 * P)
            merge(DC // 2 - 1, D)
            with e.Fori(0, DC // 2) as i:
                for s in range(2):
                    refill(OUT1 + i + 1, s)

            for c in range(DC):
                e.wait_ge(taken[c % 2], OUT1 + c // 2 + 2)
                square(1, c)
            e.wait_ge(sq_used, 2 * DC)
            root()
            shifted(1, 24)
            for half in range(2):
                p0 = FFN1 + half * FFN1_HALF
                with e.Fori(0, HALF1) as i:
                    refill(p0 + i + 1, 0)
                    e.wait_ge(prep_ready, 2)
                    e.activation(a_pad[:, 2:T + 2], unit_bank[0][:], ACT.Copy).then_inc(taken[0], 1)
                    e.wait_ge(conv_ready, HALF1 * half + i + 1)
                    e.activation(ffn_s, ffn_u, ACT.Silu).then_inc(silu_ready, 1)
                    refill(p0 + i + 1, 1)
                    e.wait_ge(taken[1], p0 + i + 2)
                    settled()
                    e.activation(h_hi[:, bass.ds(i, 1), :].rearrange("p a t -> p (a t)"), ffn_h,
                                 ACT.Copy).then_inc(hhi_ready, 1)
                with e.Fori(0, DC // 2 - half) as i:
                    for s in range(2):
                        refill(p0 + HALF1 + i + 1, s)
            for c in range(DC):
                e.wait_ge(taken[c % 2], LAYER0 - DC // 2 + c // 2 + 2)
                square(2, c)
            e.wait_ge(sq_used, 3 * DC)
            root()

            with e.Fori(0, LAYERS) as l:
                def pre_norm(k):
                    for c in range(DC):
                        e.wait_ge(x_ready, DC * (3 * l + k) + c + 1)
                        settled()
                        e.activation(u_hi[:, c, :], x[:, c, :], ACT.Identity,
                                     scale=col("norm_g", (6 * l + 2 * k) * DC + c)).then_inc(uhi_ready, 1)
                        square(3 + 3 * l + k, c)
                    e.wait_ge(sq_used, DC * (4 + 3 * l + k))
                    root()

                def f_squares(p, s, r, c):
                    e.wait_ge(taken[s], p + 2)
                    settled()
                    e.activation(sq[:, 0, :], f[:, bass.ds(c, 1), :].rearrange("p a t -> p (a t)"),
                                 ACT.Square).then_inc(fsq_ready, 1)

                def f_root(r):
                    e.wait_ge(fsum_ready, r + 1)
                    root()

                for s in range(2):
                    refill(layer(l), s)
                for s_ffn in range(2):
                    k_norm = 2 * s_ffn
                    pre_norm(k_norm)
                    for half in range(2):
                        p0 = ffn2(l, s_ffn) + half * FFN2_HALF
                        h0 = 16 + 44 * l + 22 * s_ffn + HALF2 * half

                        def hidden(i, n):
                            refill(p0 + i + 1, 0, n)
                            e.wait_ge(taken[0], p0 + i + 2)
                            e.activation(ffn_s, ffn_g, ACT.Silu).then_inc(silu_ready, 1)
                            refill(p0 + i + 1, 1, n)
                            e.wait_ge(hidden_ready, h0 - 16 + i + 1)
                            settled()
                            e.activation(h_hi[:, bass.ds(i, 1), :].rearrange("p a t -> p (a t)"), ffn_h,
                                         ACT.Copy).then_inc(hhi_ready, 1)

                        def out(i, n):
                            for s in range(2):
                                p = p0 + HALF2 + i
                                if n:
                                    refill(p + 1, s, n)
                                if half == 1:
                                    f_squares(p, s, 3 * l + k_norm, 2 * i + s)

                        with e.Fori(0, HALF2 - 1) as i:
                            hidden(i, D)
                        hidden(HALF2 - 1, RING)
                        with e.Fori(0, DC // 2 - 1) as i:
                            out(i, RING)
                        out(DC // 2 - 1, D if half == 0 or s_ffn == 0 else 0)
                    f_root(3 * l + k_norm)
                    if s_ffn:
                        continue
                    pm = layer(l) + MIX2
                    pre_norm(1)
                    for s in range(2):
                        refill(pm + 1, s)
                    with e.Fori(0, HEAD_PAIRS) as j:
                        J = HEAD_PAIRS * l + j

                        def decay(h):
                            at = 16 * J + 2 * TB * h
                            for n in range(TB):
                                i = TB - 1 - n
                                e.wait_ge(z_done, 8 * J + TB * h + n + 1)
                                e.activation(softp[:, i, 0:T - i * P], z_bank[i][:, 0:T - i * P],
                                             ACT.Abs).then_inc(act_step, 1)
                            for n in range(TB):
                                az = softp[:, TB - 1 - n, 0:(n + 1) * P]
                                e.wait_ge(act_step, at + n + 1)
                                e.activation(az, az, ACT.Exp, scale=-1.0).then_inc(act_step, 1)

                        def logs(h):
                            at = 16 * J + 2 * TB * h + TB
                            for n in range(TB):
                                az = softp[:, TB - 1 - n, 0:(n + 1) * P]
                                e.wait_ge(act_step, at + n + 1)
                                e.activation(az, az, ACT.Ln, bias=1.0).then_inc(softp_ready, 1)

                        def weights(h):
                            if h == 1:
                                e.wait_ge(pv2_done, 2 * J + 1)
                            for n in range(TB):
                                i = TB - 1 - n
                                e.wait_ge(sums_taken, 8 * J + TB * (h + 1) + n + 1)
                                e.activation(a_keys[:, i, 0:T - i * P], own[:, i, 0:T - i * P],
                                             ACT.Exp).then_inc(a_ready, 1)

                        decay(0)
                        logs(0)
                        refill(pm + 2 * j + 2, 0)
                        weights(0)
                        refill(pm + 2 * j + 2, 1)
                        decay(1)
                        logs(1)
                        refill(pm + 2 * j + 3, 0)
                        weights(1)
                        refill(pm + 2 * j + 3, 1)
                        e.wait_ge(pv2_done, 2 * J + 2)
                        settled()
                        e.activation(h_hi[:, bass.ds(j, 1), :].rearrange("p a t -> p (a t)"), out_bank[:],
                                     ACT.Copy).then_inc(ohi2_ready, 1)
                    for s in range(2):
                        refill(pm + MIX2_IN, s)
                    for m in range(2):
                        e.wait_ge(pool_done, 2 * l + m + 1)
                        settled()
                        e.activation(h_hi[:, 6 + m, :], score[m][:], ACT.Identity,
                                     scale=col("pool_scale", 2 * l + m)).then_inc(phi_ready, 1)
                    for m in range(2):
                        e.wait_ge(conv2_ready, 2 * l + m + 1)
                        e.activation(h_hi[:, 4 + m, :], cx[:, 2 + m, :], ACT.Copy).then_inc(chi_ready, 1)
                    with e.Fori(0, DC // 2) as i:
                        for s in range(2):
                            refill(pm + MIX2_IN + i + 1, s)
                            f_squares(pm + MIX2_IN + i, s, 3 * l + 1, 2 * i + s)
                    f_root(3 * l + 1)

        @block.vector
        def _(e):
            step = Steps(e, vec_step)

            def settled():
                e.wait_ge(consts_loaded, CONSTS)

            def passed():
                e.sem_inc(vec_passed, 1)

            def flat(ap):
                return ap.rearrange("p a t -> p (a t)")

            for free in (*taken, o_taken, o2_taken):
                e.sem_inc(free, 1)
            e.sem_inc(sums_taken, TB)
            settled()
            e.memset(eps[:], EPS)
            e.tensor_scalar(mask_b[:], tab("strict"), 1e30, -1e30, ALU.mult, ALU.add)
            e.memset(C_t[:], 0.0)
            e.memset(pool_w[:], 0.0)
            e.memset(slot(22, 1), 0.0)
            step(e.tensor_scalar(half_g[:], col("norm_g", 0, 96), 0.5, None, ALU.mult))
            e.sem_inc(prep_ready, 1)

            def cc(n):
                return co[:, n, :]

            def tt(out, a, b, op):
                step(e.tensor_tensor(out, a, b, op))

            lr, li = col("a_re", 0, 8), col("a_im", 0, 8)
            dt, lrdt, ang, mag, turns, red, red_c, sin, cos, abr, abi, den, rden, fre, fim, t1, t2, zr, zi = (
                cc(n) for n in range(19))
            e.wait_ge(ssm_act, 1)
            tt(lrdt, lr, dt, ALU.mult)
            tt(ang, li, dt, ALU.mult)
            step(e.tensor_scalar(turns, ang, INV_TWO_PI, ROUND_MAGIC, ALU.mult, ALU.add))
            step(e.tensor_scalar(turns, turns, ROUND_MAGIC, None, ALU.subtract))
            step(e.scalar_tensor_tensor(red, turns, -TWO_PI_1, ang, ALU.mult, ALU.add))
            step(e.scalar_tensor_tensor(red, turns, -TWO_PI_2, red, ALU.mult, ALU.add))
            step(e.scalar_tensor_tensor(red, turns, -TWO_PI_3, red, ALU.mult, ALU.add))
            step(e.tensor_scalar(red, red, PI_SAFE, -PI_SAFE, ALU.min, ALU.max))
            step(e.scalar_tensor_tensor(t1, red, -1.0, red, ALU.mult, ALU.max))
            e.tensor_scalar(red_c, t1, -1.0, HALF_PI, ALU.mult, ALU.add).then_inc(ssm_vec, 1)
            e.wait_ge(ssm_act, 2)
            tt(abr, mag, cos, ALU.mult)
            tt(abi, mag, sin, ALU.mult)
            tt(t1, lr, lr, ALU.mult)
            tt(t2, li, li, ALU.mult)
            tt(den, t1, t2, ALU.add)
            step(e.reciprocal(rden, den))
            step(e.tensor_scalar(zr, abr, -1.0, None, ALU.add))
            tt(t1, zr, lr, ALU.mult)
            tt(t2, abi, li, ALU.mult)
            tt(t1, t1, t2, ALU.add)
            tt(fre, t1, rden, ALU.mult)
            tt(t1, abi, lr, ALU.mult)
            tt(t2, zr, li, ALU.mult)
            tt(t1, t1, t2, ALU.subtract)
            tt(fim, t1, rden, ALU.mult)

            def per_state(name):
                return col(name, 0, SSM_TILES * SSM_CH).rearrange("p (i c) -> p i c", c=SSM_CH)

            def wide(ap, n):
                return ap[:, :, None].broadcast_to([P, SSM_TILES, n])

            b1 = slot(23)[:, 0:P].rearrange("p (i c) -> p i c", c=SSM_CH)
            b2 = slot(24)[:, 0:P].rearrange("p (i c) -> p i c", c=SSM_CH)
            B_pad = slot(22).rearrange("p (k i c) -> p k i c", k=2, c=32)
            for part, (x1, x2, op) in enumerate(((fre, fim, ALU.subtract), (fim, fre, ALU.add))):
                tt(b1, per_state("b_re"), wide(x1, SSM_CH), ALU.mult)
                tt(b2, per_state("b_im"), wide(x2, SSM_CH), ALU.mult)
                for h in range(2):
                    rows, ch = slice(64 * h, 64 * h + 64), slice(SSM_CH * h, SSM_CH * h + SSM_CH)
                    tt(B_pad[rows, part, :, ch], b1[rows], b2[rows], op)
            for h in range(2):
                rows, ch = slice(64 * h, 64 * h + 64), slice(SSM_CH * h, SSM_CH * h + SSM_CH)
                step(e.tensor_copy(C_t[rows, 0, :, ch], per_state("c_re")[rows]))
                step(e.tensor_scalar(C_t[rows, 1, :, ch], per_state("c_im")[rows], -1.0, None, ALU.mult))
            e.sem_inc(B_padded, 1)

            e.wait_ge(cact_ready, 1)
            for k in range(DC):
                e.wait_ge(ada_loaded[k % 2], 16 * (k // 2) + 16)
                if k == 0:
                    e.tensor_scalar(ada_acc[:], ada_w[:, 0, :], c_act[:, 0:1], None, ALU.mult).then_inc(ada_used, 1)
                else:
                    e.wait_ge(ada_used, k)
                    e.scalar_tensor_tensor(ada_acc[:], ada_w[:, k % 2, :], c_act[:, k:k + 1], ada_acc[:],
                                           ALU.mult, ALU.add).then_inc(ada_used, 1)

            def take_mod(first, columns, n, count):
                e.wait_ge(mod_sum, count)
                step(e.tensor_tensor(mod[:, first:first + n], out_bank[:, columns:columns + n],
                                     col("b_ada", first, n), ALU.add))

            def amplify(n, g_name, scale):
                step(e.scalar_tensor_tensor(amp[:, 8 * n:8 * n + 8], mod[:, scale:scale + 8], 1.0,
                                            col(g_name, 0, 8), ALU.add, ALU.mult))

            take_mod(0, 0, 16, 1)
            amplify(0, "g_mix", 8)
            e.sem_inc(mod_ready, 1)

            def invert(st):
                e.wait_ge(std_ready, st + 1)
                step(e.reciprocal(rstd[:], std))

            def modulate(n, st, shift):
                invert(st)
                for c in range(DC):
                    if c >= 2:
                        e.wait_ge(u_ready, DC * n + c - 1)
                    e.scalar_tensor_tensor(ux[:, c % 2, :], x[:, c, :], amp[:, 8 * n + c:8 * n + c + 1], rstd[:],
                                           ALU.mult, ALU.mult).then_inc(ux_ready, 1)
                    if c:
                        shift_lo(n, c - 1, shift)
                shift_lo(n, DC - 1, shift)

            def shift_lo(n, c, shift):
                e.wait_ge(uhi_ready, DC * n + c + 1)
                e.scalar_tensor_tensor(u_lo[:, c, :], ux[:, c % 2, :], mod[:, shift + c:shift + c + 1],
                                       as32(u_hi[:, c, :]), ALU.add, ALU.subtract).then_inc(u_ready, 1)

            modulate(0, 0, 0)
            e.wait_ge(B_turned, 1)
            e.tensor_copy(B_t[:].rearrange("p k n -> p (k n)"), out_bank[:]).then_inc(B_ready, 1)

            e.memset(E1[:, 0, :, 0:1], 1.0)
            e.memset(E1[:, 1, :, 0:1], 0.0)
            e.memset(E16[:, 0, :, 0:1], 1.0)
            e.memset(E16[:, 1, :, 0:1], 0.0)
            step(e.tensor_copy(zr, cos))
            step(e.tensor_copy(zi, sin))
            for E, top in ((E1, 16), (E16, 32)):
                n = 1
                while n < top:
                    re, im = E[:, 0, :, 0:n], E[:, 1, :, 0:n]
                    p1 = slot(23)[:, 0:8 * n].rearrange("p (i c) -> p i c", c=n)
                    p2 = slot(24)[:, 0:8 * n].rearrange("p (i c) -> p i c", c=n)
                    tt(p1, re, wide(zr, n), ALU.mult)
                    tt(p2, im, wide(zi, n), ALU.mult)
                    tt(E[:, 0, :, n:2 * n], p1, p2, ALU.subtract)
                    tt(p1, re, wide(zi, n), ALU.mult)
                    tt(p2, im, wide(zr, n), ALU.mult)
                    tt(E[:, 1, :, n:2 * n], p1, p2, ALU.add)
                    tt(t1, zr, zr, ALU.mult)
                    tt(t2, zi, zi, ALU.mult)
                    step(e.scalar_tensor_tensor(zi, zr, 2.0, zi, ALU.mult, ALU.mult))
                    tt(zr, t1, t2, ALU.subtract)
                    n *= 2
            e.wait_ge(bu_ready, 2 * SSM_TILES)

            def scan_tile(i):
                c_t, s_t, p1, p2, wr, wi = (ssm_tmp[:, n, :] for n in range(6))
                br, bi = flat(bu_re[:, bass.ds(i, 1), :]), flat(bu_im[:, bass.ds(i, 1), :])
                r = co[:, 3, bass.ds(i, 1)].broadcast_to([P, T])

                def power(part, b_part, out, op):
                    grid = out.rearrange("p (a b) -> p a b", b=16)
                    big = flat(E16[:, part, bass.ds(i, 1), :])[:, :, None].broadcast_to([P, 32, 16])
                    small = flat(E1[:, b_part, bass.ds(i, 1), :])[:, None, :].broadcast_to([P, 32, 16])
                    tt(grid, big, small, op)

                power(0, 0, p1, ALU.mult)
                power(1, 1, p2, ALU.mult)
                tt(c_t, p1, p2, ALU.subtract)
                power(0, 1, p1, ALU.mult)
                power(1, 0, p2, ALU.mult)
                tt(s_t, p1, p2, ALU.add)
                tt(p1, c_t, br, ALU.mult)
                tt(p2, s_t, bi, ALU.mult)
                tt(wr, p1, p2, ALU.add)
                tt(p1, c_t, bi, ALU.mult)
                tt(p2, s_t, br, ALU.mult)
                tt(wi, p1, p2, ALU.subtract)
                step(e.tensor_tensor_scan(br, r, wr, 0.0, ALU.mult, ALU.add))
                step(e.tensor_tensor_scan(bi, r, wi, 0.0, ALU.mult, ALU.add))
                tt(p1, c_t, br, ALU.mult)
                tt(p2, s_t, bi, ALU.mult)
                tt(wr, s_t, br, ALU.mult)
                tt(wi, c_t, bi, ALU.mult)
                tt(br, p1, p2, ALU.subtract)
                e.tensor_tensor(bi, wr, wi, ALU.add).then_inc(scan_ready, 1)

            with e.Fori(0, HEAD_PAIRS) as j:
                start = step.enter(j, HEADS1_STEPS)

                def bias(h):
                    step(e.tensor_scalar(bias_h, tab("dist"), col("slopes", 2 * j + h), None, ALU.mult))

                def score_bias(n):
                    b = n % TB
                    W = (b + 1) * P
                    e.wait_ge(s_done, 8 * j + n + 1)
                    passed()
                    e.tensor_tensor_reduce(nsc[:, n % 2, 0:W], score[n % 2][:, 0:W], bias_h[:, T - W:T], 1.0, 3e38,
                                           ALU.add, ALU.min, stat[:, n:n + 1]).then_inc(s_biased, 1)

                def weigh(n):
                    W = (n % TB + 1) * P
                    e.wait_ge(p_ready, 8 * j + n + 1)
                    step(e.tensor_tensor_reduce(nsc[:, n % 2, 0:W], nsc[:, n % 2, 0:W], tab("count", T - W, T),
                                                1.0, 0.0, ALU.mult, ALU.add, stat[:, 8 + n:9 + n]))
                    e.reciprocal(stat[:, 16 + n:17 + n], stat[:, 8 + n:9 + n]).then_inc(p_weighted, 1)

                def take_probs(n):
                    b = n % TB
                    e.wait_ge(p_turned, 8 * j + n + 1)
                    if n == TB:
                        e.wait_ge(pv_done, 2 * j + 1)
                    e.tensor_copy(pT(b).rearrange("p i t -> p (i t)"), mix[n % 2][:, 0:(b + 1) * P]).then_inc(
                        pT_ready, 1)

                scan_tile(2 * j)
                scan_tile(2 * j + 1)
                bias(0)
                e.wait_ge(v_turned, j + 1)
                e.tensor_copy(v_nat.rearrange("p i d -> p (i d)"), out_bank[:]).then_inc(v_ready, 1)
                score_bias(0)
                score_bias(1)
                weigh(0)
                weigh(1)
                for n in range(0, 2 * TB, 2):
                    take_probs(n)
                    if n + 2 == TB:
                        bias(1)
                    if n + 2 < 2 * TB:
                        score_bias(n + 2)
                    take_probs(n + 1)
                    if n + 2 < 2 * TB:
                        score_bias(n + 3)
                        weigh(n + 2)
                        weigh(n + 3)
                e.wait_ge(ohi_ready, j + 1)
                e.tensor_tensor(flat(h_lo[:, bass.ds(j, 1), :]), out_bank[:],
                                as32(flat(h_hi[:, bass.ds(7 + j, 1), :])), ALU.subtract).then_inc(o_taken, 1)
            step.at = start + HEAD_PAIRS * HEADS1_STEPS
            for m in range(2):
                e.wait_ge(y_done, TB * (m + 1))
                e.scalar_tensor_tensor(ssm_y[:, m, :], us[:, m, :], col("d_skip", m), mix[m][:], ALU.mult,
                                       ALU.add).then_inc(y_ready, 1)
            for m in range(2):
                e.wait_ge(glu_ready, m + 1)
                e.tensor_tensor(ssm_y[:, m, :], gelu_y[:, m, :], glu_s[:, m, :], ALU.mult).then_inc(yy_ready, 1)
            for m in range(2):
                e.wait_ge(yhi_ready, m + 1)
                e.tensor_tensor(h_lo[:, 4 + m, :], ssm_y[:, m, :], as32(h_hi[:, 5 + m, :]),
                                ALU.subtract).then_inc(y_split, 1)
            def add_rows(a, out, k, like):
                e.wait_ge(ada_rows_loaded[a % 4], 16 * (a // 4) + 16)
                if k == 0:
                    e.tensor_scalar(out, ada_rows[:, a % 4, :], c_act[:, 0:1], None, ALU.mult).then_inc(ada_used, 1)
                else:
                    e.wait_ge(ada_used, DC + a - like + 1)
                    e.scalar_tensor_tensor(out, ada_rows[:, a % 4, :], c_act[:, k:k + 1], out, ALU.mult,
                                           ALU.add).then_inc(ada_used, 1)

            e.wait_ge(y_split, 2)
            for i in range(DC // 2):
                for s in range(2):
                    p, c = MERGE1 + i, 2 * i + s
                    add_rows(c, gate_sum, c, 1)
                    g_att = flat(gates[:, bass.ds(c, 1), :])
                    g_ssm = flat(gates[:, bass.ds(c + DC, 1), :])
                    e.wait_ge(sig_ready, c + 1)
                    e.wait_ge(unit_done, 2 * p + s + 1)
                    step(e.tensor_tensor(slot(24), score[s][:], g_ssm, ALU.mult))
                    e.tensor_tensor(slot(25), unit_bank[s][:], g_att, ALU.mult).then_inc(taken[s], 1)
                    e.wait_ge(taken[s], p + 2)
                    e.tensor_tensor(slot(22 + s), slot(24), slot(25), ALU.add).then_inc(merged_ready, 1)
                    e.wait_ge(mhi_ready, c + 1)
                    e.tensor_tensor(flat(u_lo[:, bass.ds(c, 1), :]), slot(22 + s),
                                    as32(flat(u_hi[:, bass.ds(c, 1), :])), ALU.subtract).then_inc(m_ready, 1)
            take_mod(16, 0, DC, 2)

            def take_update(p, s, c, gate):
                xc = flat(x[:, bass.ds(c, 1), :])
                e.wait_ge(unit_done, 2 * p + s + 1)
                e.scalar_tensor_tensor(xc, unit_bank[s][:], mod[:, bass.ds(gate + c, 1)], xc, ALU.mult,
                                       ALU.add).then_inc(taken[s], 1)

            for k in range(DC):
                for n in range(3):
                    a = DC + 3 * k + n
                    add_rows(a, ada_sums[:, n * D:(n + 1) * D], k, 3)
                take_update(OUT1 + k // 2, k % 2, k, 16)
            take_mod(24, DC, 3 * DC, 5)
            amplify(1, "g_ffn", 32)
            e.sem_inc(mod_ready, 1)

            def gated_update(p0, gate):
                with e.Fori(0, DC // 2) as i:
                    for s in range(2):
                        take_update(p0 + i, s, 2 * i + s, gate)

            modulate(1, 1, 24)
            step(e.memset(a_pad[:, 0:2], 0.0))
            e.sem_inc(prep_ready, 1)
            for half in range(2):
                p0 = FFN1 + half * FFN1_HALF
                with e.Fori(0, HALF1) as i:
                    start = step.enter(i, CONV_STEPS)
                    c = HALF1 * half + i
                    e.wait_ge(taken[0], p0 + i + 2)
                    settled()
                    step(e.tensor_scalar(ffn_u, a_pad[:, 2:T + 2], col("w_conv", c), col("b_conv", c),
                                         ALU.mult, ALU.add))
                    step(e.scalar_tensor_tensor(ffn_u, a_pad[:, 1:T + 1], col("w_conv", 16 + c), ffn_u,
                                                ALU.mult, ALU.add))
                    e.scalar_tensor_tensor(ffn_u, a_pad[:, 0:T], col("w_conv", 32 + c), ffn_u,
                                           ALU.mult, ALU.add).then_inc(conv_ready, 1)
                    e.wait_ge(silu_ready, c + 1)
                    e.wait_ge(unit_done, 2 * (p0 + i) + 2)
                    e.tensor_tensor(ffn_h, unit_bank[1][:], ffn_s, ALU.mult).then_inc(taken[1], 1)
                    e.wait_ge(hhi_ready, c + 1)
                    e.tensor_tensor(flat(h_lo[:, bass.ds(i, 1), :]), ffn_h, as32(flat(h_hi[:, bass.ds(i, 1), :])),
                                    ALU.subtract).then_inc(h_ready, 1)
                step.at = start + HALF1 * CONV_STEPS
                gated_update(p0 + HALF1, 40)
            invert(2)
            for c in range(DC):
                e.scalar_tensor_tensor(x[:, c, :], x[:, c, :], col("g_final", c), rstd[:], ALU.mult,
                                       ALU.mult).then_inc(x_ready, 1)

            with e.Fori(0, LAYERS) as l:
                step.enter(l, LAYER_STEPS)
                calls = step.calls

                def pre_norm(k):
                    for c in range(DC):
                        e.wait_ge(uhi_ready, DC * (2 + 3 * l + k) + c + 1)
                        e.scalar_tensor_tensor(u_lo[:, c, :], x[:, c, :], col("norm_g", (6 * l + 2 * k) * DC + c),
                                               as32(u_hi[:, c, :]), ALU.mult, ALU.subtract).then_inc(u_ready, 1)
                    invert(3 + 6 * l + 2 * k)
                    passed()

                def post_norm(k):
                    invert(4 + 6 * l + 2 * k)
                    for c in range(DC):
                        at = (6 * l + 2 * k + 1) * DC + c
                        g = col("norm_g", at) if k == 1 else half_g[:, bass.ds(at, 1)]
                        step(e.scalar_tensor_tensor(ux[:, c % 2, :], f[:, c, :], g, rstd[:], ALU.mult, ALU.mult))
                        e.tensor_tensor(x[:, c, :], x[:, c, :], ux[:, c % 2, :], ALU.add).then_inc(x_ready, 1)

                def f_out(p0, r, add, squares):
                    if squares:
                        e.memset(acc, 0.0).then_inc(fsq_added, 1)
                    with e.Fori(0, DC // 2) as i:
                        for s in range(2):
                            fc = flat(f[:, bass.ds(2 * i + s, 1), :])
                            e.wait_ge(unit_done, 2 * (p0 + i) + s + 1)
                            if add:
                                e.tensor_tensor(fc, unit_bank[s][:], fc, ALU.add).then_inc(taken[s], 1)
                            else:
                                settled()
                                e.tensor_copy(fc, unit_bank[s][:]).then_inc(taken[s], 1)
                            if squares:
                                e.wait_ge(fsq_ready, DC * r + 2 * i + s + 1)
                                e.wait_ge(fsq_added, (DC + 1) * r + 2 * i + s + 1)
                                e.tensor_tensor(acc, acc, sq[:, 0, :], ALU.add).then_inc(fsq_added, 1)

                for s_ffn in range(2):
                    k_norm = 2 * s_ffn
                    pre_norm(k_norm)
                    for half in range(2):
                        p0 = ffn2(l, s_ffn) + half * FFN2_HALF
                        h0 = 16 + 44 * l + 22 * s_ffn + HALF2 * half
                        with e.Fori(0, HALF2) as i:
                            p = p0 + i
                            e.wait_ge(unit_done, 2 * p + 1)
                            e.tensor_tensor(ffn_g, unit_bank[0][:], rstd[:], ALU.mult).then_inc(taken[0], 1)
                            e.wait_ge(unit_done, 2 * p + 2)
                            e.tensor_tensor(ffn_u, unit_bank[1][:], rstd[:], ALU.mult).then_inc(taken[1], 1)
                            e.wait_ge(silu_ready, h0 + i + 1)
                            e.wait_ge(taken[1], p + 2)
                            e.tensor_tensor(ffn_h, ffn_s, ffn_u, ALU.mult).then_inc(hidden_ready, 1)
                            e.wait_ge(hhi_ready, h0 + i + 1)
                            e.tensor_tensor(flat(h_lo[:, bass.ds(i, 1), :]), ffn_h,
                                            as32(flat(h_hi[:, bass.ds(i, 1), :])), ALU.subtract).then_inc(h_ready, 1)
                        f_out(p0 + HALF2, 3 * l + k_norm, half == 1, half == 1)
                    post_norm(k_norm)
                    if s_ffn:
                        continue
                    pm = layer(l) + MIX2
                    pre_norm(1)
                    for g in range(2):
                        rows = slice(64 * g, 64 * g + 64)
                        step(e.tensor_copy(pool_w[rows, :, rows], tabs[rows, bass.ds(
                            l * P + TABS["pool_w"][0], P)].rearrange("p (m n) -> p m n", m=2)))
                    A, B = padded[:, 0, :], padded[:, 1, :]
                    Z = 16
                    lower, upper = slice(0, 64), slice(64, P)

                    def trailing(dst, src, lag, rows=slice(0, P)):
                        tt(dst[rows, Z:], src[rows, Z:], src[rows, Z - lag:T + Z - lag], ALU.add)

                    def pool(m):
                        step(e.tensor_copy(A[:, Z:], f[:, m, :]))
                        trailing(B, A, 1)
                        if m:
                            trailing(A, B, 2)
                            trailing(B, A, 4)
                        trailing(A, B, 8 if m else 2, upper)
                        head = col("inv_head", 16 * m, 16)
                        for rows, src in ((lower, B), (upper, A)):
                            step(e.tensor_scalar(pooled[rows, m, :], src[rows, Z:], col("inv_w", m)[rows], None, ALU.mult))
                            tt(pooled[rows, m, 0:16], src[rows, Z:Z + 16], head[rows], ALU.mult)
                        e.tensor_tensor(pooled[:, m, :], pooled[:, m, :], f[:, m, :], ALU.subtract).then_inc(pool_in, 1)

                    def take(p, s, out):
                        e.wait_ge(unit_done, 2 * p + s + 1)
                        e.tensor_tensor(out, unit_bank[s][:], rstd[:], ALU.mult).then_inc(taken[s], 1)

                    def take_q(j):
                        p = pm + 2 * j
                        e.wait_ge(unit_done, 2 * p + 1)
                        e.scalar_tensor_tensor(q_st, unit_bank[0][:], ATT_SCALE, rstd[:], ALU.mult,
                                               ALU.mult).then_inc(taken[0], 1)

                    def head_pair(j, last):
                        J = HEAD_PAIRS * l + j

                        def parts(h):
                            for n in range(TB):
                                i = TB - 1 - n
                                z = z_bank[i][:, 0:T - i * P]
                                e.wait_ge(act_step, 16 * J + 2 * TB * h + n + 1)
                                e.tensor_scalar(kept[:, i, 0:T - i * P], z, 0.0, None, ALU.max)
                                t = e.tensor_scalar(own[:, i, 0:T - i * P], z, 0.0, None, ALU.min)
                            step(t)

                        def keep_logs(h):
                            for n in range(TB):
                                i = TB - 1 - n
                                W = T - i * P
                                e.wait_ge(softp_ready, 8 * J + TB * h + n + 1)
                                e.scalar_tensor_tensor(kept[:, i, 0:W], softp[:, i, 0:W], -1.0, kept[:, i, 0:W],
                                                       ALU.mult, ALU.subtract)
                                step(e.tensor_tensor(own[:, i, 0:W], own[:, i, 0:W], softp[:, i, 0:W], ALU.subtract))
                                e.tensor_tensor(own[:, i, 0:P], own[:, i, 0:P], mask_b[:], ALU.add)
                                e.tensor_tensor(kept[:, i, 0:P], kept[:, i, 0:P], tab("strict"),
                                                ALU.mult).then_inc(sp_ready, 1)

                        def add_sums(h):
                            for n in range(TB):
                                i = TB - 1 - n
                                W = T - i * P
                                e.wait_ge(R_done, 8 * J + TB * h + n + 1)
                                e.tensor_tensor(own[:, i, 0:W], z_bank[i][:, 0:W], own[:, i, 0:W],
                                                ALU.add).then_inc(sums_taken, 1)

                        parts(0)
                        if last:
                            pool(0)
                        keep_logs(0)
                        take(pm + 2 * j + 1, 0, vT_st)
                        add_sums(0)
                        take(pm + 2 * j + 1, 1, flat(f[:, bass.ds(j, 1), :]))
                        e.wait_ge(v2_turned, J + 1)
                        e.tensor_copy(v_nat.rearrange("p i d -> p (i d)"), out_bank[:]).then_inc(v2_ready, 1)
                        parts(1)
                        if last:
                            pool(1)
                        keep_logs(1)
                        if last:
                            take(pm + 2 * HEAD_PAIRS, 0, f[:, HEAD_PAIRS, :])
                        else:
                            take_q(j + 1)
                        add_sums(1)
                        take(pm + 2 * j + 2, 1, f[:, HEAD_PAIRS + 1, :] if last else k_st)
                        e.wait_ge(ohi2_ready, J + 1)
                        e.tensor_tensor(flat(h_lo[:, bass.ds(j, 1), :]), out_bank[:],
                                        as32(flat(h_hi[:, bass.ds(j, 1), :])), ALU.subtract).then_inc(o2_taken, 1)

                    step(e.memset(padded[:, :, 0:Z], 0.0))
                    take_q(0)
                    take(pm, 1, k_st)
                    with e.Fori(0, HEAD_PAIRS - 1) as j:
                        start = step.enter(j, HEADS2_STEPS)
                        head_pair(j, False)
                    step.at = start + (HEAD_PAIRS - 1) * HEADS2_STEPS
                    head_pair(HEAD_PAIRS - 1, True)
                    for s in range(2):
                        take(pm + 2 * HEAD_PAIRS + 1, s, f[:, HEAD_PAIRS + 2 + s, :])
                    for m in range(2):
                        tt(A[:, Z:], f[:, 2 + m, :], f[:, 4 + m, :], ALU.mult)
                        y = cx[:, m, :]

                        def tap(n):
                            return col("conv_w2", 6 * l + 2 * n + m)

                        step(e.tensor_scalar(y, A[:, Z - 2:T + Z - 2], tap(0), None, ALU.mult))
                        for n in (1, 2):
                            step(e.scalar_tensor_tensor(y, A[:, Z - 2 + n:T + Z - 2 + n], tap(n), y, ALU.mult, ALU.add))
                        e.tensor_tensor(cx[:, 2 + m, :], y, f[:, 6 + m, :], ALU.mult).then_inc(conv2_ready, 1)
                    for m in range(2):
                        e.wait_ge(phi_ready, 2 * l + m + 1)
                        e.scalar_tensor_tensor(h_lo[:, 6 + m, :], score[m][:], col("pool_scale", 2 * l + m),
                                               as32(h_hi[:, 6 + m, :]), ALU.mult, ALU.subtract).then_inc(cat_ready, 1)
                    for m in range(2):
                        e.wait_ge(chi_ready, 2 * l + m + 1)
                        e.tensor_tensor(h_lo[:, 4 + m, :], cx[:, 2 + m, :], as32(h_hi[:, 4 + m, :]),
                                        ALU.subtract).then_inc(cat_ready, 1)
                    f_out(pm + MIX2_IN, 3 * l + 1, False, True)
                    post_norm(1)
                assert step.calls - calls + (HEAD_PAIRS - 2) * HEADS2_STEPS == LAYER_STEPS, step.calls - calls


def _tiles(w):
    K, F = w.shape
    return w.reshape(K // P, P, F // P, P).transpose(2, 1, 0, 3).reshape(F // P, P, K)


def _cols(v):
    return v.reshape(-1, P).T


def _layout(a):
    import numpy as np

    lead = {k: v[0] for k, v in a.items() if not k.endswith("_2") and k != "g_final"}
    out = {"x": lead["x"].T.reshape(DC, P, T).transpose(1, 0, 2)}
    t_s = np.arange(P)[:, None] + (T - P) - np.arange(T)[None, :]
    seen = t_s >= 0
    count = (seen * ((t_s <= P) * 1 + (t_s % 4 == 0) + (t_s % 16 == 0))).astype(np.float32)
    dist = np.where(count > 0, t_s, 1e35).astype(np.float32)
    row, colm = np.arange(P)[:, None], np.arange(P)[None, :]
    eye = (row == colm).astype(np.float32)
    windows = np.repeat(np.array([[2, 8], [4, 16]], np.float32), 64, axis=0)
    inv_head = 1.0 / np.minimum(np.arange(1, 17, dtype=np.float32)[None, None, :], windows[:, :, None])
    slopes = np.array([2.0 ** (-8.0 * (h + 1) / HEADS) for h in range(HEADS)], np.float32)

    def state(v):
        return v.reshape(SSM_TILES, P).T

    def state_ch(v):
        return v.reshape(SSM_TILES, P, SSM_CH).transpose(1, 0, 2).reshape(P, -1)

    parts = {
        "c": _cols(lead["c"]), "b_ada": _cols(lead["b_ada"]), "g_mix": _cols(lead["g_mix"]),
        "g_ffn": _cols(lead["g_ffn"]), "g_final": _cols(a["g_final"]), "norm_g": _cols(a["norm_g_2"]),
        "b_gate": _cols(lead["b_gate"]), "d_skip": _cols(lead["d_skip"]), "b_glu": _cols(lead["b_glu"]),
        "w_conv": _cols(lead["w_conv"]), "b_conv": _cols(lead["b_conv"]), "conv_w2": _cols(a["conv_w_2"]),
        "pool_scale": _cols(a["pool_scale_2"]), "slopes": np.broadcast_to(slopes, (P, HEADS)),
        "a_re": state(lead["a_re"]), "a_im": state(lead["a_im"]), "log_dt": state(np.repeat(lead["log_dt"], 64)),
        "inv_head": inv_head.reshape(P, 32).astype(np.float32), "inv_w": (1.0 / windows).astype(np.float32),
        "b_re": state_ch(lead["b_re"]), "b_im": state_ch(lead["b_im"]),
        "c_re": state_ch(lead["c_re"].transpose(0, 2, 1)), "c_im": state_ch(lead["c_im"].transpose(0, 2, 1)),
    }
    out["cols"] = np.concatenate([parts[n] for n in COLS], axis=1)
    tabs = {
        "ident": eye, "after": (row > colm).astype(np.float32), "ones": np.ones((P, P), np.float32),
        "strict": (colm > row).astype(np.float32), "dist": dist, "count": count,
        "w_glu": lead["w_glu"].reshape(2, P, 256).transpose(1, 0, 2).reshape(P, 512),
        "pool_w": a["pool_w_2"].reshape(2, 2, P, 64).transpose(2, 0, 1, 3).reshape(P, 256),
    }
    out["tabs"] = np.concatenate([tabs[n] for n in TABS], axis=1)
    w_ada = lead["w_ada"].reshape(DC, P, 6 * D)
    out["w_ada"] = w_ada[:, :, :2 * D]
    rest = w_ada[:, :, 3 * D:].reshape(DC, P, 3, D).transpose(0, 2, 1, 3).reshape(3 * DC, P, D)
    out["w_ada_rows"] = np.concatenate([w_ada[:, :, 2 * D:3 * D], rest])

    w_in = _tiles(lead["w_in"])
    q0, k0, v0, us0, g0 = 0, 4, 8, 12, 14
    order = [us0, us0 + 1]
    for j in range(HEAD_PAIRS):
        order += [q0 + j, k0 + j, v0 + j, g0 + 3 * j, g0 + 3 * j + 1, g0 + 3 * j + 2]
    order += [g0 + n for n in range(12, 16)]
    out["w_in"] = w_in[order]
    out["w_merge"] = np.concatenate([_tiles(lead["w_proj_ssm"]), _tiles(lead["w_proj_att"])], axis=2)
    out["w_out"] = _tiles(lead["w_out"])
    up = _tiles(lead["w_up"]).reshape(2, 16, P, D)
    out["w_up"] = up.transpose(1, 0, 2, 3).reshape(32, P, D)
    out["w_down"] = np.concatenate([_tiles(w) for w in lead["w_down"].reshape(2, D, D)])

    gu, dn, in2, out2 = [], [], [], []
    for l in range(LAYERS):
        for s in range(2):
            pair = np.stack([_tiles(a["ffn_w_gate_2"][l, s]), _tiles(a["ffn_w_up_2"][l, s])], axis=1)
            gu.append(pair.reshape(4 * HALF2, P, D))
            dn += [_tiles(w) for w in a["ffn_w_down_2"][l, s].reshape(2, RING, D)]
        w = _tiles(a["w_in_2"][l])
        q0, k0, v0, gb, gc, ch, pl = 0, 4, 8, 12, 14, 16, 18
        extra = [pl, pl + 1, ch, ch + 1, gc, gc + 1, gb, gb + 1]
        order = []
        for j in range(HEAD_PAIRS):
            order += [q0 + j, k0 + j, v0 + j, extra[j]]
        in2.append(w[order + extra[4:]])
        out2.append(_tiles(a["w_out_2"][l]))
    out["w_gate_up"], out["w_down2"] = np.concatenate(gu), np.concatenate(dn)
    out["w_in2"], out["w_out2"] = np.concatenate(in2), np.concatenate(out2)
    return {k: np.ascontiguousarray(v) for k, v in out.items()}


def kernel(**inputs):
    import numpy as np
    import concourse.bacc as bacc
    from concourse.bass_utils import run_bass_kernel_spmd

    arrays = _layout({k: np.asarray(v) for k, v in inputs.items()})
    nc = bacc.Bacc("TRN2", target_bir_lowering=False, num_devices=1, dynamic_dma_scratch_size=256)
    d = {k: nc.dram_tensor(f"in_{k}", v.shape, F32, kind="ExternalInput").ap() for k, v in arrays.items()}
    d["out"] = nc.dram_tensor("out", (DC, P, T), F32, kind="ExternalOutput").ap()
    program(nc, d)
    r = run_bass_kernel_spmd(nc, [{f"in_{k}": v for k, v in arrays.items()}], core_ids=[0])
    return np.ascontiguousarray(r.results[0]["out"].reshape(D, T).T)[None]
```

```python
from contextlib import ExitStack

import concourse.bass as bass
from concourse import mybir

F32 = mybir.dt.float32
F32R = mybir.dt.float32r
BF16 = mybir.dt.bfloat16
ALU = mybir.AluOpType
ACT = mybir.ActivationFunctionType

P = 128
T = 512
D = 1024
DC = D // P
EPS = 1e-6
HEADS, HD = 8, 64
HEAD_PAIRS = HEADS // 2
TB = T // P
ATT_SCALE = HD ** -0.5
LAYERS = 2
SSM_TILES = 8
SSM_CH = 16
HALF1 = 8
HALF2 = 11
RING = HALF2 * P

IN1, MERGE1, OUT1 = 0, 15, 19
FFN1 = 23
FFN1_HALF = HALF1 + DC // 2
LAYER0 = FFN1 + 2 * FFN1_HALF
FFN2_HALF = HALF2 + DC // 2
MIX2 = 2 * FFN2_HALF
MIX2_IN = 10
PAIRS_PER_LAYER = 2 * MIX2 + MIX2_IN + DC // 2

COLS = {}
_at = 0
for _name, _n in (("c", 8), ("b_ada", 48), ("g_mix", 8), ("g_ffn", 8), ("g_final", 8), ("norm_g", 96),
                  ("b_gate", 16), ("d_skip", 2), ("b_glu", 2), ("w_conv", 48), ("b_conv", 16),
                  ("conv_w2", 12), ("pool_scale", 4), ("slopes", 8), ("a_re", 8), ("a_im", 8), ("log_dt", 8),
                  ("inv_head", 32), ("inv_w", 2),
                  ("b_re", 128), ("b_im", 128), ("c_re", 128), ("c_im", 128)):
    COLS[_name] = (_at, _n)
    _at += _n
N_COLS = _at
TABS = {}
_at = 0
for _name, _n in (("ident", 128), ("after", 128), ("ones", 128), ("strict", 128), ("dist", 512), ("count", 512),
                  ("w_glu", 512), ("pool_w", 256)):
    TABS[_name] = (_at, _n)
    _at += _n
N_TABS = _at
HEADS1_STEPS, CONV_STEPS, HEADS2_STEPS = 2 * 7 + 2 + 8, 2, 10
LAYER_STEPS = 3 + 3 * 9 + 2 + HEAD_PAIRS * HEADS2_STEPS + 1 + 7 + 9 + 8

TWO_PI_1, TWO_PI_2, TWO_PI_3 = 6.28125, 0.0019350051879882812, 3.0199159819567e-07
INV_TWO_PI = 0.15915494309189535
ROUND_MAGIC = 12582912.0
PI_SAFE, HALF_PI = 3.1415925, 1.5707963267948966


class Steps:

    def __init__(self, eng, sem):
        self.eng, self.sem, self.at, self.calls = eng, sem, 0, 0

    def __call__(self, ins):
        ins.then_inc(self.sem, 1)
        self.at = self.at + 1
        self.calls += 1
        self.eng.wait_ge(self.sem, self.at)

    def enter(self, i, per_turn):
        start = self.at
        self.at = i * per_turn + start
        return start


def program(nc, d):
    ctx = ExitStack()
    with ctx:
        def sb(name, shape, dt=F32):
            return ctx.enter_context(nc.sbuf_tensor(name, shape, dt))

        def sem(name):
            return ctx.enter_context(nc.semaphore(name))

        cols = sb("cols", [P, N_COLS])
        tabs = sb("tabs", [P, N_TABS])
        x = sb("x", [P, DC, T])
        u_hi = sb("u_hi", [P, DC, T], F32R)
        u_lo = sb("u_lo", [P, DC, T], F32R)
        h_at = nc.sbuf_base
        h_hi = sb("h_hi", [P, HALF2, T], F32R)
        h_lo = sb("h_lo", [P, HALF2 + 1, T], F32R)
        f = sb("f", [P, DC, T])
        raw = sb("raw", [P, 2, RING])
        w_hi = sb("w_hi", [P, 2, RING], F32R)
        w_lo = sb("w_lo", [P, 2, RING], F32R)
        arena = sb("arena", [P, 26 * T])
        rstd = sb("rstd", [P, T])
        mod = sb("mod", [P, 48])
        amp = sb("amp", [P, 16])
        c_act = sb("c_act", [P, 8])
        half_g = sb("half_g", [P, 96])
        eps = sb("eps", [P, 1])
        mask_b = sb("mask_b", [P, P], BF16)
        stat = sb("stat", [P, 32])
        us = sb("us", [P, 2, T])
        B_t = sb("B_t", [P, 4, P])
        C_t = sb("C_t", [P, 2, SSM_TILES, 32])
        co = sb("co", [P, 26, 8])
        E1 = sb("E1", [P, 2, SSM_TILES, 16])
        E16 = sb("E16", [P, 2, SSM_TILES, 32])
        pool_w = sb("pool_w", [P, 2, P])

        def slot(n, k=1):
            return arena[:, n * T:(n + k) * T]

        def slots(n, k):
            return slot(n, k).rearrange("p (c t) -> p c t", t=T)

        gates = slots(0, 16)
        sq, acc, std, ux = slots(0, 2), slot(2), slot(3), slots(4, 2)
        ffn_g, ffn_s, ffn_u, ffn_h = slot(6), slot(7), slot(8), slot(9)
        a_pad = arena[:, 10 * T:10 * T + T + 2]
        q_st, k_st, vT_st = slot(16), slot(17), slot(18)
        v_nat = slots(19, 1)[:, 0, :].rearrange("p (i d) -> p i d", d=P)
        nsc, bias_h = slots(20, 2), slot(25)
        pt_all = arena[:, 22 * T:24 * T + 2 * P]
        kept, own = slots(0, 4), slots(4, 4)
        pooled = slots(23, 2)
        a_keys, softp = slots(8, 4), slots(12, 4)
        padded = arena[:, 20 * T:20 * T + 2 * (T + 16)].rearrange("p (a t) -> p a t", a=2)
        cx = slots(12, 4)
        gelu_y, glu_s, ssm_y = slots(16, 2), slots(18, 2), slots(20, 2)
        ssm_tmp = nc.alloc_sbuf_tensor_at("ssm_tmp", [P, 7, T], F32, offset=h_at)
        bu_im = nc.alloc_sbuf_tensor_at("bu_im", [P, SSM_TILES, T], F32, offset=h_at + 15 * T * 4)
        ada_acc = nc.alloc_sbuf_tensor_at("ada_acc", [P, 2 * D], F32, offset=h_at)
        ada_w = nc.alloc_sbuf_tensor_at("ada_w", [P, 4, 2 * D], F32, offset=h_at + 2 * D * 4)
        bu_re = f
        ada_rows = f.rearrange("p (n c) t -> p n (c t)", c=2)
        ada_sums = nc.alloc_sbuf_tensor_at("ada_sums", [P, 3 * D], F32, offset=h_at + (HALF2 + 6) * T * 4)
        gate_sum = slot(20, 2)
        banks = [ctx.enter_context(nc.psum_tensor(n, [P, T], F32)) for n in
                 ("unit_bank0", "unit_bank1", "stat_bank", "score0", "score1", "mix0", "mix1", "out_bank")]
        unit_bank, stat_bank, score, mix, out_bank = banks[0:2], banks[2], banks[3:5], banks[5:7], banks[7]
        z_bank = banks[3:7]

        consts_loaded = sem("consts_loaded")
        x_loaded = sem("x_loaded")
        ada_loaded = [sem(f"ada_loaded{i}") for i in range(4)]
        ada_rows_loaded = [sem(f"ada_rows_loaded{i}") for i in range(4)]
        raw_loaded = [sem(f"raw_loaded{i}") for i in range(2)]
        hi_ready = sem("hi_ready")
        lo_ready = sem("lo_ready")
        unit_done = sem("unit_done")
        taken = [sem(f"taken{i}") for i in range(2)]
        cact_ready = sem("cact_ready")
        ada_used = sem("ada_used")
        mod_sum = sem("mod_sum")
        mod_ready = sem("mod_ready")
        prep_ready = sem("prep_ready")
        sq_ready = sem("sq_ready")
        sq_used = sem("sq_used")
        norm_sum = sem("norm_sum")
        fsq_ready = sem("fsq_ready")
        fsq_added = sem("fsq_added")
        fsum_ready = sem("fsum_ready")
        std_ready = sem("std_ready")
        ux_ready = sem("ux_ready")
        uhi_ready = sem("uhi_ready")
        u_ready = sem("u_ready")
        x_ready = sem("x_ready")
        conv_ready = sem("conv_ready")
        silu_ready = sem("silu_ready")
        hidden_ready = sem("hidden_ready")
        hhi_ready = sem("hhi_ready")
        h_ready = sem("h_ready")
        ssm_act, ssm_vec = sem("ssm_act"), sem("ssm_vec")
        B_padded, B_turned, B_ready = sem("B_padded"), sem("B_turned"), sem("B_ready")
        bu_done, bu_ready = sem("bu_done"), sem("bu_ready")
        scan_ready = sem("scan_ready")
        y_done, y_ready, gelu_ready, glu_done, glu_ready, yy_ready, yhi_ready, y_split = (
            sem(n) for n in ("y_done", "y_ready", "gelu_ready", "glu_done", "glu_ready", "yy_ready",
                             "yhi_ready", "y_split"))
        v_turned, v_ready = sem("v_turned"), sem("v_ready")
        s_done, s_biased, p_ready, p_weighted, p_scaled, p_turned, pT_ready, pv_done = (
            sem(n) for n in ("s_done", "s_biased", "p_ready", "p_weighted", "p_scaled", "p_turned",
                             "pT_ready", "pv_done"))
        ohi_ready, o_taken = sem("ohi_ready"), sem("o_taken")
        sig_ready, merged_ready, mhi_ready, m_ready = (
            sem(n) for n in ("sig_ready", "merged_ready", "mhi_ready", "m_ready"))
        v2_turned, v2_ready = sem("v2_turned"), sem("v2_ready")
        sums_taken = sem("sums_taken")
        z_done, softp_ready, sp_ready, R_done, a_ready, pv2_done, ohi2_ready, o2_taken = (
            sem(n) for n in ("z_done", "softp_ready", "sp_ready", "R_done", "a_ready", "pv2_done",
                             "ohi2_ready", "o2_taken"))
        pool_in, pool_done, phi_ready, conv2_ready, chi_ready, cat_ready = (
            sem(n) for n in ("pool_in", "pool_done", "phi_ready", "conv2_ready", "chi_ready", "cat_ready"))
        vec_step, act_step = sem("vec_step"), sem("act_step")
        vec_passed = sem("vec_passed")
        out_stored = sem("out_stored")

        def col(name, i=0, n=1):
            return cols[:, bass.ds(COLS[name][0] + i, n)]

        def tab(name, a=0, b=None):
            at, n = TABS[name]
            return tabs[:, at + a:at + (n if b is None else b)]

        def as32(ap):
            return ap.bitcast(F32)

        def in_pair(j, n):
            return IN1 + 1 + 3 * j + n

        def layer(l):
            return LAYER0 + PAIRS_PER_LAYER * l

        def ffn2(l, s):
            return layer(l) + s * (MIX2 + MIX2_IN + DC // 2)

        def pT(b):
            return pt_all[:, P * b * (b + 1) // 2:P * (b + 1) * (b + 2) // 2].rearrange("p (i t) -> p i t", t=P)

        CONSTS = 32
        block = ctx.enter_context(nc.Block())

        @block.sync
        def _(e):
            e.dma_start(cols[:], d["cols"]).then_inc(consts_loaded, 16)
            e.dma_start(tabs[:], d["tabs"]).then_inc(consts_loaded, 16)

            def load(p, s, src, n):
                if not isinstance(p, int) or p > 0:
                    e.wait_ge(lo_ready, 2 * p + s - 1)
                e.dma_start(raw[:, s, 0:n], src).then_inc(raw_loaded[s], 16)

            def load_pairs(p0, w, first, pairs):
                n = w.shape[2]
                with e.Fori(0, pairs) as i:
                    for s in range(2):
                        load(p0 + i, s, w[bass.ds(first + 2 * i + s, 1), :, :].rearrange("a p n -> p (a n)"), n)

            for k in range(DC):
                if k >= 4:
                    e.wait_ge(ada_used, k - 3)
                e.dma_start(ada_w[:, k % 4, :], d["w_ada"][k]).then_inc(ada_loaded[k % 4], 16)
                if k == 1:
                    e.dma_start(x[:], d["x"]).then_inc(x_loaded, 16)
                if k == 3:
                    for s in range(2):
                        load(0, s, d["w_in"][s], D)
            load_pairs(1, d["w_in"], 2, MERGE1 - 1)

            def load_rows(a):
                if a >= 4:
                    e.wait_ge(ada_used, DC + a - 3)
                else:
                    e.wait_ge(y_done, SSM_TILES)
                e.dma_start(ada_rows[:, a % 4, :], d["w_ada_rows"][a]).then_inc(ada_rows_loaded[a % 4], 16)

            rows = [[u] for u in range(DC)] + [[DC + 3 * u + m for m in range(3)] for u in range(DC)]
            for u in range(2 * DC):
                w, p = (d["w_merge"], MERGE1) if u < DC else (d["w_out"], OUT1)
                load(p + u % DC // 2, u % 2, w[u % DC], w.shape[2])
                if u >= 2:
                    for a in rows[u - 2]:
                        load_rows(a)
            for a in rows[-2] + rows[-1]:
                load_rows(a)
            for half in range(2):
                load_pairs(FFN1 + half * FFN1_HALF, d["w_up"], 2 * HALF1 * half, HALF1)
                load_pairs(FFN1 + half * FFN1_HALF + HALF1, d["w_down"], DC * half, DC // 2)
            with e.Fori(0, LAYERS) as l:
                for s in range(2):
                    for half in range(2):
                        n = 2 * (2 * l + s) + half
                        load_pairs(ffn2(l, s) + half * FFN2_HALF, d["w_gate_up"], 2 * HALF2 * n, HALF2)
                        load_pairs(ffn2(l, s) + half * FFN2_HALF + HALF2, d["w_down2"], DC * n, DC // 2)
                    if s == 0:
                        load_pairs(layer(l) + MIX2, d["w_in2"], 2 * MIX2_IN * l, MIX2_IN)
                        load_pairs(layer(l) + MIX2 + MIX2_IN, d["w_out2"], DC * l, DC // 2)
            for c in range(DC):
                e.wait_ge(x_ready, DC * 3 * LAYERS + c + 1)
                e.dma_start(d["out"][c], x[:, c, :]).then_inc(out_stored, 16)
            e.wait_ge(out_stored, 16 * DC)

        @block.gpsimd
        def _(e):
            def split_pair(p, n):
                for s in range(2):
                    e.wait_ge(hi_ready, 2 * p + s + 1)
                    e.tensor_tensor(w_lo[:, s, 0:n], raw[:, s, 0:n], as32(w_hi[:, s, 0:n]),
                                    ALU.subtract).then_inc(lo_ready, 1)

            def split_pairs(p0, pairs, n):
                with e.Fori(0, pairs) as i:
                    split_pair(p0 + i, n)

            def add_squares(q):
                for c in range(1, DC):
                    e.wait_ge(sq_ready, DC * q + c + 1)
                    if c == 1:
                        e.tensor_tensor(acc, sq[:, 0, :], sq[:, 1, :], ALU.add).then_inc(sq_used, 2)
                    else:
                        e.wait_ge(sq_used, DC * q + c)
                        e.tensor_tensor(acc, acc, sq[:, c % 2, :], ALU.add).then_inc(sq_used, 1)

            split_pairs(IN1, MERGE1 - IN1, D)
            split_pairs(MERGE1, DC // 2, 6 * P)
            split_pairs(OUT1, LAYER0 - OUT1, D)
            with e.Fori(0, LAYERS) as l:
                for s in range(2):
                    for half in range(2):
                        if half == 0:
                            split_pair(ffn2(l, s), D)
                            add_squares(3 + 3 * l + 2 * s)
                        split_pairs(ffn2(l, s) + half * FFN2_HALF + 1 - half, HALF2 - 1 + half, D)
                        split_pairs(ffn2(l, s) + half * FFN2_HALF + HALF2, DC // 2, RING)
                    if s == 0:
                        split_pair(layer(l) + MIX2, D)
                        add_squares(4 + 3 * l)
                        split_pairs(layer(l) + MIX2 + 1, MIX2_IN + DC // 2 - 1, D)

        @block.tensor
        def _(e):
            def unit(p, s, hi, lo, ks, bank=None, first=0, before=None, signal=True, free=1):
                bank = unit_bank[s] if bank is None else bank
                if signal is True or signal == "first":
                    e.wait_ge(lo_ready, 2 * p + s + 1)
                    e.wait_ge(taken[s], p + free)
                for n, k in enumerate(ks):
                    if before:
                        before(n)
                    wh = w_hi[:, s, (first + n) * P:(first + n + 1) * P]
                    wl = w_lo[:, s, (first + n) * P:(first + n + 1) * P]
                    last = n == len(ks) - 1
                    e.matmul(bank[:], wh, hi(k), start=n == 0, stop=False)
                    e.matmul(bank[:], wh, lo(k), start=False, stop=False)
                    mm = e.matmul(bank[:], wl, hi(k), start=False, stop=last)
                if signal is True or signal == "last":
                    mm.then_inc(unit_done, 1)

            def from_u(k):
                return u_hi[:, k, :]

            def from_u_lo(k):
                return u_lo[:, k, :]

            def from_h(k):
                return h_hi[:, k, :]

            def from_h_lo(k):
                return h_lo[:, k, :]

            EIGHT = range(DC)

            def in_unit(p, s, free=1):
                unit(p, s, from_u, from_u_lo, EIGHT, free=free)

            def add_square(q, c):
                e.wait_ge(sq_ready, DC * q + c + 1)
                e.matmul(stat_bank[:], tab("ones"), sq[:, c % 2, :], start=c == 0,
                         stop=c == DC - 1).then_inc(sq_used, 1)

            def first_pair(p, n, q=None, into=unit_bank):
                e.wait_ge(lo_ready, 2 * p + 2)
                for s in range(2):
                    e.wait_ge(taken[s], p + 1)
                for c in EIGHT:
                    e.wait_ge(u_ready, DC * n + c + 1)
                    for s in range(2):
                        wh, wl = w_hi[:, s, c * P:(c + 1) * P], w_lo[:, s, c * P:(c + 1) * P]
                        e.matmul(into[s][:], wh, u_hi[:, c, :], start=c == 0, stop=False)
                        e.matmul(into[s][:], wh, u_lo[:, c, :], start=False, stop=False)
                        mm = e.matmul(into[s][:], wl, u_hi[:, c, :], start=False, stop=c == DC - 1)
                        if c == DC - 1:
                            mm.then_inc(unit_done, 1)
                if q is not None:
                    e.wait_ge(sq_used, DC * q + DC)
                    e.matmul(stat_bank[:], tab("ones"), acc, start=True, stop=True).then_inc(norm_sum, 1)

            def h_chunk(h0):
                return lambda c: e.wait_ge(h_ready, h0 + c + 1)

            def down(p0, h0, n_k):
                with e.Fori(0, DC // 2) as i:
                    unit(p0 + i, 0, from_h, from_h_lo, range(n_k), before=h_chunk(h0))
                    unit(p0 + i, 1, from_h, from_h_lo, range(n_k))

            def f_sum(r):
                e.wait_ge(fsq_added, (DC + 1) * (r + 1))
                e.matmul(stat_bank[:], tab("ones"), acc, start=True, stop=True).then_inc(fsum_ready, 1)

            def turn_v(free, free_at, src_sem, src_at, done):
                e.wait_ge(free, free_at)
                e.wait_ge(src_sem, src_at)
                for i in range(TB):
                    mm = e.transpose(out_bank[:, i * P:(i + 1) * P], vT_st[:, i * P:(i + 1) * P], tab("ident"))
                mm.then_inc(done, 1)

            def mixer2(l):
                pm = layer(l) + MIX2

                def head_pair(j):
                    J = HEAD_PAIRS * l + j

                    def z(h):
                        if h == 0:
                            for s in range(2):
                                e.wait_ge(taken[s], pm + 2 * j + 2)
                        rows = slice(HD * h, HD * h + HD)
                        for n in range(TB):
                            i = TB - 1 - n
                            e.wait_ge(sums_taken, 8 * J + TB * h + n + 1)
                            e.matmul(z_bank[i][:, 0:T - i * P], k_st[rows, i * P:(i + 1) * P], q_st[rows, i * P:T],
                                     start=True, stop=True).then_inc(z_done, 1)

                    def keep_sums(h):
                        for n in range(TB):
                            i = TB - 1 - n
                            e.wait_ge(sp_ready, 8 * J + TB * h + n + 1)
                            R = z_bank[i]
                            mm = e.matmul(R[:, 0:T - i * P], tab("after"), kept[:, i, 0:T - i * P], start=True,
                                          stop=n == 0)
                            for m in range(i + 1, TB):
                                mm = e.matmul(R[:, (m - i) * P:T - i * P], tab("ones"), kept[:, m, 0:T - m * P],
                                              start=False, stop=m == TB - 1)
                            mm.then_inc(R_done, 1)

                    def values(h):
                        if h == 0:
                            e.wait_ge(v2_ready, J + 1)
                        e.wait_ge(a_ready, 8 * J + TB * (h + 1))
                        rows = slice(HD * h, HD * h + HD)
                        for i in range(TB):
                            mm = e.matmul(out_bank[rows, i * P:T], v_nat[:, i, rows], a_keys[:, i, 0:T - i * P],
                                          start=i == 0, stop=i == TB - 1)
                        mm.then_inc(pv2_done, 1)

                    z(0)
                    in_unit(pm + 2 * j + 1, 1)
                    keep_sums(0)
                    turn_v(o2_taken, J + 1, taken[0], pm + 2 * j + 3, v2_turned)
                    z(1)
                    values(0)
                    in_unit(pm + 2 * j + 2, 0)
                    keep_sums(1)
                    in_unit(pm + 2 * j + 2, 1)
                    in_unit(pm + 2 * j + 3, 0)
                    values(1)

                first_pair(pm, 3 + 3 * l, 4 + 3 * l, score)
                in_unit(pm + 1, 0, free=0)
                with e.Fori(0, HEAD_PAIRS) as j:
                    head_pair(j)
                in_unit(pm + 2 * HEAD_PAIRS + 1, 1)
                for m in range(2):
                    e.wait_ge(pool_in, 2 * l + m + 1)
                    e.matmul(score[m][:], pool_w[:, m, :], pooled[:, m, :], start=True, stop=True).then_inc(pool_done, 1)
                def cat_chunk(c):
                    if c < HEAD_PAIRS:
                        e.wait_ge(o2_taken, HEAD_PAIRS * l + c + 2)
                    else:
                        e.wait_ge(cat_ready, 4 * l + (3, 4, 1, 2)[c - HEAD_PAIRS])

                with e.Fori(0, DC // 2) as i:
                    unit(pm + MIX2_IN + i, 0, from_h, from_h_lo, EIGHT,
                         before=cat_chunk)
                    unit(pm + MIX2_IN + i, 1, from_h, from_h_lo, EIGHT)
                f_sum(3 * l + 1)

            e.wait_ge(consts_loaded, CONSTS)
            for c in EIGHT:
                add_square(0, c)
            e.wait_ge(ada_used, DC)
            for c in range(16):
                mm = e.matmul(out_bank[:, c:c + 1], ada_acc[:, c * P:(c + 1) * P], tab("ones", 0, 1),
                              start=True, stop=True)
            mm.then_inc(mod_sum, 1)

            def sum_rows(n, src, at):
                e.wait_ge(ada_used, at)
                for c in range(DC):
                    mm = e.matmul(out_bank[:, DC * n + c:DC * n + c + 1], src[:, c * P:(c + 1) * P],
                                  tab("ones", 0, 1), start=True, stop=True)
                mm.then_inc(mod_sum, 1)

            first_pair(IN1, 0)
            e.wait_ge(B_padded, 1)
            for n in range(4):
                mm = e.transpose(out_bank[:, n * P:(n + 1) * P], slot(22, 1)[:, n * P:(n + 1) * P], tab("ident"))
            mm.then_inc(B_turned, 1)
            in_unit(in_pair(0, 0), 0)
            e.wait_ge(B_ready, 1)
            for s in range(2):
                e.wait_ge(taken[s], 2)
            for i in range(SSM_TILES):
                rows = slice(32 * (i % 4), 32 * (i % 4) + 32)
                for part in range(2):
                    n = 2 * i + part
                    if n >= 2:
                        e.wait_ge(bu_ready, n - 1)
                    e.matmul(score[part][:], B_t[rows, 2 * part + i // 4, :], us[rows, i // 4, :],
                             start=True, stop=True).then_inc(bu_done, 1)

            with e.Fori(0, HEAD_PAIRS) as j:
                def scores(n):
                    h, b = divmod(n, TB)
                    if n == 0:
                        for s in range(2):
                            e.wait_ge(taken[s], in_pair(j, 0) + 2)
                    if n >= 2:
                        e.wait_ge(s_biased, 8 * j + n - 1)
                    rows = slice(HD * h, HD * h + HD)
                    e.matmul(score[n % 2][:, 0:(b + 1) * P], q_st[rows, b * P:(b + 1) * P],
                             k_st[rows, 0:(b + 1) * P], start=True, stop=True).then_inc(s_done, 1)

                def turn_probs(n):
                    e.wait_ge(p_scaled, 8 * j + n + 1)
                    if n >= 2:
                        e.wait_ge(pT_ready, 8 * j + n - 1)
                    for i in range(n % TB + 1):
                        mm = e.transpose(mix[n % 2][:, i * P:(i + 1) * P], nsc[:, n % 2, i * P:(i + 1) * P],
                                         tab("ident"))
                    mm.then_inc(p_turned, 1)

                def values(h):
                    e.wait_ge(v_ready, j + 1)
                    e.wait_ge(pT_ready, 8 * j + TB * (h + 1))
                    rows = slice(HD * h, HD * h + HD)
                    for b in range(TB):
                        for i in range(b + 1):
                            mm = e.matmul(out_bank[rows, b * P:(b + 1) * P], v_nat[:, i, rows], pT(b)[:, i, :],
                                          start=i == 0, stop=i == b)
                    mm.then_inc(pv_done, 1)

                in_unit(in_pair(j, 0), 1)
                in_unit(in_pair(j, 1), 0)
                scores(0)
                scores(1)
                turn_v(o_taken, j + 1, taken[0], in_pair(j, 1) + 2, v_turned)
                for n, (p, s) in enumerate(((1, 1), (2, 0), (2, 1), (3, 0))):
                    in_unit(in_pair(j, p), s)
                    if n == 2:
                        values(0)
                    for m in (2 * n, 2 * n + 1):
                        turn_probs(m)
                        if m + 2 < 2 * TB:
                            scores(m + 2)
                values(1)
            e.wait_ge(scan_ready, SSM_TILES)
            for i in range(SSM_TILES):
                rows = slice(32 * (i % 4), 32 * (i % 4) + 32)
                e.matmul(mix[i // 4][rows, :], C_t[:, 0, i, :], bu_re[:, i, :], start=True, stop=False)
                e.matmul(mix[i // 4][rows, :], C_t[:, 1, i, :], bu_im[:, i, :], start=False,
                         stop=True).then_inc(y_done, 1)
            in_unit(in_pair(HEAD_PAIRS, 0), 1)
            e.wait_ge(gelu_ready, 2)
            for m in range(2):
                for k in range(2):
                    mm = e.matmul(score[m][:], tab("w_glu", 256 * k + P * m, 256 * k + P * m + P),
                                  gelu_y[:, k, :], start=k == 0, stop=k == 1)
                mm.then_inc(glu_done, 1)
            for s in range(2):
                in_unit(in_pair(HEAD_PAIRS, 1), s)
            e.wait_ge(y_split, 2)
            e.wait_ge(o_taken, HEAD_PAIRS + 1)
            with e.Fori(0, DC // 2) as i:
                for s in range(2):
                    p = MERGE1 + i
                    unit(p, s, lambda k: h_hi[:, 5 + k, :], lambda k: h_lo[:, 4 + k, :], range(2),
                         bank=score[s], signal="first")
                    unit(p, s, lambda k: h_hi[:, 7 + k, :], lambda k: h_lo[:, k, :], range(4), first=2,
                         signal="last")
            sum_rows(0, gate_sum, 2 * DC)
            def unit_and_square(q, c, *how, **more):
                unit(*how, **more)
                if c >= 2:
                    add_square(q, c - 2)

            for c in EIGHT:
                unit_and_square(1, c, OUT1 + c // 2, c % 2, from_u, from_u_lo, EIGHT,
                                before=(lambda k: e.wait_ge(m_ready, k + 1)) if c == 0 else None)
            for c in (DC - 2, DC - 1):
                add_square(1, c)

            for n in (1, 2):
                sum_rows(n, ada_sums[:, (n - 1) * D:n * D], 5 * DC)
            for half in range(2):
                p0 = FFN1 + half * FFN1_HALF
                if half == 0:
                    first_pair(p0, 1)
                    sum_rows(3, ada_sums[:, 2 * D:3 * D], 5 * DC)
                with e.Fori(1 - half, HALF1) as i:
                    in_unit(p0 + i, 0)
                    in_unit(p0 + i, 1)
                if half == 0:
                    down(p0 + HALF1, 0, HALF1)
            for c in EIGHT:
                unit_and_square(2, c, p0 + HALF1 + c // 2, c % 2, from_h, from_h_lo, range(HALF1),
                                before=h_chunk(HALF1) if c == 0 else None)
            for c in (DC - 2, DC - 1):
                add_square(2, c)

            with e.Fori(0, LAYERS) as l:
                for s_ffn in range(2):
                    k_norm = 2 * s_ffn
                    for half in range(2):
                        p0 = ffn2(l, s_ffn) + half * FFN2_HALF
                        if half == 0:
                            first_pair(p0, 2 + 3 * l + k_norm, 3 + 3 * l + k_norm, score)
                            in_unit(p0 + 1, 0, free=0)
                            in_unit(p0 + 1, 1, free=0)
                        with e.Fori(2 - 2 * half, HALF2) as i:
                            in_unit(p0 + i, 0)
                            in_unit(p0 + i, 1)
                        down(p0 + HALF2, 16 + 44 * l + 22 * s_ffn + HALF2 * half, HALF2)
                    f_sum(3 * l + k_norm)
                    if s_ffn == 0:
                        mixer2(l)


        @block.scalar
        def _(e):
            def settled():
                e.wait_ge(consts_loaded, CONSTS)

            def refill(p, s, n=D):
                if not isinstance(p, int) or p > 0:
                    e.wait_ge(unit_done, 2 * p + s - 1)
                e.wait_ge(raw_loaded[s], 16 * p + 16)
                e.activation(w_hi[:, s, 0:n], raw[:, s, 0:n], ACT.Copy).then_inc(hi_ready, 1)

            def square(q, c):
                if not (isinstance(q, int) and DC * q + c < 2):
                    e.wait_ge(sq_used, DC * q + c - 1)
                e.activation(sq[:, c % 2, :], x[:, c, :], ACT.Square).then_inc(sq_ready, 1)

            def root():
                e.activation(std, stat_bank[:], ACT.Sqrt, bias=eps[:], scale=1.0 / D).then_inc(std_ready, 1)

            def shifted(n, shift):
                e.wait_ge(mod_ready, n + 1)
                for c in range(DC):
                    e.wait_ge(ux_ready, DC * n + c + 1)
                    e.activation(u_hi[:, c, :], ux[:, c % 2, :], ACT.Identity,
                                 bias=mod[:, shift + c:shift + c + 1]).then_inc(uhi_ready, 1)

            e.wait_ge(consts_loaded, CONSTS)
            e.activation(c_act[:], col("c", 0, 8), ACT.Silu).then_inc(cact_ready, 1)
            e.activation(co[:, 0, :], col("log_dt", 0, 8), ACT.Exp).then_inc(ssm_act, 1)
            e.wait_ge(ssm_vec, 1)
            e.activation(co[:, 3, :], co[:, 1, :], ACT.Exp)
            e.activation(co[:, 7, :], co[:, 5, :], ACT.Sin)
            e.activation(co[:, 8, :], co[:, 6, :], ACT.Sin).then_inc(ssm_act, 1)

            e.wait_ge(x_loaded, 16)
            e.wait_ge(prep_ready, 1)
            for c in range(DC):
                square(0, c)
            for s in range(2):
                refill(0, s)
            e.wait_ge(sq_used, DC)
            root()
            shifted(0, 0)
            for s in range(2):
                refill(IN1 + 1, s)
                e.activation(us[:, s, :], unit_bank[s][:], ACT.Copy).then_inc(taken[s], 1)

            def stage_q():
                e.activation(q_st, unit_bank[0][:], ACT.Copy, scale=-ATT_SCALE).then_inc(taken[0], 1)

            refill(in_pair(0, 1), 0)
            stage_q()
            for n in range(2 * SSM_TILES):
                e.wait_ge(bu_done, n + 1)
                e.activation((bu_re, bu_im)[n % 2][:, n // 2, :], score[n % 2][:], ACT.Copy).then_inc(bu_ready, 1)

            def gate(s, g):
                settled()
                e.activation(gates[:, bass.ds(g, 1), :].rearrange("p a t -> p (a t)"), unit_bank[s][:],
                             ACT.Identity, bias=col("b_gate", g)).then_inc(taken[s], 1)

            def heads(j, last):
                def exps(n):
                    W = (n % TB + 1) * P
                    e.wait_ge(s_biased, 8 * j + n + 1)
                    e.activation(nsc[:, n % 2, 0:W], nsc[:, n % 2, 0:W], ACT.Exp, bias=stat[:, n:n + 1],
                                 scale=-1.0).then_inc(p_ready, 1)

                def divide(n):
                    W = (n % TB + 1) * P
                    e.wait_ge(p_weighted, 8 * j + n + 1)
                    e.activation(nsc[:, n % 2, 0:W], nsc[:, n % 2, 0:W], ACT.Identity,
                                 scale=stat[:, 16 + n:17 + n]).then_inc(p_scaled, 1)

                refill(in_pair(j, 1), 1)
                e.activation(k_st, unit_bank[1][:], ACT.Copy).then_inc(taken[1], 1)
                refill(in_pair(j, 2), 0)
                e.activation(vT_st, unit_bank[0][:], ACT.Copy).then_inc(taken[0], 1)
                for n, (p, s) in enumerate(((2, 1), (3, 0), (3, 1), (4, 0))):
                    for m in (2 * n, 2 * n + 1):
                        exps(m)
                    for m in (2 * n, 2 * n + 1):
                        divide(m)
                    refill(in_pair(j, p), s)
                    if n < 3 or last:
                        gate(s if n < 3 else 0, 3 * j + n)
                    else:
                        stage_q()
                e.wait_ge(pv_done, 2 * j + 2)
                settled()
                e.activation(h_hi[:, bass.ds(7 + j, 1), :].rearrange("p a t -> p (a t)"), out_bank[:],
                             ACT.Copy).then_inc(ohi_ready, 1)

            with e.Fori(0, HEAD_PAIRS - 1) as j:
                heads(j, False)
            heads(HEAD_PAIRS - 1, True)
            for m in range(2):
                e.wait_ge(y_ready, m + 1)
                e.activation(gelu_y[:, m, :], ssm_y[:, m, :], ACT.Gelu_apprx_tanh).then_inc(gelu_ready, 1)
            refill(in_pair(HEAD_PAIRS, 1), 1)
            gate(1, 3 * HEAD_PAIRS + 1)
            for m in range(2):
                e.wait_ge(glu_done, m + 1)
                e.activation(glu_s[:, m, :], score[m][:], ACT.Sigmoid, bias=col("b_glu", m)).then_inc(glu_ready, 1)
            for m in range(2):
                e.wait_ge(yy_ready, m + 1)
                e.activation(h_hi[:, 5 + m, :], ssm_y[:, m, :], ACT.Copy).then_inc(yhi_ready, 1)
            for s in range(2):
                refill(MERGE1, s, 6 * P)
                gate(s, 3 * HEAD_PAIRS + 2 + s)
            by_branch = gates.rearrange("p (g c) t -> p g c t", g=2)

            def merge(i, n):
                for s in range(2):
                    g = by_branch[:, :, bass.ds(2 * i + s, 1), :].rearrange("p g a t -> p g (a t)")
                    settled()
                    e.activation(g, g, ACT.Sigmoid).then_inc(sig_ready, 1)
                for s in range(2):
                    refill(MERGE1 + i + 1, s, n)
                    e.wait_ge(merged_ready, 2 * i + s + 1)
                    settled()
                    e.activation(u_hi[:, bass.ds(2 * i + s, 1), :].rearrange("p a t -> p (a t)"),
                                 slot(22 + s), ACT.Copy).then_inc(mhi_ready, 1)

            with e.Fori(0, DC // 2 - 1) as i:
                merge(i, 6 * P)
            merge(DC // 2 - 1, D)
            def squares_along(q, p0, refills):
                for c in range(DC):
                    if c < refills:
                        refill(p0 + c // 2 + 1, c % 2)
                    if c:
                        e.wait_ge(taken[(c - 1) % 2], p0 + (c - 1) // 2 + 2)
                        square(q, c - 1)
                e.wait_ge(taken[1], p0 + DC // 2 + 1)
                square(q, DC - 1)

            squares_along(1, OUT1, DC)

            e.wait_ge(sq_used, 2 * DC)
            root()
            shifted(1, 24)
            for half in range(2):
                p0 = FFN1 + half * FFN1_HALF
                with e.Fori(0, HALF1) as i:
                    refill(p0 + i + 1, 0)
                    e.wait_ge(prep_ready, 2)
                    e.activation(a_pad[:, 2:T + 2], unit_bank[0][:], ACT.Copy).then_inc(taken[0], 1)
                    e.wait_ge(conv_ready, HALF1 * half + i + 1)
                    e.activation(ffn_s, ffn_u, ACT.Silu).then_inc(silu_ready, 1)
                    refill(p0 + i + 1, 1)
                    e.wait_ge(taken[1], p0 + i + 2)
                    settled()
                    e.activation(h_hi[:, bass.ds(i, 1), :].rearrange("p a t -> p (a t)"), ffn_h,
                                 ACT.Copy).then_inc(hhi_ready, 1)
                if half == 0:
                    with e.Fori(0, DC // 2) as i:
                        for s in range(2):
                            refill(p0 + HALF1 + i + 1, s)
            squares_along(2, p0 + HALF1, DC - 2)
            e.wait_ge(sq_used, 3 * DC)
            root()

            with e.Fori(0, LAYERS) as l:
                def pre_norm(k, p):
                    for c in range(DC):
                        e.wait_ge(x_ready, DC * (3 * l + k) + c + 1)
                        settled()
                        e.activation(u_hi[:, c, :], x[:, c, :], ACT.Identity,
                                     scale=col("norm_g", (6 * l + 2 * k) * DC + c)).then_inc(uhi_ready, 1)
                        square(3 + 3 * l + k, c)
                    for s in range(2):
                        refill(p + 1, s)
                    e.wait_ge(norm_sum, 3 * l + k + 1)
                    root()

                def f_squares(p, s, r, c):
                    e.wait_ge(taken[s], p + 2)
                    settled()
                    e.activation(sq[:, 0, :], f[:, bass.ds(c, 1), :].rearrange("p a t -> p (a t)"),
                                 ACT.Square).then_inc(fsq_ready, 1)

                def f_root(r):
                    e.wait_ge(fsum_ready, r + 1)
                    root()

                for s in range(2):
                    refill(layer(l), s)
                for s_ffn in range(2):
                    k_norm = 2 * s_ffn
                    pre_norm(k_norm, ffn2(l, s_ffn))
                    for half in range(2):
                        p0 = ffn2(l, s_ffn) + half * FFN2_HALF
                        h0 = 16 + 44 * l + 22 * s_ffn + HALF2 * half

                        def hidden(i, n, ahead=True):
                            if ahead:
                                refill(p0 + i + 1, 0, n)
                            e.wait_ge(taken[0], p0 + i + 2)
                            e.activation(ffn_s, ffn_g, ACT.Silu).then_inc(silu_ready, 1)
                            if ahead:
                                refill(p0 + i + 1, 1, n)
                            e.wait_ge(hidden_ready, h0 - 16 + i + 1)
                            settled()
                            e.activation(h_hi[:, bass.ds(i, 1), :].rearrange("p a t -> p (a t)"), ffn_h,
                                         ACT.Copy).then_inc(hhi_ready, 1)

                        def out(i, n, last=False):
                            p = p0 + HALF2 + i
                            for s in range(2):
                                if half == 1:
                                    f_squares(p, s, 3 * l + k_norm, 2 * i + s)
                                    if last and s == 1:
                                        f_root(3 * l + k_norm)
                                if n:
                                    refill(p + 1, s, n)

                        if half == 0:
                            hidden(0, D, False)
                        with e.Fori(1 - half, HALF2 - 1) as i:
                            hidden(i, D)
                        hidden(HALF2 - 1, RING)
                        with e.Fori(0, DC // 2 - 1) as i:
                            out(i, RING)
                        out(DC // 2 - 1, D if half == 0 or s_ffn == 0 else 0, True)
                    if s_ffn:
                        continue
                    pm = layer(l) + MIX2
                    pre_norm(1, pm)
                    e.preload_act_table_set("natural_log_exp_and_others")
                    refill(pm + 2, 0)
                    with e.Fori(0, HEAD_PAIRS) as j:
                        J = HEAD_PAIRS * l + j

                        def decay(h):
                            at = 16 * J + 2 * TB * h
                            for n in range(TB):
                                i = TB - 1 - n
                                e.wait_ge(z_done, 8 * J + TB * h + n + 1)
                                e.activation(softp[:, i, 0:T - i * P], z_bank[i][:, 0:T - i * P],
                                             ACT.Abs).then_inc(act_step, 1)
                            for n in range(TB):
                                az = softp[:, TB - 1 - n, 0:(n + 1) * P]
                                e.wait_ge(act_step, at + n + 1)
                                e.activation(az, az, ACT.Exp, scale=-1.0).then_inc(act_step, 1)

                        def logs(h):
                            at = 16 * J + 2 * TB * h + TB
                            for n in range(TB):
                                az = softp[:, TB - 1 - n, 0:(n + 1) * P]
                                e.wait_ge(act_step, at + n + 1)
                                e.activation(az, az, ACT.Ln, bias=1.0).then_inc(softp_ready, 1)

                        def weights(h):
                            if h == 1:
                                e.wait_ge(pv2_done, 2 * J + 1)
                            for n in range(TB):
                                i = TB - 1 - n
                                e.wait_ge(sums_taken, 8 * J + TB * (h + 1) + n + 1)
                                e.activation(a_keys[:, i, 0:T - i * P], own[:, i, 0:T - i * P],
                                             ACT.Exp).then_inc(a_ready, 1)

                        decay(0)
                        logs(0)
                        weights(0)
                        refill(pm + 2 * j + 2, 1)
                        decay(1)
                        logs(1)
                        refill(pm + 2 * j + 3, 0)
                        weights(1)
                        refill(pm + 2 * j + 3, 1)
                        refill(pm + 2 * j + 4, 0)
                        e.wait_ge(pv2_done, 2 * J + 2)
                        settled()
                        e.activation(h_hi[:, bass.ds(j, 1), :].rearrange("p a t -> p (a t)"), out_bank[:],
                                     ACT.Copy).then_inc(ohi2_ready, 1)
                    refill(pm + MIX2_IN, 1)
                    for m in range(2):
                        e.wait_ge(pool_done, 2 * l + m + 1)
                        settled()
                        e.activation(h_hi[:, 6 + m, :], score[m][:], ACT.Identity,
                                     scale=col("pool_scale", 2 * l + m)).then_inc(phi_ready, 1)
                    for m in range(2):
                        e.wait_ge(conv2_ready, 2 * l + m + 1)
                        e.activation(h_hi[:, 4 + m, :], cx[:, 2 + m, :], ACT.Copy).then_inc(chi_ready, 1)
                    def out(i, last):
                        for s in range(2):
                            f_squares(pm + MIX2_IN + i, s, 3 * l + 1, 2 * i + s)
                            if last and s == 1:
                                f_root(3 * l + 1)
                            refill(pm + MIX2_IN + i + 1, s)

                    with e.Fori(0, DC // 2 - 1) as i:
                        out(i, False)
                    out(DC // 2 - 1, True)

        @block.vector
        def _(e):
            step = Steps(e, vec_step)

            def settled():
                e.wait_ge(consts_loaded, CONSTS)

            def passed():
                e.sem_inc(vec_passed, 1)

            def flat(ap):
                return ap.rearrange("p a t -> p (a t)")

            for free in (*taken, o_taken, o2_taken):
                e.sem_inc(free, 1)
            e.sem_inc(sums_taken, TB)
            settled()
            e.memset(eps[:], EPS)
            e.tensor_scalar(mask_b[:], tab("strict"), 1e30, -1e30, ALU.mult, ALU.add)
            e.memset(C_t[:], 0.0)
            e.memset(pool_w[:], 0.0)
            e.memset(slot(22, 1), 0.0)
            step(e.tensor_scalar(half_g[:], col("norm_g", 0, 96), 0.5, None, ALU.mult))
            e.sem_inc(prep_ready, 1)

            def cc(n):
                return co[:, n, :]

            def tt(out, a, b, op):
                step(e.tensor_tensor(out, a, b, op))

            lr, li = col("a_re", 0, 8), col("a_im", 0, 8)
            dt, lrdt, ang, mag, turns, red, red_c, sin, cos, abr, abi, den, rden, fre, fim, t1, t2, zr, zi = (
                cc(n) for n in range(19))
            e.wait_ge(ssm_act, 1)
            tt(lrdt, lr, dt, ALU.mult)
            tt(ang, li, dt, ALU.mult)
            step(e.tensor_scalar(turns, ang, INV_TWO_PI, ROUND_MAGIC, ALU.mult, ALU.add))
            step(e.tensor_scalar(turns, turns, ROUND_MAGIC, None, ALU.subtract))
            step(e.scalar_tensor_tensor(red, turns, -TWO_PI_1, ang, ALU.mult, ALU.add))
            step(e.scalar_tensor_tensor(red, turns, -TWO_PI_2, red, ALU.mult, ALU.add))
            step(e.scalar_tensor_tensor(red, turns, -TWO_PI_3, red, ALU.mult, ALU.add))
            step(e.tensor_scalar(red, red, PI_SAFE, -PI_SAFE, ALU.min, ALU.max))
            step(e.scalar_tensor_tensor(t1, red, -1.0, red, ALU.mult, ALU.max))
            e.tensor_scalar(red_c, t1, -1.0, HALF_PI, ALU.mult, ALU.add).then_inc(ssm_vec, 1)
            e.wait_ge(ssm_act, 2)
            tt(abr, mag, cos, ALU.mult)
            tt(abi, mag, sin, ALU.mult)
            tt(t1, lr, lr, ALU.mult)
            tt(t2, li, li, ALU.mult)
            tt(den, t1, t2, ALU.add)
            step(e.reciprocal(rden, den))
            step(e.tensor_scalar(zr, abr, -1.0, None, ALU.add))
            tt(t1, zr, lr, ALU.mult)
            tt(t2, abi, li, ALU.mult)
            tt(t1, t1, t2, ALU.add)
            tt(fre, t1, rden, ALU.mult)
            tt(t1, abi, lr, ALU.mult)
            tt(t2, zr, li, ALU.mult)
            tt(t1, t1, t2, ALU.subtract)
            tt(fim, t1, rden, ALU.mult)

            def per_state(name):
                return col(name, 0, SSM_TILES * SSM_CH).rearrange("p (i c) -> p i c", c=SSM_CH)

            def wide(ap, n):
                return ap[:, :, None].broadcast_to([P, SSM_TILES, n])

            b1 = slot(23)[:, 0:P].rearrange("p (i c) -> p i c", c=SSM_CH)
            b2 = slot(24)[:, 0:P].rearrange("p (i c) -> p i c", c=SSM_CH)
            B_pad = slot(22).rearrange("p (k i c) -> p k i c", k=2, c=32)
            for part, (x1, x2, op) in enumerate(((fre, fim, ALU.subtract), (fim, fre, ALU.add))):
                tt(b1, per_state("b_re"), wide(x1, SSM_CH), ALU.mult)
                tt(b2, per_state("b_im"), wide(x2, SSM_CH), ALU.mult)
                for h in range(2):
                    rows, ch = slice(64 * h, 64 * h + 64), slice(SSM_CH * h, SSM_CH * h + SSM_CH)
                    tt(B_pad[rows, part, :, ch], b1[rows], b2[rows], op)
            for h in range(2):
                rows, ch = slice(64 * h, 64 * h + 64), slice(SSM_CH * h, SSM_CH * h + SSM_CH)
                step(e.tensor_copy(C_t[rows, 0, :, ch], per_state("c_re")[rows]))
                step(e.tensor_scalar(C_t[rows, 1, :, ch], per_state("c_im")[rows], -1.0, None, ALU.mult))
            e.sem_inc(B_padded, 1)

            e.wait_ge(cact_ready, 1)
            for k in range(DC):
                e.wait_ge(ada_loaded[k % 4], 16 * (k // 4) + 16)
                if k == 0:
                    e.tensor_scalar(ada_acc[:], ada_w[:, 0, :], c_act[:, 0:1], None, ALU.mult).then_inc(ada_used, 1)
                else:
                    e.wait_ge(ada_used, k)
                    e.scalar_tensor_tensor(ada_acc[:], ada_w[:, k % 4, :], c_act[:, k:k + 1], ada_acc[:],
                                           ALU.mult, ALU.add).then_inc(ada_used, 1)

            def take_mod(first, columns, n, count):
                e.wait_ge(mod_sum, count)
                step(e.tensor_tensor(mod[:, first:first + n], out_bank[:, columns:columns + n],
                                     col("b_ada", first, n), ALU.add))

            def amplify(n, g_name, scale):
                step(e.scalar_tensor_tensor(amp[:, 8 * n:8 * n + 8], mod[:, scale:scale + 8], 1.0,
                                            col(g_name, 0, 8), ALU.add, ALU.mult))

            take_mod(0, 0, 16, 1)
            amplify(0, "g_mix", 8)
            e.sem_inc(mod_ready, 1)

            def invert(st):
                e.wait_ge(std_ready, st + 1)
                step(e.reciprocal(rstd[:], std))

            def modulate(n, shift):
                for c in range(DC):
                    if c >= 2:
                        e.wait_ge(u_ready, DC * n + c - 1)
                    e.scalar_tensor_tensor(ux[:, c % 2, :], x[:, c, :], amp[:, 8 * n + c:8 * n + c + 1], rstd[:],
                                           ALU.mult, ALU.mult).then_inc(ux_ready, 1)
                    if c:
                        shift_lo(n, c - 1, shift)
                shift_lo(n, DC - 1, shift)

            def shift_lo(n, c, shift):
                e.wait_ge(uhi_ready, DC * n + c + 1)
                e.scalar_tensor_tensor(u_lo[:, c, :], ux[:, c % 2, :], mod[:, shift + c:shift + c + 1],
                                       as32(u_hi[:, c, :]), ALU.add, ALU.subtract).then_inc(u_ready, 1)

            invert(0)
            modulate(0, 0)
            e.wait_ge(B_turned, 1)
            e.tensor_copy(B_t[:].rearrange("p k n -> p (k n)"), out_bank[:]).then_inc(B_ready, 1)

            e.memset(E1[:, 0, :, 0:1], 1.0)
            e.memset(E1[:, 1, :, 0:1], 0.0)
            e.memset(E16[:, 0, :, 0:1], 1.0)
            e.memset(E16[:, 1, :, 0:1], 0.0)
            step(e.tensor_copy(zr, cos))
            step(e.tensor_copy(zi, sin))
            for E, top in ((E1, 16), (E16, 32)):
                n = 1
                while n < top:
                    re, im = E[:, 0, :, 0:n], E[:, 1, :, 0:n]
                    p1 = slot(23)[:, 0:8 * n].rearrange("p (i c) -> p i c", c=n)
                    p2 = slot(24)[:, 0:8 * n].rearrange("p (i c) -> p i c", c=n)
                    tt(p1, re, wide(zr, n), ALU.mult)
                    tt(p2, im, wide(zi, n), ALU.mult)
                    tt(E[:, 0, :, n:2 * n], p1, p2, ALU.subtract)
                    tt(p1, re, wide(zi, n), ALU.mult)
                    tt(p2, im, wide(zr, n), ALU.mult)
                    tt(E[:, 1, :, n:2 * n], p1, p2, ALU.add)
                    tt(t1, zr, zr, ALU.mult)
                    tt(t2, zi, zi, ALU.mult)
                    step(e.scalar_tensor_tensor(zi, zr, 2.0, zi, ALU.mult, ALU.mult))
                    tt(zr, t1, t2, ALU.subtract)
                    n *= 2
            e.wait_ge(bu_ready, 2 * SSM_TILES)

            def scan_parts(i):
                c_t, s_t, p1, p2, p3, p4, p5 = (ssm_tmp[:, n, :] for n in range(7))
                br, bi = flat(bu_re[:, bass.ds(i, 1), :]), flat(bu_im[:, bass.ds(i, 1), :])
                r = co[:, 3, bass.ds(i, 1)].broadcast_to([P, T])

                def power(part, b_part, out):
                    grid = out.rearrange("p (a b) -> p a b", b=16)
                    big = flat(E16[:, part, bass.ds(i, 1), :])[:, :, None].broadcast_to([P, 32, 16])
                    small = flat(E1[:, b_part, bass.ds(i, 1), :])[:, None, :].broadcast_to([P, 32, 16])
                    return e.tensor_tensor(grid, big, small, ALU.mult)

                def turned():
                    power(0, 0, c_t)
                    step(power(1, 1, p5))
                    e.tensor_tensor(c_t, c_t, p5, ALU.subtract)
                    power(0, 1, s_t)
                    step(power(1, 0, p1))
                    tt(s_t, s_t, p1, ALU.add)
                    e.tensor_tensor(p1, c_t, br, ALU.mult)
                    e.tensor_tensor(p2, s_t, bi, ALU.mult)
                    e.tensor_tensor(p5, c_t, bi, ALU.mult)
                    tt(p3, s_t, br, ALU.mult)
                    e.tensor_tensor(p4, p1, p2, ALU.add)
                    tt(p5, p5, p3, ALU.subtract)

                def scanned():
                    e.tensor_tensor_scan(br, r, p4, 0.0, ALU.mult, ALU.add)
                    step(e.tensor_tensor_scan(bi, r, p5, 0.0, ALU.mult, ALU.add))
                    e.tensor_tensor(p1, c_t, br, ALU.mult)
                    e.tensor_tensor(p2, s_t, bi, ALU.mult)
                    e.tensor_tensor(p3, s_t, br, ALU.mult)
                    tt(p4, c_t, bi, ALU.mult)
                    e.tensor_tensor(br, p1, p2, ALU.subtract)
                    e.tensor_tensor(bi, p3, p4, ALU.add).then_inc(scan_ready, 1)

                return turned, scanned

            with e.Fori(0, HEAD_PAIRS) as j:
                start = step.enter(j, HEADS1_STEPS)

                def bias(h):
                    step(e.tensor_scalar(bias_h, tab("dist"), col("slopes", 2 * j + h), None, ALU.mult))

                def score_bias(n):
                    b = n % TB
                    W = (b + 1) * P
                    e.wait_ge(s_done, 8 * j + n + 1)
                    passed()
                    e.tensor_tensor_reduce(nsc[:, n % 2, 0:W], score[n % 2][:, 0:W], bias_h[:, T - W:T], 1.0, 3e38,
                                           ALU.add, ALU.min, stat[:, n:n + 1]).then_inc(s_biased, 1)

                def weigh(n):
                    W = (n % TB + 1) * P
                    e.wait_ge(p_ready, 8 * j + n + 1)
                    step(e.tensor_tensor_reduce(nsc[:, n % 2, 0:W], nsc[:, n % 2, 0:W], tab("count", T - W, T),
                                                1.0, 0.0, ALU.mult, ALU.add, stat[:, 8 + n:9 + n]))
                    e.reciprocal(stat[:, 16 + n:17 + n], stat[:, 8 + n:9 + n]).then_inc(p_weighted, 1)

                def take_probs(n):
                    b = n % TB
                    e.wait_ge(p_turned, 8 * j + n + 1)
                    if n == TB:
                        e.wait_ge(pv_done, 2 * j + 1)
                    e.tensor_copy(pT(b).rearrange("p i t -> p (i t)"), mix[n % 2][:, 0:(b + 1) * P]).then_inc(
                        pT_ready, 1)

                for part in scan_parts(2 * j):
                    part()
                second_tile = scan_parts(2 * j + 1)
                bias(0)
                score_bias(0)
                score_bias(1)
                e.wait_ge(v_turned, j + 1)
                e.tensor_copy(v_nat.rearrange("p i d -> p (i d)"), out_bank[:]).then_inc(v_ready, 1)
                weigh(0)
                weigh(1)
                for n in range(0, 2 * TB, 2):
                    take_probs(n)
                    if n + 2 == TB:
                        bias(1)
                    if n + 2 < 2 * TB:
                        score_bias(n + 2)
                    take_probs(n + 1)
                    if n + 2 < 2 * TB:
                        score_bias(n + 3)
                        weigh(n + 2)
                        weigh(n + 3)
                    if n < 4:
                        second_tile[n // 2]()
                e.wait_ge(ohi_ready, j + 1)
                e.tensor_tensor(flat(h_lo[:, bass.ds(j, 1), :]), out_bank[:],
                                as32(flat(h_hi[:, bass.ds(7 + j, 1), :])), ALU.subtract).then_inc(o_taken, 1)
            step.at = start + HEAD_PAIRS * HEADS1_STEPS
            for m in range(2):
                e.wait_ge(y_done, TB * (m + 1))
                e.scalar_tensor_tensor(ssm_y[:, m, :], us[:, m, :], col("d_skip", m), mix[m][:], ALU.mult,
                                       ALU.add).then_inc(y_ready, 1)
            for m in range(2):
                e.wait_ge(glu_ready, m + 1)
                e.tensor_tensor(ssm_y[:, m, :], gelu_y[:, m, :], glu_s[:, m, :], ALU.mult).then_inc(yy_ready, 1)
            for m in range(2):
                e.wait_ge(yhi_ready, m + 1)
                e.tensor_tensor(h_lo[:, 4 + m, :], ssm_y[:, m, :], as32(h_hi[:, 5 + m, :]),
                                ALU.subtract).then_inc(y_split, 1)
            def add_rows(a, out, k, like):
                e.wait_ge(ada_rows_loaded[a % 4], 16 * (a // 4) + 16)
                if k == 0:
                    e.tensor_scalar(out, ada_rows[:, a % 4, :], c_act[:, 0:1], None, ALU.mult).then_inc(ada_used, 1)
                else:
                    e.wait_ge(ada_used, DC + a - like + 1)
                    e.scalar_tensor_tensor(out, ada_rows[:, a % 4, :], c_act[:, k:k + 1], out, ALU.mult,
                                           ALU.add).then_inc(ada_used, 1)

            e.wait_ge(y_split, 2)
            for i in range(DC // 2):
                for s in range(2):
                    p, c = MERGE1 + i, 2 * i + s
                    add_rows(c, gate_sum, c, 1)
                    g_att = flat(gates[:, bass.ds(c, 1), :])
                    g_ssm = flat(gates[:, bass.ds(c + DC, 1), :])
                    e.wait_ge(sig_ready, c + 1)
                    e.wait_ge(unit_done, 2 * p + s + 1)
                    step(e.tensor_tensor(slot(24), score[s][:], g_ssm, ALU.mult))
                    e.tensor_tensor(slot(25), unit_bank[s][:], g_att, ALU.mult).then_inc(taken[s], 1)
                    e.wait_ge(taken[s], p + 2)
                    e.tensor_tensor(slot(22 + s), slot(24), slot(25), ALU.add).then_inc(merged_ready, 1)
                    e.wait_ge(mhi_ready, c + 1)
                    e.tensor_tensor(flat(u_lo[:, bass.ds(c, 1), :]), slot(22 + s),
                                    as32(flat(u_hi[:, bass.ds(c, 1), :])), ALU.subtract).then_inc(m_ready, 1)
            take_mod(16, 0, DC, 2)

            def take_update(p, s, c, gate):
                xc = flat(x[:, bass.ds(c, 1), :])
                e.wait_ge(unit_done, 2 * p + s + 1)
                e.scalar_tensor_tensor(xc, unit_bank[s][:], mod[:, bass.ds(gate + c, 1)], xc, ALU.mult,
                                       ALU.add).then_inc(taken[s], 1)

            for k in range(DC):
                for n in range(3):
                    a = DC + 3 * k + n
                    add_rows(a, ada_sums[:, n * D:(n + 1) * D], k, 3)
                take_update(OUT1 + k // 2, k % 2, k, 16)
            def gated_update(p0, gate):
                with e.Fori(0, DC // 2) as i:
                    for s in range(2):
                        take_update(p0 + i, s, 2 * i + s, gate)

            invert(1)
            take_mod(24, DC, 2 * DC, 4)
            amplify(1, "g_ffn", 32)
            e.sem_inc(mod_ready, 1)
            modulate(1, 24)
            take_mod(40, 3 * DC, DC, 5)
            step(e.memset(a_pad[:, 0:2], 0.0))
            e.sem_inc(prep_ready, 1)
            for half in range(2):
                p0 = FFN1 + half * FFN1_HALF
                with e.Fori(0, HALF1) as i:
                    start = step.enter(i, CONV_STEPS)
                    c = HALF1 * half + i
                    e.wait_ge(taken[0], p0 + i + 2)
                    settled()
                    step(e.tensor_scalar(ffn_u, a_pad[:, 2:T + 2], col("w_conv", c), col("b_conv", c),
                                         ALU.mult, ALU.add))
                    step(e.scalar_tensor_tensor(ffn_u, a_pad[:, 1:T + 1], col("w_conv", 16 + c), ffn_u,
                                                ALU.mult, ALU.add))
                    e.scalar_tensor_tensor(ffn_u, a_pad[:, 0:T], col("w_conv", 32 + c), ffn_u,
                                           ALU.mult, ALU.add).then_inc(conv_ready, 1)
                    e.wait_ge(silu_ready, c + 1)
                    e.wait_ge(unit_done, 2 * (p0 + i) + 2)
                    e.tensor_tensor(ffn_h, unit_bank[1][:], ffn_s, ALU.mult).then_inc(taken[1], 1)
                    e.wait_ge(hhi_ready, c + 1)
                    e.tensor_tensor(flat(h_lo[:, bass.ds(i, 1), :]), ffn_h, as32(flat(h_hi[:, bass.ds(i, 1), :])),
                                    ALU.subtract).then_inc(h_ready, 1)
                step.at = start + HALF1 * CONV_STEPS
                gated_update(p0 + HALF1, 40)
            invert(2)
            for c in range(DC):
                e.scalar_tensor_tensor(x[:, c, :], x[:, c, :], col("g_final", c), rstd[:], ALU.mult,
                                       ALU.mult).then_inc(x_ready, 1)

            with e.Fori(0, LAYERS) as l:
                step.enter(l, LAYER_STEPS)
                calls = step.calls

                def low_part(k, c):
                    e.wait_ge(uhi_ready, DC * (2 + 3 * l + k) + c + 1)
                    e.scalar_tensor_tensor(u_lo[:, c, :], x[:, c, :], col("norm_g", (6 * l + 2 * k) * DC + c),
                                           as32(u_hi[:, c, :]), ALU.mult, ALU.subtract).then_inc(u_ready, 1)

                def factor(k):
                    invert(3 + 6 * l + 2 * k)
                    passed()

                def post_norm(k):
                    invert(4 + 6 * l + 2 * k)
                    for c in range(DC):
                        at = (6 * l + 2 * k + 1) * DC + c
                        g = col("norm_g", at) if k == 1 else half_g[:, bass.ds(at, 1)]
                        step(e.scalar_tensor_tensor(ux[:, c % 2, :], f[:, c, :], g, rstd[:], ALU.mult, ALU.mult))
                        e.tensor_tensor(x[:, c, :], x[:, c, :], ux[:, c % 2, :], ALU.add).then_inc(x_ready, 1)
                        if k < 2 and c:
                            low_part(k + 1, c - 1)
                    if k < 2:
                        low_part(k + 1, DC - 1)
                        factor(k + 1)

                def f_out(p0, r, add, squares):
                    if squares:
                        e.memset(acc, 0.0).then_inc(fsq_added, 1)
                    with e.Fori(0, DC // 2) as i:
                        for s in range(2):
                            fc = flat(f[:, bass.ds(2 * i + s, 1), :])
                            e.wait_ge(unit_done, 2 * (p0 + i) + s + 1)
                            if add:
                                e.tensor_tensor(fc, unit_bank[s][:], fc, ALU.add).then_inc(taken[s], 1)
                            else:
                                settled()
                                e.tensor_copy(fc, unit_bank[s][:]).then_inc(taken[s], 1)
                            if squares:
                                e.wait_ge(fsq_ready, DC * r + 2 * i + s + 1)
                                e.wait_ge(fsq_added, (DC + 1) * r + 2 * i + s + 1)
                                e.tensor_tensor(acc, acc, sq[:, 0, :], ALU.add).then_inc(fsq_added, 1)

                for s_ffn in range(2):
                    k_norm = 2 * s_ffn
                    if s_ffn == 0:
                        for c in range(DC):
                            low_part(0, c)
                        factor(0)
                    for half in range(2):
                        p0 = ffn2(l, s_ffn) + half * FFN2_HALF
                        h0 = 16 + 44 * l + 22 * s_ffn + HALF2 * half

                        def hidden(i, banks):
                            p = p0 + i
                            e.wait_ge(unit_done, 2 * p + 1)
                            e.tensor_tensor(ffn_g, banks[0][:], rstd[:], ALU.mult).then_inc(taken[0], 1)
                            e.wait_ge(unit_done, 2 * p + 2)
                            e.tensor_tensor(ffn_u, banks[1][:], rstd[:], ALU.mult).then_inc(taken[1], 1)
                            e.wait_ge(silu_ready, h0 + i + 1)
                            e.wait_ge(taken[1], p + 2)
                            e.tensor_tensor(ffn_h, ffn_s, ffn_u, ALU.mult).then_inc(hidden_ready, 1)
                            e.wait_ge(hhi_ready, h0 + i + 1)
                            e.tensor_tensor(flat(h_lo[:, bass.ds(i, 1), :]), ffn_h,
                                            as32(flat(h_hi[:, bass.ds(i, 1), :])), ALU.subtract).then_inc(h_ready, 1)

                        if half == 0:
                            hidden(0, score)
                        with e.Fori(1 - half, HALF2) as i:
                            hidden(i, unit_bank)
                        f_out(p0 + HALF2, 3 * l + k_norm, half == 1, half == 1)
                    post_norm(k_norm)
                    if s_ffn:
                        continue
                    pm = layer(l) + MIX2
                    for g in range(2):
                        rows = slice(64 * g, 64 * g + 64)
                        step(e.tensor_copy(pool_w[rows, :, rows], tabs[rows, bass.ds(
                            l * P + TABS["pool_w"][0], P)].rearrange("p (m n) -> p m n", m=2)))
                    A, B = padded[:, 0, :], padded[:, 1, :]
                    Z = 16
                    lower, upper = slice(0, 64), slice(64, P)

                    def trailing(dst, src, lag, rows=slice(0, P)):
                        tt(dst[rows, Z:], src[rows, Z:], src[rows, Z - lag:T + Z - lag], ALU.add)

                    def pool(m):
                        step(e.tensor_copy(A[:, Z:], f[:, m, :]))
                        trailing(B, A, 1)
                        if m:
                            trailing(A, B, 2)
                            trailing(B, A, 4)
                        trailing(A, B, 8 if m else 2, upper)
                        head = col("inv_head", 16 * m, 16)
                        for rows, src in ((lower, B), (upper, A)):
                            step(e.tensor_scalar(pooled[rows, m, :], src[rows, Z:], col("inv_w", m)[rows], None, ALU.mult))
                            tt(pooled[rows, m, 0:16], src[rows, Z:Z + 16], head[rows], ALU.mult)
                        e.tensor_tensor(pooled[:, m, :], pooled[:, m, :], f[:, m, :], ALU.subtract).then_inc(pool_in, 1)

                    def convolve(m):
                        tt(A[:, Z:], f[:, 2 + m, :], f[:, 4 + m, :], ALU.mult)
                        y = cx[:, m, :]

                        def tap(n):
                            return col("conv_w2", 6 * l + 2 * n + m)

                        step(e.tensor_scalar(y, A[:, Z - 2:T + Z - 2], tap(0), None, ALU.mult))
                        for n in (1, 2):
                            step(e.scalar_tensor_tensor(y, A[:, Z - 2 + n:T + Z - 2 + n], tap(n), y, ALU.mult, ALU.add))

                    def take(p, s, out, banks=unit_bank):
                        e.wait_ge(unit_done, 2 * p + s + 1)
                        e.tensor_tensor(out, banks[s][:], rstd[:], ALU.mult).then_inc(taken[s], 1)

                    def take_q(j, banks=unit_bank):
                        p = pm + 2 * j
                        e.wait_ge(unit_done, 2 * p + 1)
                        e.scalar_tensor_tensor(q_st, banks[0][:], ATT_SCALE, rstd[:], ALU.mult,
                                               ALU.mult).then_inc(taken[0], 1)

                    def head_pair(j, last):
                        J = HEAD_PAIRS * l + j

                        def parts(h):
                            for n in range(TB):
                                i = TB - 1 - n
                                z = z_bank[i][:, 0:T - i * P]
                                e.wait_ge(act_step, 16 * J + 2 * TB * h + n + 1)
                                e.tensor_scalar(kept[:, i, 0:T - i * P], z, 0.0, None, ALU.max)
                                t = e.tensor_scalar(own[:, i, 0:T - i * P], z, 0.0, None, ALU.min)
                            step(t)

                        def keep_logs(h):
                            for n in range(TB):
                                i = TB - 1 - n
                                W = T - i * P
                                e.wait_ge(softp_ready, 8 * J + TB * h + n + 1)
                                e.scalar_tensor_tensor(kept[:, i, 0:W], softp[:, i, 0:W], -1.0, kept[:, i, 0:W],
                                                       ALU.mult, ALU.subtract)
                                step(e.tensor_tensor(own[:, i, 0:W], own[:, i, 0:W], softp[:, i, 0:W], ALU.subtract))
                                e.tensor_tensor(own[:, i, 0:P], own[:, i, 0:P], mask_b[:], ALU.add)
                                e.tensor_tensor(kept[:, i, 0:P], kept[:, i, 0:P], tab("strict"),
                                                ALU.mult).then_inc(sp_ready, 1)

                        def add_sums(h):
                            for n in range(TB):
                                i = TB - 1 - n
                                W = T - i * P
                                e.wait_ge(R_done, 8 * J + TB * h + n + 1)
                                e.tensor_tensor(own[:, i, 0:W], z_bank[i][:, 0:W], own[:, i, 0:W],
                                                ALU.add).then_inc(sums_taken, 1)

                        parts(0)
                        keep_logs(0)
                        add_sums(0)
                        take(pm + 2 * j + 1, 1, flat(f[:, bass.ds(j, 1), :]))
                        e.wait_ge(v2_turned, J + 1)
                        e.tensor_copy(v_nat.rearrange("p i d -> p (i d)"), out_bank[:]).then_inc(v2_ready, 1)
                        parts(1)
                        keep_logs(1)
                        if last:
                            take(pm + 2 * HEAD_PAIRS, 0, f[:, HEAD_PAIRS, :])
                            pool(0)
                        else:
                            take_q(j + 1)
                        add_sums(1)
                        if last:
                            pool(1)
                            convolve(0)
                        take(pm + 2 * j + 2, 1, f[:, HEAD_PAIRS + 1, :] if last else k_st)
                        if last:
                            e.wait_ge(taken[1], pm + 2 * HEAD_PAIRS + 2)
                            convolve(1)
                        take(pm + 2 * j + 3, 0, f[:, HEAD_PAIRS + 2, :] if last else vT_st)
                        e.wait_ge(ohi2_ready, J + 1)
                        e.tensor_tensor(flat(h_lo[:, bass.ds(j, 1), :]), out_bank[:],
                                        as32(flat(h_hi[:, bass.ds(j, 1), :])), ALU.subtract).then_inc(o2_taken, 1)

                    step(e.memset(padded[:, :, 0:Z], 0.0))
                    take_q(0, score)
                    take(pm, 1, k_st, score)
                    take(pm + 1, 0, vT_st)
                    with e.Fori(0, HEAD_PAIRS - 1) as j:
                        start = step.enter(j, HEADS2_STEPS)
                        head_pair(j, False)
                    step.at = start + (HEAD_PAIRS - 1) * HEADS2_STEPS
                    head_pair(HEAD_PAIRS - 1, True)
                    take(pm + 2 * HEAD_PAIRS + 1, 1, f[:, HEAD_PAIRS + 3, :])
                    e.wait_ge(taken[1], pm + 2 * HEAD_PAIRS + 3)
                    for m in range(2):
                        e.tensor_tensor(cx[:, 2 + m, :], cx[:, m, :], f[:, 6 + m, :], ALU.mult).then_inc(conv2_ready, 1)
                    for m in range(2):
                        e.wait_ge(phi_ready, 2 * l + m + 1)
                        e.scalar_tensor_tensor(h_lo[:, 6 + m, :], score[m][:], col("pool_scale", 2 * l + m),
                                               as32(h_hi[:, 6 + m, :]), ALU.mult, ALU.subtract).then_inc(cat_ready, 1)
                    for m in range(2):
                        e.wait_ge(chi_ready, 2 * l + m + 1)
                        e.tensor_tensor(h_lo[:, 4 + m, :], cx[:, 2 + m, :], as32(h_hi[:, 4 + m, :]),
                                        ALU.subtract).then_inc(cat_ready, 1)
                    f_out(pm + MIX2_IN, 3 * l + 1, False, True)
                    post_norm(1)
                assert step.calls - calls + (HEAD_PAIRS - 2) * HEADS2_STEPS == LAYER_STEPS, step.calls - calls


def _tiles(w):
    K, F = w.shape
    return w.reshape(K // P, P, F // P, P).transpose(2, 1, 0, 3).reshape(F // P, P, K)


def _cols(v):
    return v.reshape(-1, P).T


def _layout(a):
    import numpy as np

    lead = {k: v[0] for k, v in a.items() if not k.endswith("_2") and k != "g_final"}
    out = {"x": lead["x"].T.reshape(DC, P, T).transpose(1, 0, 2)}
    t_s = np.arange(P)[:, None] + (T - P) - np.arange(T)[None, :]
    seen = t_s >= 0
    count = (seen * ((t_s <= P) * 1 + (t_s % 4 == 0) + (t_s % 16 == 0))).astype(np.float32)
    dist = np.where(count > 0, t_s, 1e35).astype(np.float32)
    row, colm = np.arange(P)[:, None], np.arange(P)[None, :]
    eye = (row == colm).astype(np.float32)
    windows = np.repeat(np.array([[2, 8], [4, 16]], np.float32), 64, axis=0)
    inv_head = 1.0 / np.minimum(np.arange(1, 17, dtype=np.float32)[None, None, :], windows[:, :, None])
    slopes = np.array([2.0 ** (-8.0 * (h + 1) / HEADS) for h in range(HEADS)], np.float32)

    def state(v):
        return v.reshape(SSM_TILES, P).T

    def state_ch(v):
        return v.reshape(SSM_TILES, P, SSM_CH).transpose(1, 0, 2).reshape(P, -1)

    parts = {
        "c": _cols(lead["c"]), "b_ada": _cols(lead["b_ada"]), "g_mix": _cols(lead["g_mix"]),
        "g_ffn": _cols(lead["g_ffn"]), "g_final": _cols(a["g_final"]), "norm_g": _cols(a["norm_g_2"]),
        "b_gate": _cols(lead["b_gate"]), "d_skip": _cols(lead["d_skip"]), "b_glu": _cols(lead["b_glu"]),
        "w_conv": _cols(lead["w_conv"]), "b_conv": _cols(lead["b_conv"]), "conv_w2": _cols(a["conv_w_2"]),
        "pool_scale": _cols(a["pool_scale_2"]), "slopes": np.broadcast_to(slopes, (P, HEADS)),
        "a_re": state(lead["a_re"]), "a_im": state(lead["a_im"]), "log_dt": state(np.repeat(lead["log_dt"], 64)),
        "inv_head": inv_head.reshape(P, 32).astype(np.float32), "inv_w": (1.0 / windows).astype(np.float32),
        "b_re": state_ch(lead["b_re"]), "b_im": state_ch(lead["b_im"]),
        "c_re": state_ch(lead["c_re"].transpose(0, 2, 1)), "c_im": state_ch(lead["c_im"].transpose(0, 2, 1)),
    }
    out["cols"] = np.concatenate([parts[n] for n in COLS], axis=1)
    tabs = {
        "ident": eye, "after": (row > colm).astype(np.float32), "ones": np.ones((P, P), np.float32),
        "strict": (colm > row).astype(np.float32), "dist": dist, "count": count,
        "w_glu": lead["w_glu"].reshape(2, P, 256).transpose(1, 0, 2).reshape(P, 512),
        "pool_w": a["pool_w_2"].reshape(2, 2, P, 64).transpose(2, 0, 1, 3).reshape(P, 256),
    }
    out["tabs"] = np.concatenate([tabs[n] for n in TABS], axis=1)
    w_ada = lead["w_ada"].reshape(DC, P, 6 * D)
    out["w_ada"] = w_ada[:, :, :2 * D]
    rest = w_ada[:, :, 3 * D:].reshape(DC, P, 3, D).transpose(0, 2, 1, 3).reshape(3 * DC, P, D)
    out["w_ada_rows"] = np.concatenate([w_ada[:, :, 2 * D:3 * D], rest])

    w_in = _tiles(lead["w_in"])
    q0, k0, v0, us0, g0 = 0, 4, 8, 12, 14
    order = [us0, us0 + 1]
    for j in range(HEAD_PAIRS):
        order += [q0 + j, k0 + j, v0 + j, g0 + 3 * j, g0 + 3 * j + 1, g0 + 3 * j + 2]
    order += [g0 + n for n in range(12, 16)]
    out["w_in"] = w_in[order]
    out["w_merge"] = np.concatenate([_tiles(lead["w_proj_ssm"]), _tiles(lead["w_proj_att"])], axis=2)
    out["w_out"] = _tiles(lead["w_out"])
    up = _tiles(lead["w_up"]).reshape(2, 16, P, D)
    out["w_up"] = up.transpose(1, 0, 2, 3).reshape(32, P, D)
    out["w_down"] = np.concatenate([_tiles(w) for w in lead["w_down"].reshape(2, D, D)])

    gu, dn, in2, out2 = [], [], [], []
    for l in range(LAYERS):
        for s in range(2):
            pair = np.stack([_tiles(a["ffn_w_gate_2"][l, s]), _tiles(a["ffn_w_up_2"][l, s])], axis=1)
            gu.append(pair.reshape(4 * HALF2, P, D))
            dn += [_tiles(w) for w in a["ffn_w_down_2"][l, s].reshape(2, RING, D)]
        w = _tiles(a["w_in_2"][l])
        q0, k0, v0, gb, gc, ch, pl = 0, 4, 8, 12, 14, 16, 18
        extra = [pl, pl + 1, ch, ch + 1, gc, gc + 1, gb, gb + 1]
        order = []
        for j in range(HEAD_PAIRS):
            order += [q0 + j, k0 + j, v0 + j, extra[j]]
        in2.append(w[order + extra[4:]])
        out2.append(_tiles(a["w_out_2"][l]))
    out["w_gate_up"], out["w_down2"] = np.concatenate(gu), np.concatenate(dn)
    out["w_in2"], out["w_out2"] = np.concatenate(in2), np.concatenate(out2)
    return {k: np.ascontiguousarray(v) for k, v in out.items()}


def kernel(**inputs):
    import numpy as np
    import concourse.bacc as bacc
    from concourse.bass_utils import run_bass_kernel_spmd

    arrays = _layout({k: np.asarray(v) for k, v in inputs.items()})
    nc = bacc.Bacc("TRN2", target_bir_lowering=False, num_devices=1, dynamic_dma_scratch_size=256)
    d = {k: nc.dram_tensor(f"in_{k}", v.shape, F32, kind="ExternalInput").ap() for k, v in arrays.items()}
    d["out"] = nc.dram_tensor("out", (DC, P, T), F32, kind="ExternalOutput").ap()
    program(nc, d)
    r = run_bass_kernel_spmd(nc, [{f"in_{k}": v for k, v in arrays.items()}], core_ids=[0])
    return np.ascontiguousarray(r.results[0]["out"].reshape(D, T).T)[None]
```
